# Optimizing a Trainium2 kernel written in Bass

```python
import math
import jax, jax.numpy as jnp
from jax import lax
import numpy as np

D_MODEL = 1024
BATCH = 1
SEQ = 256
DEPTH = 2
DEC_BATCH = 8
DEC_SEQ = 4
PAST_LEN = 2048
PAGE_SIZE = 128

N_MIXERS = 4
GROUP_W = D_MODEL // N_MIXERS
MIX_W = N_MIXERS * GROUP_W
HEAD_DIM = 64
N_HEADS = GROUP_W // HEAD_DIM
SSM_STATE = 64
SSM_GROUPS = 2
CONV_W = 4
D_FF = ((8 * D_MODEL // 3 + 127) // 128) * 128
CHUNK = 64
EPS = 1e-6
ROPE_BASE = 10000.0

RET_IN = 4 * GROUP_W
SSM_CONV_CH = GROUP_W + 2 * SSM_GROUPS * SSM_STATE
SSM_IN = GROUP_W + SSM_CONV_CH + N_HEADS
GDN_CONV_CH = 3 * GROUP_W
GDN_IN = GDN_CONV_CH + GROUP_W + 2 * N_HEADS
MLSTM_IN = 4 * GROUP_W + 2 * N_HEADS
IN_DIM = RET_IN + SSM_IN + GDN_IN + MLSTM_IN

kernel_name = "hymba_four_recurrent_group_decoder_step"

def _split(a, sizes):
    offs = [int(o) for o in np.cumsum(sizes)[:-1]]
    return jnp.split(a, offs, axis=-1)

def rmsnorm(x, g):
    xf = x.astype(jnp.float32)
    y = xf * lax.rsqrt(jnp.mean(xf * xf, axis=-1, keepdims=True) + EPS)
    return (y * g.astype(jnp.float32)).astype(x.dtype)

def head_rmsnorm(x, g):
    shp = x.shape
    xh = x.reshape(shp[:-1] + (N_HEADS, HEAD_DIM)).astype(jnp.float32)
    xh = xh * lax.rsqrt(jnp.mean(xh * xh, axis=-1, keepdims=True) + EPS)
    return xh.reshape(shp) * g.astype(jnp.float32)

def l2norm(x):
    return x * lax.rsqrt(jnp.sum(x * x, axis=-1, keepdims=True) + EPS)

def rotary(x, pos):
    half = HEAD_DIM // 2
    inv = ROPE_BASE ** (-jnp.arange(half, dtype=jnp.float32) / half)
    ang = pos.astype(jnp.float32)[:, None] * inv[None, :]
    cos = jnp.cos(ang)[None, :, None, :]
    sin = jnp.sin(ang)[None, :, None, :]
    x1, x2 = x[..., :half], x[..., half:]
    return jnp.concatenate([x1 * cos - x2 * sin, x1 * sin + x2 * cos], axis=-1)

def causal_conv(x, buf, w):
    xp = jnp.concatenate([buf.astype(x.dtype), x], axis=1)
    L = x.shape[1]
    out = xp[:, 0:L] * w[0]
    for j in range(1, CONV_W):
        out = out + xp[:, j:j + L] * w[j]
    return out, xp[:, -(CONV_W - 1):]

def to_chunks(a, c):
    b, L = a.shape[:2]
    return jnp.moveaxis(a.reshape((b, L // c, c) + a.shape[2:]), 1, 0)

def from_chunks(a):
    n, b, c = a.shape[:3]
    return jnp.moveaxis(a, 0, 1).reshape((b, n * c) + a.shape[3:])

def pick_chunk(L):
    return CHUNK if L % CHUNK == 0 else L

def retention_chunked(q, k, v, s0, chunk):
    lg = jnp.log(1.0 - jnp.exp2(-5.0 - jnp.arange(N_HEADS, dtype=jnp.float32)))
    idx = jnp.arange(chunk, dtype=jnp.float32)
    rel = idx[:, None] - idx[None, :]
    intra = jnp.exp(jnp.where((rel >= 0)[None], rel[None] * lg[:, None, None], -jnp.inf))
    inter = jnp.exp((idx[None, :] + 1.0) * lg[:, None])
    tail = jnp.exp((chunk - 1.0 - idx[None, :]) * lg[:, None])
    carry_decay = jnp.exp(chunk * lg)

    def body(s, xs):
        qc, kc, vc = xs
        att = jnp.einsum('bnhd,bmhd->bhnm', qc, kc) * intra
        o = (jnp.einsum('bhnm,bmhd->bnhd', att, vc)
             + jnp.einsum('bnhd,bhde,hn->bnhe', qc, s, inter))
        s = s * carry_decay[:, None, None] + jnp.einsum('bmhd,hm,bmhe->bhde', kc, tail, vc)
        return s, o

    s, o = lax.scan(body, s0, (to_chunks(q, chunk), to_chunks(k, chunk), to_chunks(v, chunk)))
    return from_chunks(o), s

def ssd_chunked(x, dt, A, bmat, cmat, h0, chunk):
    tri = jnp.tril(jnp.ones((chunk, chunk), dtype=bool))

    def body(h, xs):
        xc, dtc, bc, cc = xs
        cum = jnp.cumsum(dtc * A, axis=1)
        seg = cum[:, :, None, :] - cum[:, None, :, :]
        lmat = jnp.exp(jnp.where(tri[None, :, :, None], seg, -jnp.inf))
        scores = jnp.einsum('bthn,bshn->btsh', cc, bc) * lmat * dtc[:, None, :, :]
        y = (jnp.einsum('btsh,bshp->bthp', scores, xc)
             + jnp.einsum('bthn,bhpn->bthp', cc, h) * jnp.exp(cum)[..., None])
        w = jnp.exp(cum[:, -1:, :] - cum) * dtc
        h = h * jnp.exp(cum[:, -1, :])[:, :, None, None] + jnp.einsum('bsh,bshp,bshn->bhpn', w, xc, bc)
        return h, y

    h, y = lax.scan(body, h0, (to_chunks(x, chunk), to_chunks(dt, chunk),
                               to_chunks(bmat, chunk), to_chunks(cmat, chunk)))
    return from_chunks(y), h

def gated_delta_chunked(q, k, v, g, beta, s0, chunk):
    tri = jnp.tril(jnp.ones((chunk, chunk), dtype=bool))
    strict = jnp.tril(jnp.ones((chunk, chunk), dtype=bool), -1)

    def body(s, xs):
        qc, kc, vc, gc, bc = xs
        qh, kh, vh = (jnp.swapaxes(t, 1, 2) for t in (qc, kc, vc))
        gh, bh = jnp.swapaxes(gc, 1, 2), jnp.swapaxes(bc, 1, 2)
        cum = jnp.cumsum(gh, axis=-1)
        diff = cum[..., :, None] - cum[..., None, :]
        gam = jnp.exp(jnp.where(tri, diff, -jnp.inf))
        amat = jnp.einsum('bhtd,bhsd->bhts', kh, kh) * jnp.where(strict, gam, 0.0) * bh[..., :, None]
        rhs = jnp.concatenate([vh * bh[..., None], kh * (bh * jnp.exp(cum))[..., None]], axis=-1)
        sol = lax.linalg.triangular_solve(amat, rhs, left_side=True, lower=True, unit_diagonal=True)
        u, w = sol[..., :HEAD_DIM], sol[..., HEAD_DIM:]
        v_new = u - jnp.einsum('bhtd,bhde->bhte', w, s)
        qk = jnp.einsum('bhtd,bhsd->bhts', qh, kh) * gam
        o = (jnp.einsum('bhtd,bhde->bhte', qh * jnp.exp(cum)[..., None], s)
             + jnp.einsum('bhts,bhse->bhte', qk, v_new))
        s = (s * jnp.exp(cum[..., -1])[..., None, None]
             + jnp.einsum('bhsd,bhse->bhde', kh * jnp.exp(cum[..., -1:] - cum)[..., None], v_new))
        return s, jnp.swapaxes(o, 1, 2)

    s, o = lax.scan(body, s0, (to_chunks(q, chunk), to_chunks(k, chunk), to_chunks(v, chunk),
                               to_chunks(g, chunk), to_chunks(beta, chunk)))
    return from_chunks(o), s

def mlstm_chunked(q, k, v, logi, logf, c0, n0, m0, chunk):
    tri = jnp.tril(jnp.ones((chunk, chunk), dtype=bool))

    def body(carry, xs):
        cm, nm, mm = carry
        qc, kc, vc, ic, fc = xs
        qh, kh, vh = (jnp.swapaxes(t, 1, 2) for t in (qc, kc, vc))
        ih, fh = jnp.swapaxes(ic, 1, 2), jnp.swapaxes(fc, 1, 2)
        b = jnp.cumsum(fh, axis=-1)
        dmat = jnp.where(tri, b[..., :, None] - b[..., None, :] + ih[..., None, :], -jnp.inf)
        m_t = jnp.maximum(b + mm[..., None], jnp.max(dmat, axis=-1))
        wts = jnp.exp(dmat - m_t[..., None])
        inter = jnp.exp(b + mm[..., None] - m_t)
        qk = jnp.einsum('bhtd,bhsd->bhts', qh, kh) * wts
        num = (jnp.einsum('bhts,bhse->bhte', qk, vh)
               + inter[..., None] * jnp.einsum('bhtd,bhde->bhte', qh, cm))
        den = jnp.sum(qk, axis=-1) + inter * jnp.einsum('bhtd,bhd->bht', qh, nm)
        hout = num / jnp.maximum(jnp.abs(den), jnp.exp(-m_t))[..., None]
        m_new = m_t[..., -1]
        ws = jnp.exp(b[..., -1:] - b + ih - m_new[..., None])
        cs = jnp.exp(b[..., -1] + mm - m_new)
        cm = cm * cs[..., None, None] + jnp.einsum('bhs,bhsd,bhse->bhde', ws, kh, vh)
        nm = nm * cs[..., None] + jnp.einsum('bhs,bhsd->bhd', ws, kh)
        return (cm, nm, m_new), jnp.swapaxes(hout, 1, 2)

    (cm, nm, mm), h = lax.scan(body, (c0, n0, m0),
                               (to_chunks(q, chunk), to_chunks(k, chunk), to_chunks(v, chunk),
                                to_chunks(logi, chunk), to_chunks(logf, chunk)))
    return from_chunks(h), cm, nm, mm

def token_mixers(h, pos, p, st, chunk):
    f32 = jnp.float32
    bsz, L, _ = h.shape
    proj = (h @ p['w_in']).astype(f32)
    ret_p, ssm_p, gdn_p, ml_p = _split(proj, [RET_IN, SSM_IN, GDN_IN, MLSTM_IN])
    heads = lambda t: t.reshape(bsz, L, N_HEADS, -1)
    flat = lambda t: t.reshape(bsz, L, GROUP_W)

    rq, rk, rv, rg = _split(ret_p, [GROUP_W] * 4)
    rq = rotary(heads(rq), pos)
    rk = rotary(heads(rk), pos) * HEAD_DIM ** -0.5
    ro, ret_s = retention_chunked(rq, rk, heads(rv), st[0].astype(f32), chunk)
    out_ret = head_rmsnorm(flat(ro), p['ret_norm']) * jax.nn.silu(rg)

    z, xbc, dt_raw = _split(ssm_p, [GROUP_W, SSM_CONV_CH, N_HEADS])
    xbc, ssm_buf = causal_conv(xbc, st[2].astype(f32), p['ssm_conv_w'])
    xbc = jax.nn.silu(xbc + p['ssm_conv_b'])
    xs, bm, cm = _split(xbc, [GROUP_W, SSM_GROUPS * SSM_STATE, SSM_GROUPS * SSM_STATE])
    rep = N_HEADS // SSM_GROUPS
    bm = jnp.repeat(bm.reshape(bsz, L, SSM_GROUPS, SSM_STATE), rep, axis=2)
    cm = jnp.repeat(cm.reshape(bsz, L, SSM_GROUPS, SSM_STATE), rep, axis=2)
    dt = jax.nn.softplus(dt_raw + p['ssm_dt_bias'])
    A = -jnp.exp(p['ssm_A_log'].astype(f32))
    xh = heads(xs)
    y, ssm_h = ssd_chunked(xh, dt, A, bm, cm, st[1].astype(f32), chunk)
    y = y + p['ssm_D'][:, None] * xh
    out_ssm = rmsnorm(flat(y) * jax.nn.silu(z), p['ssm_norm'])

    qkv, gg, ga, gb = _split(gdn_p, [GDN_CONV_CH, GROUP_W, N_HEADS, N_HEADS])
    qkv, gdn_buf = causal_conv(qkv, st[4].astype(f32), p['gdn_conv_w'])
    qkv = jax.nn.silu(qkv)
    gq, gk, gv = _split(qkv, [GROUP_W] * 3)
    gq = l2norm(heads(gq)) * HEAD_DIM ** -0.5
    gk = l2norm(heads(gk))
    beta = jax.nn.sigmoid(gb)
    glog = -jnp.exp(p['gdn_A_log'].astype(f32)) * jax.nn.softplus(ga + p['gdn_dt_bias'])
    go, gdn_s = gated_delta_chunked(gq, gk, heads(gv), glog, beta, st[3].astype(f32), chunk)
    out_gdn = head_rmsnorm(flat(go), p['gdn_norm']) * jax.nn.silu(gg)

    mq, mk, mv, mo, mi, mf = _split(ml_p, [GROUP_W] * 4 + [N_HEADS] * 2)
    logi = mi + p['mlstm_i_bias']
    logf = jax.nn.log_sigmoid(mf + p['mlstm_f_bias'])
    mh, m_c, m_n, m_m = mlstm_chunked(heads(mq), heads(mk) * HEAD_DIM ** -0.5, heads(mv), logi, logf,
                                      st[5].astype(f32), st[6].astype(f32), st[7].astype(f32), chunk)
    out_ml = jax.nn.sigmoid(mo) * head_rmsnorm(flat(mh), p['mlstm_norm'])

    mixed = jnp.concatenate([out_ret, out_ssm, out_gdn, out_ml], axis=-1).astype(h.dtype) @ p['w_out']
    return mixed, (ret_s, ssm_h, ssm_buf, gdn_s, gdn_buf, m_c, m_n, m_m)

def swiglu(h, wg, wu, wd):
    return (jax.nn.silu(h @ wg) * (h @ wu)) @ wd

def run_trunk(x, pos, states, params, chunk):
    new = []
    for l in range(DEPTH):
        p = {name: arr[l] for name, arr in params.items()}
        st = tuple(s[l] for s in states)
        ns = p['norm_sandwich']
        hdn = rmsnorm(x, ns[0])
        x = x + 0.5 * rmsnorm(swiglu(hdn, p['ffn_w_gate'][0], p['ffn_w_up'][0], p['ffn_w_down'][0]), ns[1])
        hdn = rmsnorm(x, ns[2])
        mix, st_new = token_mixers(hdn, pos, p, st, chunk)
        x = x + rmsnorm(mix, ns[3])
        hdn = rmsnorm(x, ns[4])
        x = x + 0.5 * rmsnorm(swiglu(hdn, p['ffn_w_gate'][1], p['ffn_w_up'][1], p['ffn_w_down'][1]), ns[5])
        new.append(st_new)
    stacked = tuple(jnp.stack([n[i] for n in new], axis=0) for i in range(8))
    return x, stacked

def zero_states(b):
    f = jnp.float32
    return (jnp.zeros((DEPTH, b, N_HEADS, HEAD_DIM, HEAD_DIM), f),
            jnp.zeros((DEPTH, b, N_HEADS, HEAD_DIM, SSM_STATE), f),
            jnp.zeros((DEPTH, b, CONV_W - 1, SSM_CONV_CH), f),
            jnp.zeros((DEPTH, b, N_HEADS, HEAD_DIM, HEAD_DIM), f),
            jnp.zeros((DEPTH, b, CONV_W - 1, GDN_CONV_CH), f),
            jnp.zeros((DEPTH, b, N_HEADS, HEAD_DIM, HEAD_DIM), f),
            jnp.zeros((DEPTH, b, N_HEADS, HEAD_DIM), f),
            jnp.zeros((DEPTH, b, N_HEADS), f))

def setup_inputs(seed: int = 0) -> dict:
    key = jax.random.key(seed)
    ks = jax.random.split(key, 32)
    f = jnp.float32

    def nrm(i, shape, scale):
        return scale * jax.random.normal(ks[i], shape, f)

    def gain(i, shape):
        return 1.0 + 0.05 * jax.random.normal(ks[i], shape, f)

    def dt_bias(i):
        dt = jnp.exp(jax.random.uniform(ks[i], (DEPTH, N_HEADS), f, math.log(1e-3), math.log(1e-1)))
        return dt + jnp.log(-jnp.expm1(-dt))

    def a_log(i):
        return jnp.log(jax.random.uniform(ks[i], (DEPTH, N_HEADS), f, 1.0, 16.0))

    return {
        "x_prompt": nrm(0, (BATCH, SEQ, D_MODEL), 1.0),
        "x_sample": nrm(1, (DEC_BATCH, DEC_SEQ, D_MODEL), 1.0),
        "state_ret": nrm(2, (DEPTH, DEC_BATCH, N_HEADS, HEAD_DIM, HEAD_DIM), 0.5),
        "state_ssm": nrm(3, (DEPTH, DEC_BATCH, N_HEADS, HEAD_DIM, SSM_STATE), 0.5),
        "state_ssm_conv": nrm(4, (DEPTH, DEC_BATCH, CONV_W - 1, SSM_CONV_CH), 1.0),
        "state_gdn": nrm(5, (DEPTH, DEC_BATCH, N_HEADS, HEAD_DIM, HEAD_DIM), 0.2),
        "state_gdn_conv": nrm(6, (DEPTH, DEC_BATCH, CONV_W - 1, GDN_CONV_CH), 1.0),
        "state_mlstm_C": nrm(7, (DEPTH, DEC_BATCH, N_HEADS, HEAD_DIM, HEAD_DIM), 0.5),
        "state_mlstm_n": nrm(8, (DEPTH, DEC_BATCH, N_HEADS, HEAD_DIM), 0.5),
        "state_mlstm_m": nrm(9, (DEPTH, DEC_BATCH, N_HEADS), 1.0),
        "w_in": nrm(10, (DEPTH, D_MODEL, IN_DIM), D_MODEL ** -0.5),
        "w_out": nrm(11, (DEPTH, MIX_W, D_MODEL), MIX_W ** -0.5),
        "norm_sandwich": gain(12, (DEPTH, 6, D_MODEL)),
        "ffn_w_gate": nrm(13, (DEPTH, 2, D_MODEL, D_FF), D_MODEL ** -0.5),
        "ffn_w_up": nrm(14, (DEPTH, 2, D_MODEL, D_FF), D_MODEL ** -0.5),
        "ffn_w_down": nrm(15, (DEPTH, 2, D_FF, D_MODEL), D_FF ** -0.5),
        "ret_norm": gain(16, (DEPTH, GROUP_W)),
        "ssm_conv_w": nrm(17, (DEPTH, CONV_W, SSM_CONV_CH), CONV_W ** -0.5),
        "ssm_conv_b": nrm(18, (DEPTH, SSM_CONV_CH), 0.02),
        "ssm_dt_bias": dt_bias(19),
        "ssm_A_log": a_log(20),
        "ssm_D": 1.0 + 0.1 * jax.random.normal(ks[21], (DEPTH, N_HEADS), f),
        "ssm_norm": gain(22, (DEPTH, GROUP_W)),
        "gdn_conv_w": nrm(23, (DEPTH, CONV_W, GDN_CONV_CH), CONV_W ** -0.5),
        "gdn_dt_bias": dt_bias(24),
        "gdn_A_log": a_log(25),
        "gdn_norm": gain(26, (DEPTH, GROUP_W)),
        "mlstm_i_bias": nrm(27, (DEPTH, N_HEADS), 0.1),
        "mlstm_f_bias": jnp.linspace(3.0, 6.0, N_HEADS, dtype=f)[None, :] + nrm(28, (DEPTH, N_HEADS), 0.1),
        "mlstm_norm": gain(29, (DEPTH, GROUP_W)),
    }

def reference(x_prompt, x_sample, state_ret, state_ssm, state_ssm_conv, state_gdn, state_gdn_conv,
              state_mlstm_C, state_mlstm_n, state_mlstm_m, w_in, w_out, norm_sandwich,
              ffn_w_gate, ffn_w_up, ffn_w_down, ret_norm, ssm_conv_w, ssm_conv_b, ssm_dt_bias,
              ssm_A_log, ssm_D, ssm_norm, gdn_conv_w, gdn_dt_bias, gdn_A_log, gdn_norm,
              mlstm_i_bias, mlstm_f_bias, mlstm_norm):
    params = dict(w_in=w_in, w_out=w_out, norm_sandwich=norm_sandwich, ffn_w_gate=ffn_w_gate,
                  ffn_w_up=ffn_w_up, ffn_w_down=ffn_w_down, ret_norm=ret_norm,
                  ssm_conv_w=ssm_conv_w, ssm_conv_b=ssm_conv_b, ssm_dt_bias=ssm_dt_bias,
                  ssm_A_log=ssm_A_log, ssm_D=ssm_D, ssm_norm=ssm_norm, gdn_conv_w=gdn_conv_w,
                  gdn_dt_bias=gdn_dt_bias, gdn_A_log=gdn_A_log, gdn_norm=gdn_norm,
                  mlstm_i_bias=mlstm_i_bias, mlstm_f_bias=mlstm_f_bias, mlstm_norm=mlstm_norm)

    lp = x_prompt.shape[1]
    pos_p = jnp.arange(lp, dtype=jnp.int32)
    y_prompt, pst = run_trunk(x_prompt, pos_p, zero_states(x_prompt.shape[0]), params, pick_chunk(lp))
    p_ret, p_ssm, p_ssm_conv, p_gdn, p_gdn_conv, p_mC, p_mn, p_mm = pst

    ls = x_sample.shape[1]
    pos_s = PAST_LEN + jnp.arange(ls, dtype=jnp.int32)
    states_s = (state_ret, state_ssm, state_ssm_conv, state_gdn, state_gdn_conv,
                state_mlstm_C, state_mlstm_n, state_mlstm_m)
    y_sample, sst = run_trunk(x_sample, pos_s, states_s, params, pick_chunk(ls))
    s_ret, s_ssm, s_ssm_conv, s_gdn, s_gdn_conv, s_mC, s_mn, s_mm = sst

    return (y_prompt, y_sample, p_ret, p_ssm, p_ssm_conv, p_gdn, p_gdn_conv, p_mC, p_mn, p_mm,
            s_ret, s_ssm, s_ssm_conv, s_gdn, s_gdn_conv, s_mC, s_mn, s_mm)


_drawn_inputs = setup_inputs


def setup_inputs(seed=0):
    import zlib

    import numpy as np

    out = dict(_drawn_inputs(seed))
    spreads = {}
    factors = {'ssm_D': 4.676, 'gdn_norm': 2.713, 'mlstm_norm': 2.78}
    for name, (base, spread) in spreads.items():
        noise = np.random.default_rng([zlib.crc32(name.encode()), seed]).standard_normal(out[name].shape)
        drawn = base * np.exp(spread * noise) if base else spread * noise
        out[name] = __import__('jax').numpy.asarray(drawn.astype(out[name].dtype))
    for name, factor in factors.items():
        out[name] = (out[name] * factor).astype(out[name].dtype)
    return out
```

```python
from contextlib import ExitStack

import numpy as np

import concourse.bass as bass
from concourse import mybir

F32 = mybir.dt.float32
ALU = mybir.AluOpType
ACT = mybir.ActivationFunctionType
AX = mybir.AxisListType.X
P = 128

D = 1024
KT = D // P
SEQ = 256
DEPTH = 2
NB, LS = 8, 4
PAST = 2048
NS = NB * LS
T = SEQ + NS
H, HD = 4, 64
GW = 256
FF = 2816
FT = FF // P
RET_IN = 4 * GW
SSM_CH = GW + 4 * HD
GDN_CH = 3 * GW
Z0 = RET_IN
XBC0 = Z0 + GW
DT0 = XBC0 + SSM_CH
GDN0 = DT0 + H
GG0 = GDN0 + GDN_CH
GAB0 = GG0 + GW
ML0 = GAB0 + 2 * H
MIF0 = ML0 + 4 * GW
IN_DIM = MIF0 + 2 * H
EPS = 1e-6
NEG = -1.0e30
HE = HD + 1

CH = [(0, 128), (128, 128), (256, 32)]
GDN_T, SSD_T, RET_T, ML_T = 0, 8, 14, 22
NPT = 30
BLOCKS = ([GDN0 + GW * i for i in range(4)] + [XBC0, XBC0 + GW, Z0] + [GW * i for i in range(4)]
          + [ML0 + GW * i for i in range(4)])
CONV_T = [0, 1, 2, 3, 4, 5, 8, 9, 10, 11]
NC = len(CONV_T)
SILU_T = (6, 7, 12, 13, 20, 21)
MIX = ("gdn", "ssd", "ret", "ml")
OUT_T = {"ret": 0, "ssd": 2, "gdn": 4, "ml": 6}

RING = 4
SLOT = KT * 256
DOWN = (8, 8, 6)
PAIRS = FT // 2
FFN_SLOTS = 2 * PAIRS + 4 * len(DOWN)
N_IN = len(BLOCKS)
POS_FFN = (0, FFN_SLOTS + N_IN + 4)
POS_IN = FFN_SLOTS
POS_OUT = POS_IN + N_IN
POSITIONS = 2 * FFN_SLOTS + N_IN + 5
assert POSITIONS % RING == 0
PER_SLOT = POSITIONS // RING
H_CREDIT = 2
Y_CREDIT = 4
FREE = 1


def constants():
    i = np.arange(P)
    same = (i[:, None] // LS == i[None, :] // LS) & (i[:, None] < NS) & (i[None, :] < NS)
    lg = np.log(1.0 - np.exp2(-5.0 - np.arange(H)))
    c = {}
    c["ident"] = np.eye(P)
    c["ones"] = np.ones((P, P))
    c["bdones"] = (i[:, None] // HD == i[None, :] // HD)
    rot = np.zeros((P, P))
    for d in range(P):
        if d % HD < HD // 2:
            rot[d + HD // 2, d] = -1
        else:
            rot[d - HD // 2, d] = 1
    c["rot"] = rot
    le = i[:, None] <= i[None, :]
    c["tri"] = le
    c["tri_s"] = le & same
    c["blk_s"] = same
    c["neg"] = np.where(le, 0, NEG)
    c["neg_s"] = np.where(le & same, 0, NEG)[:, :NS]
    lv = np.zeros((P, 7, P))
    for k in range(7):
        s = 1 << k
        t, u = i[:, None], i[None, :]
        lv[:, k] = (t // (2 * s) == u // (2 * s)) & (t % (2 * s) >= s) & (u % (2 * s) < s)
    c["level"] = lv.reshape(P, -1)
    pos = np.concatenate([np.arange(SEQ), PAST + np.arange(NS) % LS]).astype(np.float32)
    inv = np.float32(10000.0) ** (-np.arange(HD // 2, dtype=np.float32) / np.float32(HD // 2))
    ang = (inv[i % (HD // 2)][:, None] * pos[None, :]).astype(np.float32).astype(np.float64)
    c["cos"], c["sin"] = np.cos(ang), np.sin(ang)
    dp = np.zeros((P, H, P))
    ds = np.zeros((P, H, NS))
    for h in range(H):
        dp[:, h] = np.where(le, np.exp(np.where(le, i[None, :] - i[:, None], 0) * lg[h]), 0)
        ds[:, h] = np.where(le & same, np.exp(np.where(le, i[None, :] - i[:, None], 0) * lg[h]), 0)[:, :NS]
    c["ret_d"], c["ret_ds"] = dp.reshape(P, -1), ds.reshape(P, -1)
    inter = np.zeros((P, 2, P + NS))
    for a in range(2):
        for b in range(2):
            inter[b * HD:(b + 1) * HD, a] = np.exp(
                np.concatenate([i + 1, np.arange(NS) % LS + 1]) * lg[2 * a + b])
    c["ret_inter"] = inter.reshape(P, -1)
    tail = np.zeros((P, 3, H))
    tail[:, 0] = tail[:, 1] = np.exp((P - 1 - i)[:, None] * lg)
    tail[:, 2] = np.where(i[:, None] < NS, np.exp((LS - 1 - i % LS)[:, None] * lg), 0)
    c["ret_tail"] = tail.reshape(P, -1)
    c["ret_dec"] = np.exp(P * lg)[2 * np.arange(2)[None, :] + i[:, None] // HD]
    c["ret_decs"] = np.broadcast_to(np.exp(LS * lg), (P, H))
    dup = np.zeros((P, 2, P))
    for b in range(2):
        dup[:, b] = (i[:, None] // HD == b) & (i[:, None] % HD == i[None, :] % HD)
    c["dup"] = dup.reshape(P, -1)
    tok = np.arange(NS)
    bm = (tok[None, None, :] // LS == 2 * np.arange(4)[None, :, None] + i[:, None, None] // HD)
    c["bmask"] = bm.reshape(P, -1)
    c["onehot"] = (i[:, None] // LS == np.arange(NB)[None, :])
    c["blsel"] = ((i[:, None] // LS) % 2 == i[None, :] // HD) & (i[:, None] < NS)
    c["obp"] = (i[:, None] // (2 * LS) == np.arange(4)[None, :])
    c["first"] = (i[:, None] // (2 * LS) == np.arange(4)[None, :]) & (i[:, None] % LS == 0)
    s2 = np.zeros((P, 2, P))
    for h in range(H):
        s2[h, h // 2, (h % 2) * HD:(h % 2 + 1) * HD] = 1
    c["nident"], c["sel2"] = -np.eye(P)[:, :H], s2.reshape(P, -1)
    reset = np.zeros((P, T))
    reset[:, SEQ::LS] = NEG
    c["reset"] = reset
    sign = np.ones((P, 5, H))
    sign[:, 2:4] = -1
    c["sign"] = sign.reshape(P, -1)
    return {k: np.ascontiguousarray(v, dtype=np.float32) for k, v in c.items()}


CONST = constants()
CONST_AT, _at = {}, 0
for _n, _v in CONST.items():
    CONST_AT[_n] = (_at, _v.shape[1])
    _at += _v.shape[1]
CONST_W = _at

CHAIN = {"dve": 95, "act": 20}
STRICT = True
PS_BEFORE = {"gdn": 0, "ssd": 32, "ret": 64, "ml": 96}
PSTORES = 96 + 64
SSTORES = 16 * (5 * NB + 1 + NB)


def trunk_kernel(nc, I, O):
    ctx = ExitStack()
    with ctx:
        used = {}

        def sb(name, shape):
            return ctx.enter_context(nc.sbuf_tensor(name, shape, F32))

        def sem(name):
            if name not in used:
                used[name] = ctx.enter_context(nc.semaphore(name))
            return used[name]

        cst = sb("cst", [P, CONST_W])
        x = sb("x", [P, KT, T])
        hdn = sb("hdn", [P, KT, 3 * P])
        big = sb("big", [P, NPT, T])
        y = sb("y", [P, KT, T])
        ring = sb("ring", [P, RING, SLOT])
        rrow = sb("rrow", [P, T])
        lnr = sb("lnr", [P, T])
        ssum = sb("ssum", [P, T])
        sq = sb("sq", [P, 2, T])
        sg = sb("sg", [P, 2, T])
        gn = sb("gn", [P, DEPTH, 6, KT])
        p2 = sb("p2", [P, DEPTH, 52])
        gcol = sb("gcol", [P, 6, KT])
        ghalf = sb("ghalf", [P, 6, KT])
        pcol = sb("pcol", [P, 52])
        taps = sb("taps", [P, NC, 4])
        cbias = sb("cbias", [P, NC])
        wg2 = sb("wg2", [P, DEPTH, KT, 20])
        wg = sb("wg", [P, KT, 20])
        gb2 = sb("gb2", [P, DEPTH, 20])
        al2 = sb("al2", [P, DEPTH, 12])
        sd2 = sb("sd2", [P, DEPTH, H])
        gbias = sb("gbias", [P, 20])
        alog = sb("alog", [P, 12])
        sD = sb("sD", [P, H])
        epsc = sb("epsc", [P, 1])
        stage = sb("stage", [104, P])
        lastT = sb("lastT", [27, NC, P])
        hist = lastT[0:NB * 3]
        xP = sb("xP", [P, NC, 3 + SEQ])
        xS = sb("xS", [P, NC, NB, 3 + LS])
        last = sb("last", [P, NC, 27])
        U = sb("U", [P, 3, 20])
        AB = sb("AB", [P, 3, 12])
        SP = sb("SP", [P, 3, 12])
        G = sb("G", [P, 3, 12])
        beta = sb("beta", [P, 3, H])
        cum = sb("cum", [P, 3, 12])
        wexp = sb("wexp", [P, 3, 12])
        onfin = sb("onfin", [P, 3 * GW + 2 * P])
        on = onfin[:, 0:3 * GW].rearrange("p (c n) -> p c n", c=3)
        fin = onfin[0:HD, 3 * GW:].rearrange("p (a n) -> p a n", a=2)
        Gb = onfin[:, :].rearrange("p (c s d) -> p c s d", c=2, s=8)
        er = sb("er", [P, 6, P + NS])
        decP = sb("decP", [P, 6])
        Gx = sb("Gx", [NS, 64])
        decS = sb("decS", [P, 64])
        aT = sb("aT", [P, 3, H])
        aH = sb("aH", [H, T])
        mH = sb("mH", [H, T])
        mL = sb("mL", [H, T])
        mPv = sb("mPv", [H, T])
        eI = aH
        eD = mPv
        mm = sb("mm", [H, DEPTH, NB])
        mmc = sb("mmc", [H, NB])
        mTok = sb("mTok", [P, 3, 3, H])
        mt = sb("mt", [P, 3, H])
        emt = sb("emt", [P, 3, H])
        qbd = sb("qbd", [P, 2, 2, T])
        qi = sb("qi", [P, 2, P + NS])
        ki = sb("ki", [P, 2, P + NS])
        V = sb("V", [P, 3, H, HE])
        K = sb("K", [P, 3, GW])
        ctmp = K[:, :, :].rearrange("p c n -> p (c n)")[:, 0:NC * NS].rearrange("p (c b t) -> p c b t", c=NC, b=NB)
        VW = sb("VW", [P, 3, H, HE])
        Bb = VW[:, :, :, :].rearrange("p c h e -> p (c h e)")[:, 0:3 * GW]\
            .rearrange("p (c h d) -> p c h d", c=3, h=H)
        DT = sb("DT", [P, 3, H, P])
        xPf = xP[:, :, :].rearrange("p c n -> p (c n)")
        PT = xPf[:, 0:3 * H * P].rearrange("p (c h n) -> p c h n", c=3, h=H)
        DTf = DT[:, :, :, :].rearrange("p c h n -> p (c h n)")
        Dx = xPf[:, 3 * H * P:3 * H * P + 3 * GW].rearrange("p (c h n) -> p c h n", c=3, h=H)
        xtok_s = big[:, 0:11, :].rearrange("p k t -> p (k t)")[:, 0:3 * D].rearrange("p (c n) -> p c n", c=3)
        Sbd = sb("Sbd", [P, 2, 2, HE])
        S1 = sb("S1", [P, 2, HE])
        SX = [sb(f"Sx{n}", [P, 4, H, HE]) for n in range(2)]
        SX = {m: SX[n % 2] for n, m in enumerate(MIX)}
        snat = sb("snat", [P, H * NB * HD])
        Snat = snat[0:HD, :].rearrange("p (h b n) -> p h b n", h=H, b=NB)
        kbd = snat[:, 0:4 * T].rearrange("p (a b t) -> p a b t", a=2, b=2)
        KQX = snat[:, 4 * T:4 * T + 16 * NS].rearrange("p (h b n) -> p h b n", h=H, b=4)
        atm = sb("atm", [P, 4 * H * P])
        AT = atm[:, 0:2 * H * P].rearrange("p (c h n) -> p c h n", c=2, h=H)
        Tm = atm[:, 2 * H * P:].rearrange("p (c h n) -> p c h n", c=2, h=H)
        KX = atm[0:NS, :].rearrange("p (h b n) -> p h b n", h=H, b=NB)
        QX = xS[:, :, :, :].rearrange("p c b j -> p (c b j)")[:, 0:H * 4 * NS]\
            .rearrange("p (h b n) -> p h b n", h=H, b=4)
        hout = rrow[:, 0:GW]
        osq = ssum[:, 0:GW]
        C4 = sg[:, :, :].rearrange("p a t -> p (a t)")[:, 0:NC * NS].rearrange("p (c b t) -> p c b t", c=NC, b=NB)
        sml = sb("sml", [P, 4, H])
        tiny = sq
        yflat = y[:, :, :].rearrange("p k t -> p (k t)")
        X = yflat[:, 0:8 * P].rearrange("p (s n) -> p s n", n=P)
        XT = yflat[:, 8 * P:16 * P].rearrange("p (c h n) -> p c h n", c=2, h=H)
        Xs, XTs = (yflat[0:NS, (16 + n) * P:(17 + n) * P].rearrange("p (h n) -> p h n", h=H) for n in range(2))
        ATs = sb("ATs", [NS, H, NS])
        Tms = sb("Tms", [NS, H, NS])
        ps = ctx.enter_context(nc.psum_tensor("ps", [P, 8, 512], F32))

        def C(name, rows=P):
            at, w = CONST_AT[name]
            return cst[0:rows, at:at + w]

        ident, ones, bdones = C("ident"), C("ones"), C("bdones")
        level = C("level").rearrange("p (k n) -> p k n", k=7)
        retD = C("ret_d").rearrange("p (h n) -> p h n", h=H)
        retDs = C("ret_ds").rearrange("p (h n) -> p h n", h=H)
        retI = C("ret_inter").rearrange("p (a n) -> p a n", a=2)
        tail = C("ret_tail").rearrange("p (c h) -> p c h", c=3)
        dup = C("dup").rearrange("p (b n) -> p b n", b=2)
        bmask = C("bmask").rearrange("p (b n) -> p b n", b=4)
        sel2 = C("sel2").rearrange("p (a n) -> p a n", a=2)
        sign = C("sign")
        y4 = None

        def B(bank, *shape, rows=P, off=0):
            n = int(np.prod(shape))
            v = ps[0:rows, bank, off:off + n]
            if len(shape) == 2:
                return v.rearrange("p (a b) -> p a b", a=shape[0])
            if len(shape) == 3:
                return v.rearrange("p (a b c) -> p a b c", a=shape[0], b=shape[1])
            return v

        def bc(ap, dim, n):
            a = ap.unsqueeze(dim)
            s = list(a.shape)
            s[dim] = n
            return a.broadcast_to(s)

        def slots(ap, m):
            if m == "ssd":
                return ap.rearrange("p (b a) n -> p a b n", a=2)
            return ap.rearrange("p (a b) n -> p a b n", a=2)

        def slots1(ap, m):
            if m == "ssd":
                return ap.rearrange("p (b a) -> p a b", a=2)
            return ap.rearrange("p (a b) -> p a b", a=2)

        def head(m, a, b):
            return 2 * b + a if m == "ssd" else 2 * a + b

        QT = {"gdn": 0, "ssd": 11, "ret": 14, "ml": 22}
        KTL = {"gdn": 2, "ssd": 10, "ret": 16, "ml": 24}
        VTL = {"gdn": 4, "ssd": 8, "ret": 18, "ml": 26}
        GATE = {"gdn": 6, "ssd": 12, "ret": 20, "ml": 28}
        DC = {"ssd": 0, "gdn": 4, "ml": 8}
        HW = {m: (HE if m == "ml" else HD) for m in MIX}
        NORM = {"ret": 0, "ssd": 2, "gdn": 4, "ml": 6}
        OUTB = {"gdn": (1, 4), "ssd": (5, 6), "ret": (5, 6), "ml": (5, 6)}

        def LB(kind, c, L):
            if c == 2:
                return B(6, H, NS, rows=NS, off=P * kind)
            return B(((0, 1), (2, 5), (7, 4))[kind][c], H, P)

        w_in_s = [sem(f"weights_loaded_{s}") for s in range(RING)]

        def ring_pos(l, pos):
            s, i = pos % RING, pos // RING
            per = PER_SLOT - (1 if s == (POSITIONS - 1) % RING else 0)
            return s, (l * per + i + 1) * 16

        ctx.enter_context(nc.allow_non_contiguous_dma(reason="a few small states with heads or features on partitions"))
        block = ctx.enter_context(nc.Block())

        @block.sync
        def _(sp):
            def load(l, pos, rows, src, j=0):
                s = pos % RING
                sp.dma_start(ring[:, s, 0:rows * 256].rearrange("p (k n) -> p k n", k=rows),
                             src).then_inc(w_in_s[s], 16)

            def products_read(l, post, m):
                sp.wait_ge(sem("y_done"), l * 24 + post * 8 + m + Y_CREDIT)

            def ffn(l, f):
                wgd = I["ffn_w_gate"][bass.ds(l, 1), f].rearrange("o (k p) n -> p (o k) n", p=P)
                wud = I["ffn_w_up"][bass.ds(l, 1), f].rearrange("o (k p) n -> p (o k) n", p=P)
                wdd = I["ffn_w_down"][bass.ds(l, 1), f].rearrange("o (k p) n -> p (o k) n", p=P)
                pos, post = POS_FFN[f], 2 * f
                h0 = l * 2 * FT + f * FT
                before = (0, 0, 0, 0) if f == 0 else (8 + 2, 8 + 4, 8 + 6, 8 + 8)
                for t in range(2):
                    for n, w in enumerate((wgd, wud)):
                        sp.wait_ge(sem("y_done"), l * 24 + Y_CREDIT + before[2 * t + n])
                        load(l, pos + 2 * t + n, KT, w[:, :, 256 * t:256 * t + 256])
                with sp.Fori(1, PAIRS // 2) as j:
                    for t in range(2):
                        sp.wait_ge(sem("h_done"), h0 + j * 4 + 2 * t - 2 + H_CREDIT)
                        for n, w in enumerate((wgd, wud)):
                            load(l, pos + 2 * t + n, KT, w[:, :, bass.ds(j * 512 + 256 * t, 256)])
                pos += 4 * (PAIRS // 2)
                sp.wait_ge(sem("h_done"), h0 + 2 * PAIRS - 4 + H_CREDIT)
                for n, w in enumerate((wgd, wud)):
                    load(l, pos + n, KT, w[:, :, FF - 256:FF])
                pos += 2
                for mp in range(4):
                    for part, n in enumerate(DOWN):
                        i = 3 * mp + part
                        if i < RING:
                            sp.wait_ge(sem("h_done"), h0 + 2 * PAIRS - 2 + 2 * (i // 2) + H_CREDIT)
                        else:
                            products_read(l, post, 2 * ((i - RING) // 3) + 2)
                        load(l, pos + i, n, wdd[:, 8 * part:8 * part + n, 256 * mp:256 * mp + 256])

            with sp.Fori(0, DEPTH) as l:
                ffn(l, 0)
                win = I["w_in"][bass.ds(l, 1)].rearrange("o (k p) n -> p (o k) n", p=P)
                for i, c0 in enumerate(BLOCKS):
                    if i < 4:
                        products_read(l, 0, 2 * ((8 + i) // 3) + 2)
                    else:
                        sp.wait_ge(sem("proj_read"), l * NPT + 2 * i - 6)
                        sp.sem_inc(sem("sp_held"), 1)
                    load(l, POS_IN + i, KT, win[:, :, c0:c0 + 256])
                wo = I["w_out"][bass.ds(l, 1)].rearrange("o (k p) n -> p (o k) n", p=P)
                for i in range(4):
                    sp.wait_ge(sem("proj_read"), l * NPT + 2 * (N_IN - 4 + i) + 2)
                    load(l, POS_OUT + i, KT, wo[:, :, 256 * i:256 * i + 256])
                ffn(l, 1)

        @block.tensor
        def _(pe):
            def mm(out, lhsT, rhs, start=True, stop=True, **k):
                return pe.matmul(out, lhsT, rhs, start=start, stop=stop, **k)

            def tr(out, in_):
                return pe.transpose(out, in_, ident[0:in_.shape[0], 0:in_.shape[0]])

            def hold(s, v):
                pe.wait_ge(s, v)
                pe.sem_inc(sem("pe_held"), 1)

            def slot_ready(l, pos, extra=0):
                s, v = ring_pos(l, pos)
                pe.wait_ge(w_in_s[s], v + extra)
                return s

            pe.sem_inc(sem("sadd_done"), FREE)
            pe.wait_ge(sem("const_loaded"), 16)
            pe.wait_ge(sem("gain_rows_loaded"), 16)
            tr(B(0, 96), stage[0:96, :]).then_inc(sem("gains_turned"), 1)
            pe.wait_ge(sem("param_rows_loaded"), 14 * 16)
            tr(B(1, 104), stage[0:104, :]).then_inc(sem("params_turned"), 1)
            pe.wait_ge(sem("x_loaded"), 32)
            for k in range(KT):
                if k < 2:
                    pe.wait_ge(sem("params_placed"), 2)
                for c, (o, L) in enumerate(CH):
                    last_mm = tr(ps[:, k, o:o + L], xtok_s[0:L, c, k * P:(k + 1) * P])
                last_mm.then_inc(sem("x_turned"), 1)

            pe.wait_ge(sem("x_done"), KT)

            def ffn(l, f):
                pre = 0 if f == 0 else 2
                post = 0 if f == 0 else 2

                def pair(pos, tile0, j):
                    ga = ring[:, pos % RING, 0:KT * 256].rearrange("p (k n) -> p k n", k=KT)
                    up = ring[:, (pos + 1) % RING, 0:KT * 256].rearrange("p (k n) -> p k n", k=KT)
                    for t in range(2):
                        pe.wait_ge(sem("h_done"), tile0 + t + 1)
                        bank = 2 * t
                        if t == 0:
                            slot_ready(l, pos, extra=j * 16)
                        for k in range(KT):
                            g = mm(ps[:, bank, 0:T], ga[:, k, t * P:(t + 1) * P], hdn[:, k, 0:T],
                                   k == 0, k == KT - 1)
                        g.then_inc(sem("gate_done"), 1)
                        if t == 0:
                            slot_ready(l, pos + 1, extra=j * 16)
                        for k in range(KT):
                            u = mm(ps[:, bank + 1, 0:T], up[:, k, t * P:(t + 1) * P], hdn[:, k, 0:T],
                                   k == 0, k == KT - 1)
                        u.then_inc(sem("up_done"), 1)

                base = POS_FFN[f]
                hold(sem("hdn_ready"), l * 24 + pre * 8 + 8)
                with pe.Fori(0, PAIRS // 2) as j:
                    for t in range(2):
                        pair(base + 2 * t, l * 44 + f * 22 + j * 4 + 2 * t, j)
                pair(base + 4 * (PAIRS // 2), l * 44 + f * 22 + 20, 0)
                pos = base + 2 * PAIRS
                pe.wait_ge(sem("h_done"), l * 44 + f * 22 + 22 + H_CREDIT)
                for mp in range(4):
                    for half, nk in enumerate(DOWN):
                        s = slot_ready(l, pos + 3 * mp + half)
                        wd = ring[:, s, 0:nk * 256].rearrange("p (k n) -> p k n", k=nk)
                        for t in range(2):
                            m = 2 * mp + t
                            if half == 0:
                                pe.wait_ge(sem("y_done"), l * 24 + post * 8 + m + 1)
                            for k in range(nk):
                                d = mm(ps[:, m % 4, 0:T], wd[:, k, t * P:(t + 1) * P],
                                       big[:, 8 * half + k, :], half == 0 and k == 0,
                                       half == 2 and k == nk - 1)
                            if half == 2:
                                d.then_inc(sem("post_product_done"), 1)

            def norm_post(l, post):
                pe.wait_ge(sem("squares_added"), l * 24 + post * 8 + 8)
                mm(ps[:, 4, 0:T], ones, ssum[:, :]).then_inc(sem("norm_sum"), 1)

            def norm_pre(l, pre):
                for k in range(KT):
                    pe.wait_ge(sem("x_squared"), l * 24 + pre * 8 + k + 1)
                    n = mm(ps[:, 4, 0:T], ones, y[:, k, :], k == 0, k == KT - 1)
                n.then_inc(sem("norm_sum"), 1)

            def mixers(l):
                l1 = l + 1
                hold(sem("hdn_ready"), l * 24 + 8 + 8)
                hold(sem("layer_params"), l1)
                for c in range(3):
                    for k in range(KT):
                        g = mm(ps[:, 5, 20 * c:20 * c + 20], hdn[:, k, c * P:(c + 1) * P], wg[:, k, :],
                               k == 0, k == KT - 1)
                g.then_inc(sem("gates_done"), 1)
                hold(sem("hist_loaded"), l1 * 32)
                for t in range(NC):
                    g = tr(B(6, NC, NB * 3)[:, t, :], hist[:, t, :])
                g.then_inc(sem("hist_turned"), 1)
                for i in range(NPT):
                    if i >= 4:
                        pe.wait_ge(sem("proj_read"), l * NPT + i - 3)
                    if i % 2 == 0:
                        s = slot_ready(l, POS_IN + i // 2)
                    w = ring[:, s, 0:KT * 256].rearrange("p (k n) -> p k n", k=KT)
                    for k in range(KT):
                        g = mm(ps[:, i % 4, 0:T], w[:, k, (i % 2) * P:(i % 2 + 1) * P], hdn[:, k, 0:T],
                               k == 0, k == KT - 1)
                    g.then_inc(sem("proj_done"), 1)
                hold(sem("proj_read"), l * NPT + NPT)
                hold(sem("decays_ready"), l1)
                cb, tb = B(4, 3, 12), B(7, 3, 12)
                mm(cb[:, 0, :], C("tri"), G[:, 0, :])
                mm(cb[:, 1, :], C("tri"), G[:, 1, :], True, False)
                mm(cb[:, 1, 8:12], ones, G[:, 0, 8:12], False, True)
                mm(cb[:, 2, :], C("tri_s"), G[:, 2, :])
                mm(tb[:, 0, :], ones, G[:, 0, :])
                mm(tb[:, 1, :], ones, G[:, 1, :])
                mm(tb[:, 2, :], C("blk_s"), G[:, 2, :]).then_inc(sem("cum_done"), 1)
                hold(sem("decays_spread"), l1)
                for n in range(4):
                    e = ps[:, n // 2, 160 * (n % 2):160 * (n % 2) + 160]
                    mm(e[:, 0:P], Gb[:, 0, 2 * n:2 * n + 2, :].rearrange("p s d -> p (s d)"), C("tri"))
                    mm(e[:, P:], Gb[:, 1, 2 * n:2 * n + 2, :].rearrange("p s d -> p (s d)"),
                       C("tri_s")[:, 0:NS])
                    mm(ps[:, 2, n:n + 1], Gb[:, 0, 2 * n:2 * n + 2, :].rearrange("p s d -> p (s d)"),
                       ones[:, 0:1])
                mm(ps[:, 3, 0:16], C("blsel", NS), Gx[:, 0:16])
                mm(ps[:, 3, 16:48], ones[0:NS, :], Gx[:, 16:48]).then_inc(sem("erow_done"), 1)
                hold(sem("a_ready"), l1)
                for c, (o, L) in enumerate(CH):
                    g = tr(ps[0:H, 5, o:o + L], aT[0:L, c, :])
                g.then_inc(sem("a_turned"), 1)
                hold(sem("m_rows_ready"), l1)
                for n, row in enumerate((mH, mL, eD)):
                    for c, (o, L) in enumerate(CH):
                        g = tr(ps[0:L, 5, 300 + (3 * n + c) * H:300 + (3 * n + c) * H + H], row[:, o:o + L])
                for a in range(2):
                    mm(ps[:, 6, 160 * a:160 * a + 160], sel2[0:H, a, :], eI[:, P:T])
                for a in range(2):
                    g = mm(ps[:, 6, 320 + a:321 + a], sel2[0:H, a, :], eD[:, P:P + 1])
                g.then_inc(sem("m_tok_done"), 1)
                hold(sem("ml_decay_spread"), l1)
                mm(ps[:, 7, 64:80], C("blsel", NS), Gx[:, 48:64]).then_inc(sem("ml_decS_done"), 1)
                hold(sem("qk_squared"), l1)
                hold(sem("er_read"), l1)
                for n in range(4):
                    g = mm(ps[:, n, 0:T], bdones, DTf[:, n * T:(n + 1) * T])
                g.then_inc(sem("qk_norms_done"), 1)
                hold(sem("qk_norms_read"), l1)
                for n in range(4):
                    g = mm(ps[:, n, 0:T], C("rot"), big[:, RET_T + n, :])
                g.then_inc(sem("rotated"), 1)
                for a in range(2):
                    for c, (o, L) in enumerate(CH):
                        g = mm(ps[:, 4 + a, o:o + L],
                               Bb[0:L, c, 2 * a:2 * a + 2, :].rearrange("p h d -> p (h d)"), ident[0:L, 0:L])
                g.then_inc(sem("beta_rows_done"), 1)
                for mi, m in enumerate(MIX):
                    mixer(l, l1, mi, m)
                hold(sem("mixed_ready"), l * 4 + 4 + FREE)
                for t in range(NC):
                    g = tr(ps[0:27, 4 + t // 4, (t % 4) * P:(t % 4 + 1) * P], last[:, t, :])
                g.then_inc(sem("last_turned"), 1)

            def mixer(l, l1, mi, m):
                w = HW[m]
                Sx = SX[m]
                hold(sem("mixed_ready"), l * 4 + mi + FREE)
                hold(sem("qk_ready"), l * 4 + mi + 1)
                for c, (o, L) in enumerate(CH):
                    if c or mi:
                        hold(sem("kv_read"), l * 12 + 3 * mi + c)
                    kts = (KTL[m],) if m == "ssd" else (KTL[m], KTL[m] + 1)
                    for n, t in enumerate(kts):
                        tr(ps[0:L, 4, n * P:(n + 1) * P], big[:, t, o:o + L])
                    for n in range(2):
                        g = tr(ps[0:L, 4, GW + n * P:GW + (n + 1) * P], big[:, VTL[m] + n, o:o + L])
                    g.then_inc(sem("kv_turned"), 1)
                if m != "ret":
                    for c, (o, L) in enumerate(CH):
                        if c:
                            hold(sem("decay_arg"), l * 9 + 3 * [0, 1, 0, 2][mi] + c)
                        for s in range(H):
                            out = ps[0:L, 1, s * L:(s + 1) * L]
                            if m == "ml":
                                g = mm(out, C("nident", H)[:, s:s + 1].broadcast_to([H, L]), mH[:, o:o + L])
                            else:
                                h = head(m, s // 2, s % 2)
                                tri = C("tri") if c < 2 else C("tri_s")[0:NS, 0:NS]
                                g = mm(out, G[0:L, c, DC[m] + h:DC[m] + h + 1].broadcast_to([L, L]), tri)
                        g.then_inc(sem("decay_rows"), 1)
                for s in range(H):
                    g = mm(ps[:, 3, s * NS:(s + 1) * NS], dup[:, s % 2, :], qi[:, s // 2, P:])
                if m == "gdn":
                    for s in range(H):
                        g = mm(ps[:, 3, P + s * NS:P + (s + 1) * NS], dup[:, s % 2, :], ki[:, s // 2, P:])
                g.then_inc(sem("dup_done"), 1)
                if m == "ssd":
                    states_in(l1, m)
                    for bp in range(4):
                        if bp:
                            hold(sem("snat_read"), l * 4 + bp)
                        for s in range(H):
                            h = head(m, s // 2, s % 2)
                            g = tr(ps[:, 5, s * HD:(s + 1) * HD],
                                   Snat[:, h, 2 * bp:2 * bp + 2, :].rearrange("p b n -> p (b n)"))
                        g.then_inc(sem("snat_turned"), 1)
                if m == "gdn":
                    gdn_solve(l, l1)
                for c, (o, L) in enumerate(CH):
                    if c:
                        hold(sem("probs_ready"), l * 12 + 3 * mi + c)
                    if m == "ssd":
                        g = mm(ps[0:L, 0, 0:2 * L], big[:, KTL[m], o:o + L],
                               qbd[:, 0, :, o:o + L])
                    else:
                        for a in range(2):
                            g = mm(ps[0:L, 0, 2 * L * a:2 * L * (a + 1)], big[:, KTL[m] + a, o:o + L],
                                   qbd[:, a, :, o:o + L])
                    g.then_inc(sem("scores_done"), 1)
                    if m == "gdn":
                        if c:
                            if c == 1:
                                for a in range(2):
                                    g = mm(ps[:, 5, a * P:(a + 1) * P], ki[:, a, 0:P],
                                           Sbd[:, a, :, 0:HD])
                            else:
                                states_in(l1, m)
                                for s in range(H):
                                    for bp in range(4):
                                        g = mm(ps[0:NS, 5, s * HD:(s + 1) * HD], KQX[:, s, bp, :],
                                               Sx[:, bp, s, 0:HD], bp == 0, bp == 3)
                            g.then_inc(sem("ks_done"), 1)
                        hold(sem("resid_ready"), l * 3 + c + 1)
                        for s in range(H):
                            xt = XT[:, c, s, :] if c < 2 else XTs[:, s, :]
                            g = mm(ps[0:L, 6, s * HD:(s + 1) * HD], xt, VW[0:L, c, s, 0:HD])
                        g.then_inc(sem("vnew_done"), 1)
                    hold(sem("probs_ready"), l * 12 + 3 * mi + c + 1)
                    hold(sem("values_ready"), l * 12 + 3 * mi + c + 1)
                    if c or mi:
                        hold(sem("on_ready"), l * 12 + 3 * mi + c)
                    if c == 2:
                        states_in(l1, m)
                        hold(sem("qx_ready"), l * 4 + mi + 1)
                    for s in range(H):
                        out = ps[0:L, 2, s * w:(s + 1) * w]
                        if c == 1:
                            b = s % 2
                            mm(out, qi[:, s // 2, 0:P], Sbd[:, s // 2, b, 0:w], True, False)
                        if c == 2:
                            for bp in range(4):
                                mm(out, QX[:, s, bp, :], Sx[:, bp, s, 0:w], bp == 0, False)
                        g = mm(out, PT[0:L, c, s, 0:L], V[0:L, c, s, 0:w], c == 0, True)
                    g.then_inc(sem("out_done"), 1)
                    hold(sem("vw_ready"), l * 12 + 3 * mi + c + 1)
                    if c < 2:
                        if c:
                            hold(sem("state_read"), l * 8 + 2 * mi + c)
                        for s in range(H):
                            a, b = s // 2, s % 2
                            kc = b if m == "ssd" else s
                            g = mm(ps[b * HD:(b + 1) * HD, 7, a * w:(a + 1) * w],
                                   K[:, c, kc * HD:(kc + 1) * HD], VW[:, c, s, 0:w])
                        g.then_inc(sem("state_add"), 1)
                        if c == 0:
                            hold(sem("state_read"), l * 8 + 2 * mi + 1)
                    elif m == "ssd":
                        hold(sem("kx_ready"), l * 4 + mi + 1)
                        for s in range(H):
                            if s:
                                hold(sem("sadd_read"), l * 16 + 4 * mi + s)
                            mm(ps[0:HD, 3, :], VW[0:NS, 2, s, 0:HD],
                               KX[:, s % 2, :, :].rearrange("p b n -> p (b n)")).then_inc(sem("sadd_done"), 1)
                    else:
                        hold(sem("kx_ready"), l * 4 + mi + 1)
                        for bp in range(4):
                            if bp:
                                hold(sem("sadd_read"), l * 16 + 4 * mi + bp)
                            for s in range(H):
                                g = mm(ps[:, 3, s * w:(s + 1) * w],
                                       KX[:, s, 2 * bp:2 * bp + 2, :].rearrange("p b d -> p (b d)"),
                                       VW[0:NS, 2, s, 0:w])
                            g.then_inc(sem("sadd_done"), 1)
                    hold(sem("on_ready"), l * 12 + 3 * mi + c + 1)
                    for n in range(2):
                        g = tr(outT(m, n)[:, o:o + L], on[0:L, c, n * P:(n + 1) * P])
                    g.then_inc(sem("on_turned"), 1)
                if m == "ssd":
                    hold(sem("ssd_squared"), l1)
                    for n in range(2):
                        g = mm(ps[:, 0, 0:T], ones, tiny[:, n, :], n == 0, n == 1)
                    g.then_inc(sem("ssd_sum"), 1)
                    hold(sem("state_read"), l * 8 + 2 * mi + 2)
                    for a in range(2):
                        g = tr(ps[0:HD, 7, a * P:(a + 1) * P], S1[:, a, 0:HD])
                    g.then_inc(sem("ssd_state_turned"), 1)

            def states_in(l1, m):
                hold(sem("states_loaded_" + m), l1 * (256 if m == "ml" else 128))

            def outT(m, n):
                return ps[:, OUTB[m][n], :]

            def gdn_solve(l, l1):
                hold(sem("kbd_ready"), l1)
                for c, (o, L) in enumerate(CH):
                    if c:
                        hold(sem("at_ready"), l * 3 + c)
                    for a in range(2):
                        g = mm(ps[0:L, 0, 2 * L * a:2 * L * (a + 1)], big[:, KTL["gdn"] + a, o:o + L],
                               kbd[:, a, :, o:o + L])
                    g.then_inc(sem("gram_done"), 1)
                hold(sem("at_ready"), l * 3 + 3)
                for k in range(7):
                    cs = (0, 1, 2) if k < 2 else (0, 1)
                    for c in cs:
                        L = CH[c][1]
                        n = k * 3 + c if k < 2 else 6 + (k - 2) * 2 + c
                        if k:
                            hold(sem("x_level"), l * 16 + ([0, 3, 6, 8, 10, 12, 14][k - 1]) + c + 1)
                        for s in range(H):
                            at = AT[:, c, s, :] if c < 2 else ATs[:, s, :]
                            xx = X[:, 4 * c + s, :] if c < 2 else Xs[:, s, :]
                            g = mm(LB(0, c, L)[:, s, :], at, xx)
                        g.then_inc(sem("level_t"), 1)
                    for c in cs:
                        L = CH[c][1]
                        hold(sem("t_masked"), l * 16 + [0, 3, 6, 8, 10, 12, 14][k] + c + 1)
                        for s in range(H):
                            xt = XT[:, c, s, :] if c < 2 else XTs[:, s, :]
                            tm = Tm[:, c, s, :] if c < 2 else Tms[:, s, :]
                            mm(LB(1, c, L)[:, s, :], xt, tm)
                            g = mm(LB(2, c, L)[:, s, :], tm, xt)
                        g.then_inc(sem("level_y"), 1)
                hold(sem("x_level"), l * 16 + 16)

            with pe.Fori(0, DEPTH) as l:
                norm_pre(l, 0)
                ffn(l, 0)
                norm_post(l, 0)
                norm_pre(l, 1)
                mixers(l)
                pe.wait_ge(sem("last_read"), l + 1)
                for i in range(4):
                    s = slot_ready(l, POS_OUT + i)
                    w = ring[:, s, 0:KT * 256].rearrange("p (k n) -> p k n", k=KT)
                    for t in range(2):
                        m = 2 * i + t
                        pe.wait_ge(sem("y_done"), l * 24 + 8 + m + 1)
                        for k in range(KT):
                            g = mm(ps[:, m % 4, 0:T], w[:, k, t * P:(t + 1) * P], hdn[:, k, 0:T],
                                   k == 0, k == KT - 1)
                        g.then_inc(sem("post_product_done"), 1)
                norm_post(l, 1)
                norm_pre(l, 2)
                ffn(l, 1)
                norm_post(l, 2)
            pe.wait_ge(sem("x_done"), 24 * DEPTH + KT)
            for c, (o, L) in enumerate(CH):
                if c:
                    pe.wait_ge(sem("x_out_read"), c)
                for k in range(KT):
                    g = tr(ps[0:L, k // 4, (k % 4) * P:(k % 4 + 1) * P], x[:, k, o:o + L])
                g.then_inc(sem("x_back"), 1)

        @block.scalar
        def _(act):
            A = act.activation
            n_chain = [0]

            def link(l, ins):
                n_chain[0] += 1
                ins.then_inc(sem("act_chain"), 1)
                act.wait_ge(sem("act_chain"), l * CHAIN["act"] + n_chain[0])

            act.sem_inc(sem("y_done"), Y_CREDIT)
            act.dma_start(cst[:, :], I["const"]).then_inc(sem("const_loaded"), 16)

            def rsqrt(l, out, src, scale, eps=True):
                link(l, A(out, src, ACT.Ln, bias=epsc[0:out.shape[0], :], scale=scale))
                return A(out, out, ACT.Exp, scale=-0.5)

            def norm(l, i):
                act.wait_ge(sem("norm_sum"), l * 6 + i + 1)
                act.wait_ge(sem("rrow_used"), l * 6 + i + FREE)
                link(l, A(lnr[:, :], ps[:, 4, 0:T], ACT.Ln, bias=epsc[:, :], scale=1.0 / D))
                A(rrow[:, :], lnr[:, :], ACT.Exp, scale=-0.5).then_inc(sem("rrow_ready"), 1)

            def squares(l, pre, post_done):
                for k in range(KT):
                    act.wait_ge(sem("x_done"), post_done + k + 1)
                    A(y[:, k, :], x[:, k, :], ACT.Square).then_inc(sem("x_squared"), 1)

            def products(l, post):
                for m in range(KT):
                    act.wait_ge(sem("post_product_done"), l * 24 + post * 8 + m + 1)
                    if m >= 2:
                        act.wait_ge(sem("squares_added"), l * 24 + post * 8 + m - 1)
                    A(sq[:, m % 2, :], ps[:, m % 4, 0:T], ACT.Square)
                    A(y[:, m, :], ps[:, m % 4, 0:T], ACT.Copy).then_inc(sem("y_done"), 1)

            def ffn(l, f):
                with act.Fori(0, FT // 2) as j:
                    for t in range(2):
                        i = l * 2 * FT + f * FT + j * 2 + t
                        act.wait_ge(sem("gate_done"), i + 1)
                        act.wait_ge(sem("h_done"), i - 1 + H_CREDIT)
                        A(sg[:, t, :], ps[:, 2 * t, 0:T], ACT.Silu).then_inc(sem("silu_done"), 1)
                products(l, 2 * f)

            def mixers(l):
                l1 = l + 1
                silu_q = []

                def conv_silu(ct):
                    act.wait_ge(sem("conv_done"), l * NC + ct + 1)
                    A(big[:, CONV_T[ct], 0:SEQ], big[:, CONV_T[ct], 0:SEQ], ACT.Silu)\
                        .then_inc(sem("conv_silu"), 1)

                for i in range(NPT):
                    act.wait_ge(sem("proj_done"), l * NPT + i + 1)
                    src = ps[:, i % 4, 0:T]
                    if i in CONV_T:
                        ct = CONV_T.index(i)
                        A(xP[:, ct, 3:], src[:, 0:SEQ], ACT.Copy)
                        g = A(xS[:, ct, :, 3:], src[:, SEQ:].rearrange("p (b t) -> p b t", t=LS), ACT.Copy)
                    elif i in SILU_T:
                        g = A(big[:, i, :], src, ACT.Silu)
                    elif i >= 28:
                        g = A(big[:, i, :], src, ACT.Tanh, scale=0.5)
                    elif i in (16, 17, 24, 25):
                        g = A(big[:, i, :], src, ACT.Copy, scale=HD ** -0.5)
                    else:
                        g = A(big[:, i, :], src, ACT.Copy)
                    g.then_inc(sem("proj_read"), 1)
                    if i >= 6 and i - 6 < NC:
                        conv_silu(i - 6)
                act.wait_ge(sem("conv_s_done"), l1)
                for ct in range(NC):
                    g = A(big[:, CONV_T[ct], SEQ:T],
                          ctmp[:, ct, :, :].rearrange("p b t -> p (b t)"), ACT.Silu)
                g.then_inc(sem("conv_s_silu"), 1)
                act.wait_ge(sem("u_ready"), l1)
                link(l, A(AB[:, :, :], U[:, :, 0:12], ACT.Abs))
                link(l, A(AB[:, :, :], AB[:, :, :], ACT.Exp, scale=-1.0))
                A(AB[:, :, :], AB[:, :, :], ACT.Ln, bias=1.0)
                A(alog[:, 0:8], alog[:, 0:8], ACT.Exp)
                A(beta[:, :, :], U[:, :, 12:16], ACT.Exp).then_inc(sem("gate_exps"), 1)
                act.wait_ge(sem("act_chain"), l * CHAIN["act"] + n_chain[0])
                act.wait_ge(sem("conv_s_silu"), l1)
                link(l, A(DTf[:, 0:4 * T], big[:, 0:4, :].rearrange("p k t -> p (k t)"), ACT.Square))
                A(sml[0:1, 0, 0:1], epsc[0:1, :], ACT.Copy).then_inc(sem("qk_squared"), 1)
                act.wait_ge(sem("w_arg"), l1)
                A(wexp[:, :, 0:8], wexp[:, :, 0:8], ACT.Exp).then_inc(sem("wexp_ready"), 1)
                act.wait_ge(sem("erow_done"), l1)
                for n in range(2):
                    A(er[:, 2 * n:2 * n + 2, :], B(n, 2, 160), ACT.Exp)
                A(decP[:, 0:4], ps[:, 2, 0:4], ACT.Exp)
                A(decS[:, 0:48], ps[:, 3, 0:48], ACT.Exp).then_inc(sem("er_read"), 1)
                act.wait_ge(sem("m_rows_arg"), l1)
                A(eI[:, :], eI[:, :], ACT.Exp)
                A(eD[:, :], eD[:, :], ACT.Exp).then_inc(sem("m_rows_ready"), 1)
                act.wait_ge(sem("ml_arg"), l1)
                for rows, cc in ((P, slice(0, 2)), (NS, slice(2, 3))):
                    A(emt[0:rows, cc, :], mt[0:rows, cc, :], ACT.Exp, scale=-1.0)
                    g = A(wexp[0:rows, cc, 8:12], wexp[0:rows, cc, 8:12], ACT.Exp)
                g.then_inc(sem("ml_exps"), 1)
                act.wait_ge(sem("qk_norms_done"), l1)
                for n in range(4):
                    g = A(DTf[:, n * T:(n + 1) * T], ps[:, n, 0:T], ACT.Ln, bias=epsc[:, :])
                link(l, g)
                A(DTf[:, 0:4 * T], DTf[:, 0:4 * T], ACT.Exp, scale=-0.5).then_inc(sem("qk_norms_read"), 1)
                for mi, m in enumerate(MIX):
                    if m != "ret":
                        for c, (o, L) in enumerate(CH):
                            act.wait_ge(sem("decay_arg"), l * 9 + 3 * [0, 1, 0, 2][mi] + c + 1)
                            A(DT[0:L, c, :, 0:L], DT[0:L, c, :, 0:L], ACT.Exp).then_inc(sem("decay_ready"), 1)
                    if m == "ssd":
                        act.wait_ge(sem("ssd_gated"), l1)
                        for n in range(2):
                            g = A(tiny[:, n, :], big[:, 8 + n, :], ACT.Square)
                        g.then_inc(sem("ssd_squared"), 1)
                        act.wait_ge(sem("ssd_sum"), l1)
                        link(l, A(lnr[:, :], ps[:, 0, 0:T], ACT.Ln, bias=epsc[:, :], scale=1.0 / GW))
                        A(lnr[:, :], lnr[:, :], ACT.Exp, scale=-0.5).then_inc(sem("ssd_rrow"), 1)
                        continue
                    for c, (o, L) in enumerate(CH):
                        i3 = l * 9 + 3 * [0, 0, 1, 2][mi] + c + 1
                        if m == "ml":
                            act.wait_ge(sem("hout_ready"), l * 3 + c + 1)
                            src = hout[0:L, :]
                        else:
                            act.wait_ge(sem("out_done"), l * 12 + 3 * mi + c + 1)
                            src = ps[0:L, 2, 0:GW]
                        A(osq[0:L, :], src, ACT.Square).then_inc(sem("out_sq"), 1)
                        act.wait_ge(sem("out_ss"), i3)
                        link(l, A(sml[0:L, 1, :], sml[0:L, 0, :], ACT.Ln, bias=epsc[0:L, :], scale=1.0 / HD))
                        A(sml[0:L, 2, :], sml[0:L, 1, :], ACT.Exp, scale=-0.5).then_inc(sem("out_rn"), 1)

            with act.Fori(0, DEPTH) as l:
                n_chain[0] = 0
                squares(l, 0, l * 24)
                norm(l, 0)
                ffn(l, 0)
                norm(l, 1)
                squares(l, 1, l * 24 + 8)
                norm(l, 2)
                mixers(l)
                products(l, 1)
                norm(l, 3)
                squares(l, 2, l * 24 + 16)
                norm(l, 4)
                ffn(l, 1)
                norm(l, 5)
            print("act chain", n_chain[0])
            assert n_chain[0] == CHAIN["act"] or not STRICT

        @block.vector
        def _(dve):
            TT, TS, STT, CP = dve.tensor_tensor, dve.tensor_scalar, dve.scalar_tensor_tensor, dve.tensor_copy
            n_chain = [0]

            def link(l, ins):
                n_chain[0] += 1
                ins.then_inc(sem("dve_chain"), 1)
                dve.wait_ge(sem("dve_chain"), l * CHAIN["dve"] + n_chain[0])

            dve.sem_inc(sem("h_done"), H_CREDIT)
            dve.sem_inc(sem("rrow_used"), FREE)
            dve.sem_inc(sem("mixed_ready"), FREE)
            dve.memset(epsc[:, :], EPS)
            dve.memset(gb2[:, :, 12:16], 0.0)
            dve.memset(hdn[:, :, T:], 0.0)
            dve.memset(V[:, :, :, HD:], 1.0)
            dve.memset(Sbd[:, :, :, :], 0.0)
            dve.memset(qbd[:, :, :, :], 0.0)
            dve.memset(cbias[:, 0:6], 0.0)
            dve.memset(al2[:, :, 8:12], -1.0).then_inc(sem("dve_set"), 1)
            dve.wait_ge(sem("gains_turned"), 1)
            CP(gn[:, :, :, :].rearrange("p l i k -> p (l i k)"), B(0, 96)).then_inc(sem("params_placed"), 1)
            dve.wait_ge(sem("params_turned"), 1)
            CP(p2[:, :, :].rearrange("p l n -> p (l n)"), B(1, 104)).then_inc(sem("params_placed"), 1)
            for k in range(KT):
                dve.wait_ge(sem("x_turned"), k + 1)
                CP(x[:, k, :], ps[:, k, 0:T]).then_inc(sem("x_done"), 1)
            dve.wait_ge(sem("x_done"), KT)
            dve.wait_ge(sem("params_placed"), 2)
            dve.wait_ge(sem("dve_set"), 1)

            def pre(l, i):
                dve.wait_ge(sem("rrow_ready"), l * 6 + i + 1)
                for k in range(KT):
                    g = STT(hdn[:, k, 0:T], x[:, k, :], gcol[:, i, k:k + 1], rrow[:, :], ALU.mult, ALU.mult)
                    g.then_inc(sem("hdn_ready"), 1)
                TS(ssum[:, 0:1], rrow[:, 0:1], 1.0, None, ALU.mult).then_inc(sem("rrow_used"), 1)

            def post(l, p, half):
                i = 2 * p + 1
                g_ = ghalf if half else gcol
                for m in range(KT):
                    dve.wait_ge(sem("y_done"), l * 24 + 8 * p + m + 1 + Y_CREDIT)
                    if m == 0:
                        g = CP(ssum[:, :], sq[:, 0, :])
                    else:
                        dve.wait_ge(sem("squares_added"), l * 24 + 8 * p + m)
                        g = TT(ssum[:, :], ssum[:, :], sq[:, m % 2, :], ALU.add)
                    g.then_inc(sem("squares_added"), 1)
                dve.wait_ge(sem("rrow_ready"), l * 6 + i + 1)
                for k in range(KT):
                    link(l, STT(y[:, k, :], y[:, k, :], g_[:, i, k:k + 1], rrow[:, :], ALU.mult, ALU.mult))
                    TT(x[:, k, :], x[:, k, :], y[:, k, :], ALU.add).then_inc(sem("x_done"), 1)
                TS(ssum[:, 0:1], rrow[:, 0:1], 1.0, None, ALU.mult).then_inc(sem("rrow_used"), 1)

            def ffn(l, f):
                with dve.Fori(0, FT // 2) as j:
                    for t in range(2):
                        i = l * 2 * FT + f * FT + j * 2 + t
                        dve.wait_ge(sem("silu_done"), i + 1)
                        dve.wait_ge(sem("up_done"), i + 1)
                        TT(big[:, bass.ds(j * 2 + t, 1), :].rearrange("p o t -> p (o t)"), sg[:, t, :],
                           ps[:, 2 * t + 1, 0:T], ALU.mult).then_inc(sem("h_done"), 1)
                post(l, 2 * f, True)

            def mixers(l):
                l1 = l + 1
                dve.memset(xP[:, :, 0:3], 0.0)
                dve.wait_ge(sem("layers_stored"), l + FREE)
                link(l, dve.memset(kbd, 0.0))
                dve.wait_ge(sem("gates_done"), l1)
                link(l, TT(U[:, :, :], B(5, 3, 20), bc(gbias[:, :], 1, 3), ALU.add))
                TT(U[:, :, :], U[:, :, :], bc(sign, 1, 3), ALU.mult).then_inc(sem("u_ready"), 1)
                dve.wait_ge(sem("hist_turned"), l1)
                CP(xS[:, :, :, 0:3], B(6, NC, NB * 3).rearrange("p c (b j) -> p c b j", j=3))\
                    .then_inc(sem("hist_placed"), 1)
                for ct in range(NC):
                    i = CONV_T[ct]
                    dve.wait_ge(sem("proj_read"), l * NPT + i + 1)
                    out = big[:, i, 0:SEQ]
                    link(l, TS(out, xP[:, ct, 0:SEQ], taps[:, ct, 0:1], cbias[:, ct:ct + 1], ALU.mult, ALU.add))
                    for j in (1, 2, 3):
                        g = STT(out, xP[:, ct, j:j + SEQ], taps[:, ct, j:j + 1], out, ALU.mult, ALU.add)
                        if j < 3:
                            link(l, g)
                        else:
                            g.then_inc(sem("conv_done"), 1)
                dve.wait_ge(sem("hist_placed"), l1)
                bcw = lambda j: taps[:, :, j:j + 1].unsqueeze(3).broadcast_to([P, NC, NB, LS])
                cs = C4[:, :, :, :]
                link(l, TT(ctmp[:, :, :, :], xS[:, :, :, 0:LS], bcw(0), ALU.mult))
                for j in (1, 2, 3):
                    link(l, TT(cs, xS[:, :, :, j:j + LS], bcw(j), ALU.mult))
                    link(l, TT(ctmp[:, :, :, :], ctmp[:, :, :, :], cs, ALU.add))
                TT(ctmp[:, :, :, :], ctmp[:, :, :, :],
                   cbias[:, :].unsqueeze(2).unsqueeze(3).broadcast_to([P, NC, NB, LS]), ALU.add)\
                    .then_inc(sem("conv_s_done"), 1)
                CP(last[:, :, 0:3], xP[:, :, SEQ:SEQ + 3])
                CP(last[:, :, 3:27].rearrange("p c (b j) -> p c b j", j=3), xS[:, :, :, LS:LS + 3])\
                    .then_inc(sem("last_ready"), 1)
                dve.wait_ge(sem("gate_exps"), l1)
                link(l, STT(SP[:, :, :], U[:, :, 0:12], 0.0, AB[:, :, :], ALU.max, ALU.add))
                TS(alog[:, 0:8], alog[:, 0:8], -1.0, None, ALU.mult)
                link(l, TS(beta[:, :, :], beta[:, :, :], 1.0, None, ALU.add))
                link(l, dve.reciprocal(beta[:, :, :], beta[:, :, :]))
                TT(G[:, :, :], SP[:, :, :], bc(alog[:, :], 1, 3), ALU.mult).then_inc(sem("decays_ready"), 1)
                dve.wait_ge(sem("decays_ready"), l1)
                CP(Bb[:, :, :, :], bc(beta[:, :, :], 3, HD))
                CP(Gb[:, :, 0:4, :].rearrange("p c (a b) d -> p c a b d", a=2)[:, 0],
                   bc(slots1(G[:, 1, 0:4], "ssd"), 3, HD))
                CP(Gb[:, :, 0:4, :].rearrange("p c (a b) d -> p c a b d", a=2)[:, 1],
                   bc(slots1(G[:, 2, 0:4], "ssd"), 3, HD))
                CP(Gb[:, :, 4:8, :], bc(G[:, 1:3, 4:8], 3, HD))
                TT(Gx[:, 0:16].rearrange("p (a h) -> p a h", h=H), bc(G[0:NS, 2, 4:8], 1, 4),
                   bc(C("obp", NS), 2, H), ALU.mult)
                TT(Gx[:, 16:48].rearrange("p (a h) -> p a h", h=H), bc(G[0:NS, 2, 0:4], 1, NB),
                   bc(C("onehot", NS), 2, H), ALU.mult).then_inc(sem("decays_spread"), 1)
                dve.wait_ge(sem("cum_done"), l1)
                link(l, CP(cum[:, :, :], B(4, 3, 12)))
                TT(wexp[:, :, 0:8], B(7, 3, 12)[:, :, 0:8], cum[:, :, 0:8], ALU.subtract).then_inc(sem("w_arg"), 1)
                TT(aT[:, :, :], U[:, :, 16:20], cum[:, :, 8:12], ALU.subtract).then_inc(sem("a_ready"), 1)
                dve.wait_ge(sem("a_turned"), l1)
                link(l, CP(aH[:, :], ps[0:H, 5, 0:T]))
                link(l, TT(aH[:, SEQ::LS], aH[:, SEQ::LS], mmc[:, :], ALU.max))
                link(l, dve.tensor_tensor_scan(mH[:, :], C("reset", H), aH[:, :], 0.0, ALU.add, ALU.max))
                CP(mL[:, 0:SEQ].rearrange("p (c n) -> p c n", c=2), bc(mH[:, P - 1:SEQ:P], 2, P))
                CP(mL[:, SEQ:].rearrange("p (b t) -> p b t", t=LS), bc(mH[:, SEQ + LS - 1::LS], 2, LS))
                dve.memset(mPv[:, 0:P], 0.0)
                CP(mPv[:, P:SEQ], mH[:, P - 1:P].broadcast_to([H, P]))
                link(l, CP(mPv[:, SEQ:].rearrange("p (b t) -> p b t", t=LS), bc(mmc[:, :], 2, LS)))
                TT(eI[:, :], mPv[:, :], mH[:, :], ALU.subtract)
                TT(eD[:, :], mPv[:, :], mL[:, :], ALU.subtract).then_inc(sem("m_rows_arg"), 1)
                dve.wait_ge(sem("m_tok_done"), l1)
                mtk = lambda n: ps[:, 5, 300 + 12 * n:312 + 12 * n].rearrange("p (c h) -> p c h", h=H)
                for rows, cc in ((P, slice(0, 2)), (NS, slice(2, 3))):
                    TT(mt[0:rows, cc, :], mtk(0)[0:rows, cc, :], cum[0:rows, cc, 8:12], ALU.add)
                    g = TT(wexp[0:rows, cc, 8:12], aT[0:rows, cc, :], mtk(1)[0:rows, cc, :], ALU.subtract)
                g.then_inc(sem("ml_arg"), 1)
                CP(er[:, 4:6, :], B(6, 2, 160))
                CP(decP[:, 4:6], ps[:, 6, 320:322])
                link(l, CP(sml[0:NS, 3, :], mtk(2)[0:NS, 2, :]))
                TT(Gx[:, 48:64].rearrange("p (a h) -> p a h", h=H), bc(sml[0:NS, 3, :], 1, 4),
                   bc(C("first", NS), 2, H), ALU.mult).then_inc(sem("ml_decay_spread"), 1)
                dve.wait_ge(sem("ml_decS_done"), l1)
                CP(decS[:, 48:64], ps[:, 7, 64:80])
                dve.wait_ge(sem("qk_norms_read"), l1)
                STT(big[:, 0:2, :].rearrange("p k t -> p (k t)"), big[:, 0:2, :].rearrange("p k t -> p (k t)"),
                    HD ** -0.5, DTf[:, 0:2 * T], ALU.mult, ALU.mult)
                link(l, TT(big[:, 2:4, :].rearrange("p k t -> p (k t)"),
                           big[:, 2:4, :].rearrange("p k t -> p (k t)"), DTf[:, 2 * T:4 * T], ALU.mult))
                dve.wait_ge(sem("beta_rows_done"), l1)
                for b in range(2):
                    r = slice(b * HD, (b + 1) * HD)
                    g = TT(kbd[r, :, b, :], big[r, 2:4, :], ps[r, 4:6, 0:T], ALU.mult)
                g.then_inc(sem("kbd_ready"), 1)
                TT(ki[:, :, :], big[:, 2:4, P:T], er[:, 2:4, :], ALU.mult)
                dve.wait_ge(sem("rotated"), l1)
                rq = big[:, RET_T:RET_T + 4, :]
                tmp = DTf[:, 0:4 * T].rearrange("p (k t) -> p k t", k=4)
                TT(tmp, ps[:, 0:4, 0:T], bc(C("sin"), 1, 4), ALU.mult)
                link(l, TT(rq, rq, bc(C("cos"), 1, 4), ALU.mult))
                link(l, TT(rq, rq, tmp, ALU.add))
                link(l, TS(big[:, 28:30, :].rearrange("p k t -> p (k t)"),
                           big[:, 28:30, :].rearrange("p k t -> p (k t)"), 0.5, 0.5, ALU.mult, ALU.add))
                for mi, m in enumerate(MIX):
                    mixer(l, l1, mi, m)
                dve.wait_ge(sem("last_turned"), l1)
                dve.wait_ge(sem("layers_stored"), l + FREE)
                for n in range(3):
                    w = min(4, NC - 4 * n)
                    g = CP(lastT[:, 4 * n:4 * n + w, :].rearrange("p c n -> p (c n)"), ps[0:27, 4 + n, 0:w * P])
                g.then_inc(sem("last_read"), 1)

            def mixer(l, l1, mi, m):
                w = HW[m]
                Sx = SX[m]
                i12 = l * 12 + 3 * mi
                q = QT[m]
                for b in range(2):
                    r = slice(b * HD, (b + 1) * HD)
                    if m == "ssd":
                        CP(qbd[r, 0, b, :], big[r, q, :])
                    else:
                        CP(qbd[r, :, b, :], big[r, q:q + 2, :])
                if m == "ssd":
                    g = TT(qi[:, :, :], bc(big[:, q, P:T], 1, 2), er[:, 0:2, :], ALU.mult)
                else:
                    e = retI if m == "ret" else er[:, 2:4, :] if m == "gdn" else er[:, 4:6, :]
                    g = TT(qi[:, :, :], big[:, q:q + 2, P:T], e, ALU.mult)
                g.then_inc(sem("qk_ready"), 1)
                for c, (o, L) in enumerate(CH):
                    dve.wait_ge(sem("kv_turned"), i12 + c + 1)
                    nk = P if m == "ssd" else GW
                    CP(K[0:L, c, 0:nk], ps[0:L, 4, 0:nk])
                    vsrc = slots(B(4, H, HD, rows=L, off=GW), m)
                    vdst = V[0:L, c, :, 0:HD].rearrange("p (a b) d -> p a b d", a=2)
                    if m == "ssd":
                        TT(Dx[0:L, c].rearrange("p (a b) d -> p a b d", a=2), vsrc,
                           bc(slots1(sD[0:L, :], m), 3, HD), ALU.mult)
                        g = TT(vdst, vsrc, bc(slots1(SP[0:L, c, 0:4], m), 3, HD), ALU.mult)
                    else:
                        g = CP(vdst, vsrc)
                    g.then_inc(sem("kv_read"), 1)
                if m != "ret":
                    neg = (C("neg"), C("neg"), C("neg_s", NS))
                    for c, (o, L) in enumerate(CH):
                        dve.wait_ge(sem("decay_rows"), l * 9 + 3 * [0, 1, 0, 2][mi] + c + 1)
                        for s in range(H):
                            h = head(m, s // 2, s % 2)
                            if m == "ml":
                                col, op = aT[0:L, c, s:s + 1], ALU.add
                            else:
                                col, op = cum[0:L, c, DC[m] + h:DC[m] + h + 1], ALU.subtract
                            g = STT(DT[0:L, c, s, 0:L], ps[0:L, 1, s * L:(s + 1) * L], col, neg[c], op, ALU.add)
                        g.then_inc(sem("decay_arg"), 1)
                dve.wait_ge(sem("dup_done"), l * 4 + mi + 1)
                spread = lambda off: bc(B(3, H, NS, off=off), 2, 4)
                g = TT(QX[:, :, :, :], spread(0), bc(bmask, 1, H), ALU.mult)
                if m == "gdn":
                    g = TT(KQX[:, :, :, :], spread(P), bc(bmask, 1, H), ALU.mult)
                g.then_inc(sem("qx_ready"), 1)
                if m == "ssd":
                    for bp in range(4):
                        dve.wait_ge(sem("snat_turned"), l * 4 + bp + 1)
                        CP(Sx[:, bp, :, 0:HD], B(5, H, HD)).then_inc(sem("snat_read"), 1)
                if m == "gdn":
                    gdn_solve(l, l1)
                for c, (o, L) in enumerate(CH):
                    dve.wait_ge(sem("scores_done"), i12 + c + 1)
                    if m == "ret":
                        d = retD if c < 2 else retDs[0:NS]
                    else:
                        dve.wait_ge(sem("decay_ready"), l * 9 + 3 * [0, 1, 0, 2][mi] + c + 1)
                        d = DT[0:L, c, :, 0:L]
                    if m == "ssd":
                        g = TT(PT[0:L, c, :, 0:L].rearrange("p (a b) n -> p a b n", a=2),
                               bc(B(0, 2, L, rows=L), 1, 2), d.rearrange("p (a b) n -> p a b n", a=2), ALU.mult)
                    else:
                        g = TT(PT[0:L, c, :, 0:L], B(0, H, L, rows=L), d, ALU.mult)
                    g.then_inc(sem("probs_ready"), 1)
                    if m == "gdn":
                        bt = bc(beta[0:L, c, :], 2, HD)
                        if c:
                            dve.wait_ge(sem("ks_done"), l * 2 + c)
                            link(l, TT(VW[0:L, c, :, 0:HD], V[0:L, c, :, 0:HD], B(5, H, HD, rows=L), ALU.subtract))
                            TT(VW[0:L, c, :, 0:HD], VW[0:L, c, :, 0:HD], bt, ALU.mult)\
                                .then_inc(sem("resid_ready"), 1)
                        else:
                            TT(VW[0:L, c, :, 0:HD], V[0:L, c, :, 0:HD], bt, ALU.mult)\
                                .then_inc(sem("resid_ready"), 1)
                        dve.wait_ge(sem("vnew_done"), l * 3 + c + 1)
                        g = CP(V[0:L, c, :, 0:HD], B(6, H, HD, rows=L))
                    else:
                        g = TS(sml[0:1, 0, 0:1], epsc[0:1, :], 1.0, None, ALU.mult)
                    g.then_inc(sem("values_ready"), 1)
                    dve.wait_ge(sem("values_ready"), i12 + c + 1)
                    if m == "ret":
                        wt = bc(tail[0:L, c, :], 2, w)
                    elif m == "ssd":
                        wt = bc(slots1(wexp[0:L, c, 0:4], m), 3, w)
                    else:
                        wt = bc(wexp[0:L, c, DC[m]:DC[m] + 4], 2, w)
                    dst, src = VW[0:L, c, :, 0:w], V[0:L, c, :, 0:w]
                    if m == "ssd":
                        dst, src = (v.rearrange("p (a b) n -> p a b n", a=2) for v in (dst, src))
                    TT(dst, src, wt, ALU.mult).then_inc(sem("vw_ready"), 1)
                    if c < 2:
                        dve.wait_ge(sem("state_add"), l * 8 + 2 * mi + c + 1)
                        sp_ = B(7, 2, w)
                        if c == 0:
                            if mi:
                                dve.wait_ge(sem("prompt_stored"), l * PSTORES + PS_BEFORE[m])
                            for b in range(2):
                                r = slice(b * HD, (b + 1) * HD)
                                CP(Sbd[r, :, b, 0:w], sp_[r])
                            g = CP(S1[:, :, 0:w], sp_)
                        else:
                            dec = C("ret_dec") if m == "ret" else decP[:, {"ssd": 0, "gdn": 2, "ml": 4}[m]:][:, 0:2]
                            for a in range(2):
                                g = STT(S1[:, a, 0:w], S1[:, a, 0:w], dec[:, a:a + 1], sp_[:, a, :],
                                        ALU.mult, ALU.add)
                        g.then_inc(sem("state_read"), 1)
                        dve.wait_ge(sem("state_read"), l * 8 + 2 * mi + c + 1)
                    finish(l, l1, mi, m, c, L)
                    if c == 2:
                        sample_states(l, l1, mi, m)
                gt, ot, nb = GATE[m], OUT_T[m], NORM[m]
                dve.wait_ge(sem("on_turned"), i12 + 3)
                if m == "ssd":
                    for n in range(2):
                        g = TT(big[:, 8 + n, :], ps[:, OUTB[m][n], 0:T], big[:, gt + n, :], ALU.mult)
                    g.then_inc(sem("ssd_gated"), 1)
                    dve.wait_ge(sem("ssd_state_turned"), l1)
                    CP(fin[:, :, :], B(7, 2, P, rows=HD)).then_inc(sem("ssd_state_read"), 1)
                    dve.wait_ge(sem("ssd_rrow"), l1)
                    for n in range(2):
                        g = STT(hdn[:, ot + n, 0:T], big[:, 8 + n, :], pcol[:, nb + n:nb + n + 1], lnr[:, :],
                                ALU.mult, ALU.mult)
                else:
                    for n in range(2):
                        g = STT(hdn[:, ot + n, 0:T], ps[:, OUTB[m][n], 0:T], pcol[:, nb + n:nb + n + 1],
                                big[:, gt + n, :], ALU.mult, ALU.mult)
                g.then_inc(sem("mixed_ready"), 1)

            def finish(l, l1, mi, m, c, L):
                i12 = l * 12 + 3 * mi
                w = HW[m]
                o4 = B(2, H, w, rows=L)
                on4 = on[0:L, c, :].rearrange("p (h d) -> p h d", h=H)
                dve.wait_ge(sem("out_done"), i12 + c + 1)
                if m == "ssd":
                    TT(slots(on4, m), o4.rearrange("p (a b) d -> p a b d", a=2),
                       Dx[0:L, c].rearrange("p (a b) d -> p a b d", a=2), ALU.add).then_inc(sem("on_ready"), 1)
                    return
                i3 = l * 9 + 3 * [0, 0, 1, 2][mi] + c
                if m == "ml":
                    den = o4[:, :, HD:HE].rearrange("p h o -> p (h o)")
                    link(l, CP(sml[0:L, 3, :], den))
                    link(l, STT(sml[0:L, 3, :], sml[0:L, 3, :], -1.0, sml[0:L, 3, :], ALU.mult, ALU.max))
                    link(l, TT(sml[0:L, 3, :], sml[0:L, 3, :], emt[0:L, c, :], ALU.max))
                    link(l, dve.reciprocal(sml[0:L, 3, :], sml[0:L, 3, :]))
                    TT(hout[0:L, :].rearrange("p (h d) -> p h d", h=H), o4[:, :, 0:HD],
                       bc(sml[0:L, 3, :], 2, HD), ALU.mult).then_inc(sem("hout_ready"), 1)
                dve.wait_ge(sem("out_sq"), i3 + 1)
                dve.tensor_reduce(sml[0:L, 0, :], osq[0:L, :].rearrange("p (h d) -> p h d", h=H), AX, ALU.add)\
                    .then_inc(sem("out_ss"), 1)
                dve.wait_ge(sem("out_rn"), i3 + 1)
                src = hout[0:L, :].rearrange("p (h d) -> p h d", h=H) if m == "ml" else o4
                TT(on4, src, bc(sml[0:L, 2, :], 2, HD), ALU.mult).then_inc(sem("on_ready"), 1)

            def sample_states(l, l1, mi, m):
                w = HW[m]
                if m == "ssd":
                    d = decS[0:HD, 16:48].rearrange("p (b h) -> p h b", h=H)
                    v = Snat[:, :, :, :]
                    link(l, TT(v, v, bc(d, 3, HD), ALU.mult))
                    for s in range(H):
                        dve.wait_ge(sem("sadd_done"), l * 16 + 4 * mi + s + 1 + FREE)
                        h = head(m, s // 2, s % 2)
                        TT(Snat[:, h], Snat[:, h], B(3, NB, HD, rows=HD), ALU.add).then_inc(sem("sadd_read"), 1)
                    return
                Sx = SX[m]
                if m == "ret":
                    d = bc(bc(C("ret_decs"), 1, 4), 3, w)
                else:
                    at = 0 if m == "gdn" else 48
                    d = bc(decS[:, at:at + 16].rearrange("p (a h) -> p a h", h=H), 3, w)
                link(l, TT(Sx[:, :, :, 0:w], Sx[:, :, :, 0:w], d, ALU.mult))
                for bp in range(4):
                    dve.wait_ge(sem("sadd_done"), l * 16 + 4 * mi + bp + 1 + FREE)
                    TT(Sx[:, bp, :, 0:w], Sx[:, bp, :, 0:w], B(3, H, w), ALU.add).then_inc(sem("sadd_read"), 1)

            def gdn_solve(l, l1):
                for c, (o, L) in enumerate(CH):
                    dve.wait_ge(sem("gram_done"), l * 3 + c + 1)
                    dve.wait_ge(sem("decay_ready"), l * 9 + c + 1)
                    at = AT[:, c] if c < 2 else ATs[:, :, :]
                    TT(at, B(0, H, L, rows=L), DT[0:L, c, :, 0:L], ALU.mult)
                    idb = bc(ident[0:L, 0:L], 1, H)
                    CP(X[:, 4 * c:4 * c + 4, :] if c < 2 else Xs[:, :, :], idb)
                    CP(XT[:, c] if c < 2 else XTs[:, :, :], idb).then_inc(sem("at_ready"), 1)
                for k in range(7):
                    cs = (0, 1, 2) if k < 2 else (0, 1)
                    i0 = l * 16 + [0, 3, 6, 8, 10, 12, 14][k]
                    for c in cs:
                        L = CH[c][1]
                        dve.wait_ge(sem("level_t"), i0 + c + 1)
                        tm = Tm[:, c] if c < 2 else Tms[:, :, :]
                        TT(tm, LB(0, c, L), bc(level[0:L, k, 0:L], 1, H), ALU.mult).then_inc(sem("t_masked"), 1)
                    for c in cs:
                        L = CH[c][1]
                        dve.wait_ge(sem("level_y"), i0 + c + 1)
                        xx = X[:, 4 * c:4 * c + 4, :] if c < 2 else Xs[:, :, :]
                        xt = XT[:, c] if c < 2 else XTs[:, :, :]
                        TT(xx, xx, LB(1, c, L), ALU.subtract)
                        TT(xt, xt, LB(2, c, L), ALU.subtract).then_inc(sem("x_level"), 1)

            with dve.Fori(0, DEPTH) as l:
                n_chain[0] = 0
                l1 = l + 1
                CP(gcol[:, :, :], gn[:, bass.ds(l, 1), :, :].rearrange("p o i k -> p (o i) k"))
                link(l, CP(pcol[:, :], p2[:, bass.ds(l, 1), :].rearrange("p o n -> p (o n)")))
                TS(ghalf[:, :, :], gcol[:, :, :], 0.5, None, ALU.mult)
                CP(taps[:, 0:6, :], pcol[:, 28:52].rearrange("p (j t) -> p t j", j=4))
                CP(taps[:, 6:10, :], pcol[:, 12:28].rearrange("p (j t) -> p t j", j=4))
                CP(cbias[:, 6:10], pcol[:, 8:12])
                dve.wait_ge(sem("gate_params_loaded"), 16 * 18)
                CP(gbias[:, :], gb2[:, bass.ds(l, 1), :].rearrange("p o n -> p (o n)"))
                CP(alog[:, :], al2[:, bass.ds(l, 1), :].rearrange("p o n -> p (o n)"))
                CP(sD[:, :], sd2[:, bass.ds(l, 1), :].rearrange("p o n -> p (o n)"))
                CP(mmc[:, :], mm[:, bass.ds(l, 1), :].rearrange("p o n -> p (o n)"))
                CP(wg[:, :, :], wg2[:, bass.ds(l, 1), :, :].rearrange("p o k n -> p (o k) n"))\
                    .then_inc(sem("layer_params"), 1)
                dve.wait_ge(sem("layer_params"), l1)
                pre(l, 0)
                ffn(l, 0)
                pre(l, 2)
                mixers(l)
                post(l, 1, False)
                pre(l, 4)
                ffn(l, 1)
            print("dve chain", n_chain[0])
            assert n_chain[0] == CHAIN["dve"] or not STRICT
            for c, (o, L) in enumerate(CH):
                dve.wait_ge(sem("x_back"), c + 1)
                for n in range(2):
                    g = CP(xtok_s[0:L, c, 512 * n:512 * n + 512], ps[0:L, n, :])
                g.then_inc(sem("x_out_read"), 1)

        @block.gpsimd
        def _(pool):
            dma = pool.dma_start

            def hold(s, v):
                pool.wait_ge(s, v)
                pool.sem_inc(sem("pool_held"), 1)

            pool.sem_inc(sem("layers_stored"), FREE)
            xp, xs = I["x_prompt"], I["x_sample"].rearrange("b t d -> (b t) d")
            dma(stage[0:96, :], I["norm_sandwich"].rearrange("l i (k p) -> (l i k) p", p=P))\
                .then_inc(sem("gain_rows_loaded"), 16)
            dma(xtok_s[:, 0:2, :], xp.rearrange("o (c p) d -> p (o c) d", p=P)).then_inc(sem("x_loaded"), 16)
            dma(xtok_s[0:NS, 2, :], xs).then_inc(sem("x_loaded"), 16)
            gl = sem("gate_params_loaded")
            win = I["w_in"].rearrange("l (k p) n -> p l k n", p=P)
            for n, c0 in enumerate((DT0, GAB0, MIF0 + H, GAB0 + H, MIF0)):
                for l in range(DEPTH):
                    dma(wg2[:, l, :, 4 * n:4 * n + 4], win[:, l, :, c0:c0 + 4]).then_inc(gl, 16)
            for n, v in enumerate(("ssm_dt_bias", "gdn_dt_bias", "mlstm_f_bias", None, "mlstm_i_bias")):
                if v:
                    dma(gb2[:, :, 4 * n:4 * n + 4], I[v].partition_broadcast(P)).then_inc(gl, 16)
            dma(al2[:, :, 0:4], I["ssm_A_log"].partition_broadcast(P)).then_inc(gl, 16)
            dma(al2[:, :, 4:8], I["gdn_A_log"].partition_broadcast(P)).then_inc(gl, 16)
            dma(sd2[:, :, :], I["ssm_D"].partition_broadcast(P)).then_inc(gl, 16)
            dma(mm[:, :, :], I["state_mlstm_m"].rearrange("l b h -> h l b")).then_inc(gl, 16)
            pool.wait_ge(sem("gains_turned"), 1)
            pr = sem("param_rows_loaded")
            for l in range(DEPTH):
                r = 52 * l
                for n, v in enumerate(("ret_norm", "ssm_norm", "gdn_norm", "mlstm_norm")):
                    dma(stage[r + 2 * n:r + 2 * n + 2, :], I[v][l].rearrange("(k p) -> k p", p=P)).then_inc(pr, 16)
                dma(stage[r + 8:r + 12, :], I["ssm_conv_b"][l].rearrange("(k p) -> k p", p=P)).then_inc(pr, 16)
                dma(stage[r + 12:r + 28, :], I["ssm_conv_w"][l].rearrange("j (k p) -> (j k) p", p=P)).then_inc(pr, 16)
                dma(stage[r + 28:r + 52, :], I["gdn_conv_w"][l].rearrange("j (k p) -> (j k) p", p=P)).then_inc(pr, 16)

            def at(name, l):
                return I[name][bass.ds(l, 1)]

            with pool.Fori(0, DEPTH) as l:
                l1 = l + 1
                dma(hist[:, 0:6, :], at("state_gdn_conv", l).rearrange("o b j (k p) -> (o b j) k p", p=P))\
                    .then_inc(sem("hist_loaded"), 16)
                dma(hist[:, 6:10, :], at("state_ssm_conv", l).rearrange("o b j (k p) -> (o b j) k p", p=P))\
                    .then_inc(sem("hist_loaded"), 16)
                def load_states(m):
                    name = {"gdn": "state_gdn", "ret": "state_ret", "ml": "state_mlstm_C", "ssd": "state_ssm"}[m]
                    for b in range(NB):
                        src = at(name, l)[:, b].rearrange("o h d e -> d (o h) e")
                        dst = Snat[:, :, b, :] if m == "ssd" else \
                            SX[m][(b % 2) * HD:(b % 2 + 1) * HD, b // 2, :, 0:HD]
                        dma(dst, src).then_inc(sem("states_loaded_" + m), 16)
                    if m == "ml":
                        for b in range(NB):
                            dma(SX["ml"][(b % 2) * HD:(b % 2 + 1) * HD, b // 2, :, HD:],
                                at("state_mlstm_n", l)[:, b].rearrange("o h d -> d (o h)").unsqueeze(2))\
                                .then_inc(sem("states_loaded_ml"), 16)

                load_states("gdn")
                for mi, m in enumerate(MIX):
                    if m == "gdn":
                        hold(sem("x_level"), l * 16 + 16)
                    hold(sem("kv_read"), l * 12 + 3 * mi + 3)
                    hold(sem("sadd_done"), l * 16 + 4 * mi + FREE)
                    for s in range(2 if m == "ssd" else H):
                        g = pool.tensor_tensor(KX[:, s], bc(K[0:NS, 2, s * HD:(s + 1) * HD], 1, NB),
                                               bc(C("onehot", NS), 2, HD), ALU.mult)
                    g.then_inc(sem("kx_ready"), 1)
                    pstored = sem("prompt_stored")
                    hold(sem("state_read"), l * 8 + 2 * mi + 2)
                    if m == "ssd":
                        hold(sem("ssd_state_read"), l1)
                        for a in range(2):
                            dma(O["p_ssm"][bass.ds(l, 1), 0].rearrange("o (g a) p n -> a p (o g) n", a=2)[a],
                                fin[:, a, :].rearrange("p (g n) -> p g n", g=2)).then_inc(pstored, 16)
                    else:
                        out = {"gdn": "p_gdn", "ret": "p_ret", "ml": "p_mC"}[m]
                        for a in range(2):
                            dma(O[out][bass.ds(l, 1), 0, 2 * a:2 * a + 2].rearrange("o h d e -> (o h d) e"),
                                S1[:, a, 0:HD]).then_inc(pstored, 16)
                            if m == "ml":
                                dma(O["p_mn"][bass.ds(l, 1), 0, 2 * a:2 * a + 2].rearrange("o h d -> (o h d)").unsqueeze(1),
                                    S1[:, a, HD:]).then_inc(pstored, 16)
                    stored = sem("sample_stored")
                    hold(sem("sadd_read"), l * 16 + 4 * mi + 4)
                    out = {"gdn": "s_gdn", "ret": "s_ret", "ml": "s_mC", "ssd": "s_ssm"}[m]
                    for b in range(NB):
                        dst = O[out][bass.ds(l, 1), b].rearrange("o h d e -> d (o h) e")
                        src = Snat[:, :, b, :] if m == "ssd" else \
                            SX[m][(b % 2) * HD:(b % 2 + 1) * HD, b // 2, :, 0:HD]
                        dma(dst, src).then_inc(stored, 16)
                        if m == "ml":
                            dma(O["s_mn"][bass.ds(l, 1), b].rearrange("o h d -> d (o h)").unsqueeze(2),
                                SX[m][(b % 2) * HD:(b % 2 + 1) * HD, b // 2, :, HD:]).then_inc(stored, 16)
                    if m == "gdn":
                        hold(sem("mixed_ready"), l * 4 + 1 + FREE)
                        load_states("ssd")
                        hold(stored, l * SSTORES + NB * 16)
                        load_states("ret")
                    if m == "ssd":
                        load_states("ml")
                dma(O["p_mm"][bass.ds(l, 1), 0], mt[P - 1:P, 1, :]).then_inc(stored, 16)
                for b in range(NB):
                    dma(O["s_mm"][bass.ds(l, 1), b], mt[LS * b + LS - 1:LS * b + LS, 2, :]).then_inc(stored, 16)
                hold(sem("last_read"), l1)
                ls = sem("last_stored")
                gc = lastT[:, 0:6, :].rearrange("p c n -> p (c n)")
                sc = lastT[:, 6:10, :].rearrange("p c n -> p (c n)")
                dma(O["p_gdn_conv"][bass.ds(l, 1), 0].rearrange("o j c -> (o j) c"), gc[0:3]).then_inc(ls, 16)
                dma(O["p_ssm_conv"][bass.ds(l, 1), 0].rearrange("o j c -> (o j) c"), sc[0:3]).then_inc(ls, 16)
                dma(O["s_gdn_conv"][bass.ds(l, 1)].rearrange("o b j c -> (o b j) c"), gc[3:27]).then_inc(ls, 16)
                dma(O["s_ssm_conv"][bass.ds(l, 1)].rearrange("o b j c -> (o b j) c"), sc[3:27]).then_inc(ls, 16)
                hold(sem("prompt_stored"), l1 * PSTORES)
                hold(stored, l1 * SSTORES)
                pool.wait_ge(ls, l1 * 64)
                pool.sem_inc(sem("layers_stored"), 1)
            yp = O["y_prompt"].rearrange("o (c p) d -> c p (o d)", p=P)
            ys = O["y_sample"].rearrange("b t d -> (b t) d")
            for c in range(3):
                pool.wait_ge(sem("x_out_read"), c + 1)
                dma(yp[c] if c < 2 else ys, xtok_s[0:CH[c][1], c, :]).then_inc(sem("y_stored"), 16)
            pool.wait_ge(sem("y_stored"), 48)


_INS = ["x_prompt", "x_sample", "state_ret", "state_ssm", "state_ssm_conv", "state_gdn", "state_gdn_conv",
        "state_mlstm_C", "state_mlstm_n", "state_mlstm_m", "w_in", "w_out", "norm_sandwich", "ffn_w_gate",
        "ffn_w_up", "ffn_w_down", "ret_norm", "ssm_conv_w", "ssm_conv_b", "ssm_dt_bias", "ssm_A_log", "ssm_D",
        "ssm_norm", "gdn_conv_w", "gdn_dt_bias", "gdn_A_log", "gdn_norm", "mlstm_i_bias", "mlstm_f_bias",
        "mlstm_norm"]
_OUTS = {"y_prompt": (1, SEQ, D), "y_sample": (NB, LS, D)}
for _p, _b in (("p", 1), ("s", NB)):
    _OUTS |= {f"{_p}_ret": (DEPTH, _b, H, HD, HD), f"{_p}_ssm": (DEPTH, _b, H, HD, HD),
              f"{_p}_ssm_conv": (DEPTH, _b, 3, SSM_CH), f"{_p}_gdn": (DEPTH, _b, H, HD, HD),
              f"{_p}_gdn_conv": (DEPTH, _b, 3, GDN_CH), f"{_p}_mC": (DEPTH, _b, H, HD, HD),
              f"{_p}_mn": (DEPTH, _b, H, HD), f"{_p}_mm": (DEPTH, _b, H)}


def kernel(**inputs):
    import concourse.bacc as bacc
    from concourse.bass_utils import run_bass_kernel_spmd

    nc = bacc.Bacc("TRN2", target_bir_lowering=False, num_devices=1)
    arrays, ins, outs = {}, {}, {}
    for name in _INS:
        a = np.ascontiguousarray(inputs[name])
        arrays["in_" + name] = a
        ins[name] = nc.dram_tensor("in_" + name, a.shape, mybir.dt.from_np(a.dtype), kind="ExternalInput").ap()
    table = np.ascontiguousarray(np.concatenate(list(CONST.values()), axis=1))
    arrays["in_const"] = table
    ins["const"] = nc.dram_tensor("in_const", table.shape, F32, kind="ExternalInput").ap()
    for name, shape in _OUTS.items():
        outs[name] = nc.dram_tensor("out_" + name, shape, F32, kind="ExternalOutput").ap()
    trunk_kernel(nc, ins, outs)
    r = run_bass_kernel_spmd(nc, [arrays], core_ids=[0])
    return tuple(r.results[0]["out_" + name] for name in _OUTS)
```

```python
from contextlib import ExitStack

import numpy as np

import concourse.bass as bass
from concourse import mybir

F32 = mybir.dt.float32
F32R = mybir.dt.float32r
ALU = mybir.AluOpType
ACT = mybir.ActivationFunctionType
AX = mybir.AxisListType.X
P = 128

D = 1024
KT = D // P
SEQ = 256
DEPTH = 2
NB, LS = 8, 4
PAST = 2048
NS = NB * LS
T = SEQ + NS
H, HD = 4, 64
GW = 256
FF = 2816
FT = FF // P
RET_IN = 4 * GW
SSM_CH = GW + 4 * HD
GDN_CH = 3 * GW
Z0 = RET_IN
XBC0 = Z0 + GW
DT0 = XBC0 + SSM_CH
GDN0 = DT0 + H
GG0 = GDN0 + GDN_CH
GAB0 = GG0 + GW
ML0 = GAB0 + 2 * H
MIF0 = ML0 + 4 * GW
IN_DIM = MIF0 + 2 * H
EPS = 1e-6
NEG = -1.0e30
HE = HD + 1

CH = [(0, 128), (128, 128), (256, 32)]
GDN_T, SSD_T, RET_T, ML_T = 0, 8, 14, 22
NPT = 30
BLOCKS = ([GDN0 + GW * i for i in range(4)] + [XBC0, XBC0 + GW, Z0] + [GW * i for i in range(4)]
          + [ML0 + GW * i for i in range(4)])
CONV_T = [0, 1, 2, 3, 4, 5, 8, 9, 10, 11]
NC = len(CONV_T)
SILU_T = (6, 7, 12, 13, 20, 21)
MIX = ("gdn", "ssd", "ret", "ml")
OUT_T = {"ret": 0, "ssd": 2, "gdn": 4, "ml": 6}

RING = 4
SLOT = KT * 256
DOWN = (8, 8, 6)
PAIRS = FT // 2
FFN_SLOTS = 2 * PAIRS + 4 * len(DOWN)
N_IN = len(BLOCKS)
POS_FFN = (0, FFN_SLOTS + N_IN + 4)
POS_IN = FFN_SLOTS
POS_OUT = POS_IN + N_IN
N_POS = 2 * FFN_SLOTS + N_IN + 4
POSITIONS = N_POS + 1
assert POSITIONS % RING == 0
PER_SLOT = POSITIONS // RING
H_CREDIT = 2
Y_CREDIT = 4
FREE = 1


def constants():
    i = np.arange(P)
    same = (i[:, None] // LS == i[None, :] // LS) & (i[:, None] < NS) & (i[None, :] < NS)
    lg = np.log(1.0 - np.exp2(-5.0 - np.arange(H)))
    c = {}
    c["ident"] = np.eye(P)
    c["ones"] = np.ones((P, P))
    c["bdones"] = (i[:, None] // HD == i[None, :] // HD)
    rot = np.zeros((P, P))
    for d in range(P):
        if d % HD < HD // 2:
            rot[d + HD // 2, d] = -1
        else:
            rot[d - HD // 2, d] = 1
    c["rot"] = rot
    le = i[:, None] <= i[None, :]
    c["tri"] = le
    c["tri_s"] = le & same
    c["blk_s"] = same
    c["neg"] = np.where(le, 0, NEG)
    c["neg_s"] = np.where(le & same, 0, NEG)[:, :NS]
    lv = np.zeros((P, 7, P))
    for k in range(7):
        s = 1 << k
        t, u = i[:, None], i[None, :]
        lv[:, k] = (t // (2 * s) == u // (2 * s)) & (t % (2 * s) >= s) & (u % (2 * s) < s)
    c["level"] = lv.reshape(P, -1)
    pos = np.concatenate([np.arange(SEQ), PAST + np.arange(NS) % LS]).astype(np.float32)
    inv = np.float32(10000.0) ** (-np.arange(HD // 2, dtype=np.float32) / np.float32(HD // 2))
    ang = (inv[i % (HD // 2)][:, None] * pos[None, :]).astype(np.float32).astype(np.float64)
    c["cos"], c["sin"] = np.cos(ang), np.sin(ang)
    dp = np.zeros((P, H, P))
    ds = np.zeros((P, H, NS))
    for h in range(H):
        dp[:, h] = np.where(le, np.exp(np.where(le, i[None, :] - i[:, None], 0) * lg[h]), 0)
        ds[:, h] = np.where(le & same, np.exp(np.where(le, i[None, :] - i[:, None], 0) * lg[h]), 0)[:, :NS]
    c["ret_d"], c["ret_ds"] = dp.reshape(P, -1), ds.reshape(P, -1)
    inter = np.zeros((P, 2, P + NS))
    for a in range(2):
        for b in range(2):
            inter[b * HD:(b + 1) * HD, a] = np.exp(
                np.concatenate([i + 1, np.arange(NS) % LS + 1]) * lg[2 * a + b])
    c["ret_inter"] = inter.reshape(P, -1)
    tail = np.zeros((P, 3, H))
    tail[:, 0] = tail[:, 1] = np.exp((P - 1 - i)[:, None] * lg)
    tail[:, 2] = np.where(i[:, None] < NS, np.exp((LS - 1 - i % LS)[:, None] * lg), 0)
    c["ret_tail"] = tail.reshape(P, -1)
    c["ret_dec"] = np.exp(P * lg)[2 * np.arange(2)[None, :] + i[:, None] // HD]
    c["ret_decs"] = np.broadcast_to(np.exp(LS * lg), (P, H))
    dup = np.zeros((P, 2, P))
    for b in range(2):
        dup[:, b] = (i[:, None] // HD == b) & (i[:, None] % HD == i[None, :] % HD)
    c["dup"] = dup.reshape(P, -1)
    tok = np.arange(NS)
    bm = (tok[None, None, :] // LS == 2 * np.arange(4)[None, :, None] + i[:, None, None] // HD)
    c["bmask"] = bm.reshape(P, -1)
    c["onehot"] = (i[:, None] // LS == np.arange(NB)[None, :])
    c["blsel"] = ((i[:, None] // LS) % 2 == i[None, :] // HD) & (i[:, None] < NS)
    c["obp"] = (i[:, None] // (2 * LS) == np.arange(4)[None, :])
    c["first"] = (i[:, None] // (2 * LS) == np.arange(4)[None, :]) & (i[:, None] % LS == 0)
    s2 = np.zeros((P, 2, P))
    for h in range(H):
        s2[h, h // 2, (h % 2) * HD:(h % 2 + 1) * HD] = 1
    c["nident"], c["sel2"] = -np.eye(P)[:, :H], s2.reshape(P, -1)
    reset = np.zeros((P, T))
    reset[:, SEQ::LS] = NEG
    c["reset"] = reset
    sign = np.ones((P, 5, H))
    sign[:, 2:4] = -1
    c["sign"] = sign.reshape(P, -1)
    return {k: np.ascontiguousarray(v, dtype=np.float32) for k, v in c.items()}


CONST = constants()
CONST_AT, _at = {}, 0
for _n, _v in CONST.items():
    CONST_AT[_n] = (_at, _v.shape[1])
    _at += _v.shape[1]
CONST_W = _at

CHAIN = {"dve": 104, "act": 20}
STRICT = True
PS_BEFORE = {"gdn": 0, "ssd": 32, "ret": 64, "ml": 96}
PSTORES = 96 + 64
SSTORES = 16 * (4 * NB + 1 + NB)


def trunk_kernel(nc, I, O):
    ctx = ExitStack()
    with ctx:
        named = {}

        def sb(name, shape):
            return ctx.enter_context(nc.sbuf_tensor(name, shape, F32))

        def sb2(name, shape):
            offset = (nc.sbuf_base + 31) // 32 * 32
            return sb(name, shape), nc.alloc_sbuf_tensor_at(name + "_r", shape, F32R, offset=offset)

        def sem(name):
            if name not in named:
                named[name] = ctx.enter_context(nc.semaphore(name))
            return named[name]

        cst = sb("cst", [P, CONST_W])
        x = sb("x", [P, KT, T])
        hdnf = sb("hdn", [P, KT * T + 3 * P - T])
        hdn = hdnf[:, 0:KT * T].rearrange("p (k t) -> p k t", k=KT)
        big, bigR = sb2("big", [P, NPT, T])
        yf, yfR = sb2("y", [P, KT * T + 3 * P - T])
        y, yR = (v[:, 0:KT * T].rearrange("p (k t) -> p k t", k=KT) for v in (yf, yfR))
        ring, ringR = sb2("ring", [P, RING, SLOT])
        rrow = sb("rrow", [P, T])
        lnr = sb("lnr", [P, T])
        ssum = sb("ssum", [P, T])
        sq = sb("sq", [P, 2, T])
        sg = sb("sg", [P, 2, T])
        gn = sb("gn", [P, DEPTH, 6, KT])
        p2 = sb("p2", [P, DEPTH, 52])
        gcol = sb("gcol", [P, 6, KT])
        ghalf = sb("ghalf", [P, 6, KT])
        pcol = sb("pcol", [P, 52])
        taps = sb("taps", [P, NC, 4])
        cbias = sb("cbias", [P, NC])
        wg2 = sb("wg2", [P, DEPTH, KT, 20])
        wg, wgR = sb2("wg", [P, KT, 20])
        wgh = sb("wgh", [P, KT, 20])
        gb2 = sb("gb2", [P, DEPTH, 20])
        al2 = sb("al2", [P, DEPTH, 12])
        sd2 = sb("sd2", [P, DEPTH, H])
        gbias = sb("gbias", [P, 20])
        alog = sb("alog", [P, 12])
        sD = sb("sD", [P, H])
        epsc = sb("epsc", [P, 1])
        stage = sb("stage", [104, P])
        lastT = sb("lastT", [27, NC, P])
        hist = lastT[0:NB * 3]
        arena, arenaR = sb2("arena", [P, NC * (3 + SEQ) + NC * NB * (3 + LS) + 3 * H * P + 3 * GW + 3 * H * HE + 2 * (P + NS)])
        at_ = [0]

        def carve(*shape):
            n = int(np.prod(shape))
            v = arena[:, at_[0]:at_[0] + n]
            at_[0] += n
            names = "abcd"[:len(shape)]
            return v.rearrange(f"p ({' '.join(names)}) -> p {' '.join(names)}", **dict(zip(names, shape)))

        low, lowR = (v[:, 0:FT * T].rearrange("p (k t) -> p k t", k=FT) for v in (arena, arenaR))
        xP = carve(NC, 3 + SEQ)
        xS = carve(NC, NB, 3 + LS)
        DT = carve(3, H, P)
        K = carve(3, GW)
        VW = carve(3, H, HE)
        ki = carve(2, P + NS)
        last = sb("last", [P, NC, 27])
        U = sb("U", [P, 3, 20])
        AB = sb("AB", [P, 3, 12])
        SP = sb("SP", [P, 3, 12])
        G = sb("G", [P, 3, 12])
        beta = sb("beta", [P, 3, H])
        cum = sb("cum", [P, 3, 12])
        wexp = sb("wexp", [P, 3, 12])
        onfin = sb("onfin", [P, 3 * GW + 2 * P])
        on = onfin[:, 0:3 * GW].rearrange("p (c n) -> p c n", c=3)
        fin = onfin[0:HD, 3 * GW:].rearrange("p (a n) -> p a n", a=2)
        Gb = onfin[:, :].rearrange("p (c s d) -> p c s d", c=2, s=8)
        er = sb("er", [P, 6, P + NS])
        decP = sb("decP", [P, 6])
        Gx = sb("Gx", [NS, 64])
        decS = sb("decS", [P, 64])
        aT = sb("aT", [P, 3, H])
        aH = sb("aH", [H, T])
        mH = sb("mH", [H, T])
        mL = sb("mL", [H, T])
        mPv = sb("mPv", [H, T])
        eI = aH
        eD = mPv
        mm = sb("mm", [H, DEPTH, NB])
        mmc = sb("mmc", [H, NB])
        mTok = sb("mTok", [P, 3, 3, H])
        mt = sb("mt", [P, 3, H])
        emt = sb("emt", [P, 3, H])
        qbd = sb("qbd", [P, 2, 2, T])
        qi = sb("qi", [P, 2, P + NS])
        V = sb("V", [P, 3, H, HE])
        ctmp = K[:, :, :].rearrange("p c n -> p (c n)")[:, 0:NC * NS].rearrange("p (c b t) -> p c b t", c=NC, b=NB)
        Bb = VW[:, :, :, :].rearrange("p c h e -> p (c h e)")[:, 0:3 * GW]\
            .rearrange("p (c h d) -> p c h d", c=3, h=H)
        xPf = xP[:, :, :].rearrange("p c n -> p (c n)")
        PT = xPf[:, 0:3 * H * P].rearrange("p (c h n) -> p c h n", c=3, h=H)
        DTf = DT[:, :, :, :].rearrange("p c h n -> p (c h n)")
        Dx = xPf[:, 3 * H * P:3 * H * P + 3 * GW].rearrange("p (c h n) -> p c h n", c=3, h=H)
        xtok_s = big[:, 0:11, :].rearrange("p k t -> p (k t)")[:, 0:3 * D].rearrange("p (c n) -> p c n", c=3)
        Sbd = sb("Sbd", [P, 2, 2, HE])
        S1 = sb("S1", [P, 2, HE])
        SX = [sb(f"Sx{n}", [P, 4, H, HE]) for n in range(2)]
        SX = {m: SX[n % 2] for n, m in enumerate(MIX)}
        whigh, whighR = sb2("whigh", [P, 2, SLOT])
        snat = whigh[:, 1, :]
        Snat = snat[0:HD, :].rearrange("p (h b n) -> p h b n", h=H, b=NB)
        kbd = snat[:, 0:4 * T].rearrange("p (a b t) -> p a b t", a=2, b=2)
        KQX = snat[:, 4 * T:4 * T + 16 * NS].rearrange("p (h b n) -> p h b n", h=H, b=4)
        atm = whigh[:, 0, :]
        AT = atm[:, 0:2 * H * P].rearrange("p (c h n) -> p c h n", c=2, h=H)
        Tm = atm[:, 2 * H * P:].rearrange("p (c h n) -> p c h n", c=2, h=H)
        KX = atm[0:NS, :].rearrange("p (h b n) -> p h b n", h=H, b=NB)
        QX = xS[:, :, :, :].rearrange("p c b j -> p (c b j)")[:, 0:H * 4 * NS]\
            .rearrange("p (h b n) -> p h b n", h=H, b=4)
        hout = rrow[:, 0:GW]
        osq = ssum[:, 0:GW]
        C4 = sg[:, :, :].rearrange("p a t -> p (a t)")[:, 0:NC * NS].rearrange("p (c b t) -> p c b t", c=NC, b=NB)
        sml = sb("sml", [P, 4, H])
        tiny = sq
        yflat = yf[:, :]
        X = yflat[:, 0:8 * P].rearrange("p (s n) -> p s n", n=P)
        XT = yflat[:, 8 * P:16 * P].rearrange("p (c h n) -> p c h n", c=2, h=H)
        Xs, XTs = (yflat[0:NS, (16 + n) * P:(17 + n) * P].rearrange("p (h n) -> p h n", h=H) for n in range(2))
        ATs = sb("ATs", [NS, H, NS])
        Tms = sb("Tms", [NS, H, NS])
        ps = ctx.enter_context(nc.psum_tensor("ps", [P, 8, 512], F32))

        def C(name, rows=P):
            at, w = CONST_AT[name]
            return cst[0:rows, at:at + w]

        ident, ones, bdones = C("ident"), C("ones"), C("bdones")
        level = C("level").rearrange("p (k n) -> p k n", k=7)
        retD = C("ret_d").rearrange("p (h n) -> p h n", h=H)
        retDs = C("ret_ds").rearrange("p (h n) -> p h n", h=H)
        retI = C("ret_inter").rearrange("p (a n) -> p a n", a=2)
        tail = C("ret_tail").rearrange("p (c h) -> p c h", c=3)
        dup = C("dup").rearrange("p (b n) -> p b n", b=2)
        bmask = C("bmask").rearrange("p (b n) -> p b n", b=4)
        sel2 = C("sel2").rearrange("p (a n) -> p a n", a=2)
        sign = C("sign")

        def B(bank, *shape, rows=P, off=0):
            n = int(np.prod(shape))
            v = ps[0:rows, bank, off:off + n]
            if len(shape) == 2:
                return v.rearrange("p (a b) -> p a b", a=shape[0])
            if len(shape) == 3:
                return v.rearrange("p (a b c) -> p a b c", a=shape[0], b=shape[1])
            return v

        def bc(ap, dim, n):
            a = ap.unsqueeze(dim)
            s = list(a.shape)
            s[dim] = n
            return a.broadcast_to(s)

        def slots(ap, m):
            if m == "ssd":
                return ap.rearrange("p (b a) n -> p a b n", a=2)
            return ap.rearrange("p (a b) n -> p a b n", a=2)

        def slots1(ap, m):
            if m == "ssd":
                return ap.rearrange("p (b a) -> p a b", a=2)
            return ap.rearrange("p (a b) -> p a b", a=2)

        def head(m, a, b):
            return 2 * b + a if m == "ssd" else 2 * a + b

        QT = {"gdn": 0, "ssd": 11, "ret": 14, "ml": 22}
        KTL = {"gdn": 2, "ssd": 10, "ret": 16, "ml": 24}
        VTL = {"gdn": 4, "ssd": 8, "ret": 18, "ml": 26}
        GATE = {"gdn": 6, "ssd": 12, "ret": 20, "ml": 28}
        DC = {"ssd": 0, "gdn": 4, "ml": 8}
        HW = {m: (HE if m == "ml" else HD) for m in MIX}
        NORM = {"ret": 0, "ssd": 2, "gdn": 4, "ml": 6}
        OUTB = {"gdn": (1, 4), "ssd": (5, 6), "ret": (5, 6), "ml": (5, 6)}

        def LB(kind, c, L):
            if c == 2:
                return B(6, H, NS, rows=NS, off=P * kind)
            return B(((0, 1), (2, 5), (7, 4))[kind][c], H, P)

        w_in_s = [sem(f"weights_loaded_{s}") for s in range(RING)]

        def gate_used(l, f, pair):
            return sem("gate_done"), l * 2 * FT + f * FT + pair * 2 + 2

        def up_used(l, f, pair):
            return sem("up_done"), l * 2 * FT + f * FT + pair * 2 + 2

        def used(l, pos):
            for f in range(2):
                n = pos - POS_FFN[f]
                if 0 <= n < 2 * PAIRS:
                    return (up_used if n % 2 else gate_used)(l, f, n // 2)
                if 2 * PAIRS <= n < FFN_SLOTS:
                    mp, part = divmod(n - 2 * PAIRS, 3)
                    if part < 2:
                        return sem("down_part_done"), l * 16 + f * 8 + 2 * mp + part + 1
                    return sem("post_product_done"), l * 24 + 16 * f + 2 * mp + 2
            if pos < POS_OUT:
                return sem("proj_done"), l * NPT + 2 * (pos - POS_IN) + 2
            return sem("post_product_done"), l * 24 + 8 + 2 * (pos - POS_OUT) + 2

        def ring_pos(l, pos):
            s, i = pos % RING, pos // RING
            per = PER_SLOT - (1 if s == (POSITIONS - 1) % RING else 0)
            return s, (l * per + i + 1) * 16

        ctx.enter_context(nc.allow_non_contiguous_dma(reason="a few small states with heads or features on partitions"))
        block = ctx.enter_context(nc.Block())

        @block.sync
        def _(sp):
            def hold(s, v):
                sp.wait_ge(s, v)
                sp.sem_inc(sem("sp_held"), 1)

            def load(l, pos, rows, src, free=None):
                if free is None:
                    free = used(l, pos - RING) if pos >= RING else (sem("y_done"), l * 24 + Y_CREDIT)
                hold(*free)
                s = pos % RING
                sp.dma_start(ring[:, s, 0:rows * 256].rearrange("p (k n) -> p k n", k=rows),
                             src).then_inc(w_in_s[s], 16)

            def ffn(l, f):
                wgd = I["ffn_w_gate"][bass.ds(l, 1), f].rearrange("o (k p) n -> p (o k) n", p=P)
                wud = I["ffn_w_up"][bass.ds(l, 1), f].rearrange("o (k p) n -> p (o k) n", p=P)
                wdd = I["ffn_w_down"][bass.ds(l, 1), f].rearrange("o (k p) n -> p (o k) n", p=P)
                pos = POS_FFN[f]
                for t in range(2):
                    for n, w in enumerate((wgd, wud)):
                        load(l, pos + 2 * t + n, KT, w[:, :, 256 * t:256 * t + 256])
                with sp.Fori(1, PAIRS // 2) as j:
                    for t in range(2):
                        for n, (w, before) in enumerate(((wgd, gate_used), (wud, up_used))):
                            load(l, pos + 2 * t + n, KT, w[:, :, bass.ds(j * 512 + 256 * t, 256)],
                                 before(l, f, j * 2 + (t - 2)))
                pos += 4 * (PAIRS // 2)
                for n, w in enumerate((wgd, wud)):
                    load(l, pos + n, KT, w[:, :, FF - 256:FF])
                pos += 2
                for mp in range(4):
                    for part, n in enumerate(DOWN):
                        load(l, pos + 3 * mp + part, n, wdd[:, 8 * part:8 * part + n, 256 * mp:256 * mp + 256])

            with sp.Fori(0, DEPTH) as l:
                ffn(l, 0)
                win = I["w_in"][bass.ds(l, 1)].rearrange("o (k p) n -> p (o k) n", p=P)
                for i, c0 in enumerate(BLOCKS):
                    load(l, POS_IN + i, KT, win[:, :, c0:c0 + 256])
                wo = I["w_out"][bass.ds(l, 1)].rearrange("o (k p) n -> p (o k) n", p=P)
                for i in range(4):
                    load(l, POS_OUT + i, KT, wo[:, :, 256 * i:256 * i + 256])
                ffn(l, 1)

        @block.tensor
        def _(pe):
            def mm(out, lhsT, rhs, start=True, stop=True, **k):
                return pe.matmul(out, lhsT, rhs, start=start, stop=stop, **k)

            def tr(out, in_):
                return pe.transpose(out, in_, ident[0:in_.shape[0], 0:in_.shape[0]])

            def hold(s, v):
                pe.wait_ge(s, v)
                pe.sem_inc(sem("pe_held"), 1)

            def slot_ready(l, pos, j=0):
                hold(sem("weights_split"), l * N_POS + pos + 1 + j * 4)

            hdnR = hdn.bitcast(F32R)

            def product(out, pos, t, rows, high, low_, start=True, stop=True, low_ready=None):
                wl, wh = ringR[:, pos % RING], whighR[:, pos % 2]
                cols = [slice(k * 256 + t * P, k * 256 + t * P + P) for k in range(rows)]
                for k in range(rows):
                    mm(out, wh[:, cols[k]], high[:, k, :], start and k == 0, False)
                for k in range(rows):
                    mm(out, wl[:, cols[k]], high[:, k, :], False, False)
                if low_ready is not None:
                    hold(sem("hdn_low"), low_ready)
                for k in range(rows):
                    g = mm(out, wh[:, cols[k]], low_[:, k, :], False, stop and k == rows - 1)
                return g

            pe.sem_inc(sem("sadd_done"), FREE)
            pe.wait_ge(sem("const_loaded"), 16)
            pe.wait_ge(sem("gain_rows_loaded"), 16)
            tr(B(0, 96), stage[0:96, :]).then_inc(sem("gains_turned"), 1)
            pe.wait_ge(sem("param_rows_loaded"), 14 * 16)
            tr(B(1, 104), stage[0:104, :]).then_inc(sem("params_turned"), 1)
            pe.wait_ge(sem("x_loaded"), 32)
            for k in range(KT):
                if k < 2:
                    pe.wait_ge(sem("params_placed"), 2)
                for c, (o, L) in enumerate(CH):
                    last_mm = tr(ps[:, k, o:o + L], xtok_s[0:L, c, k * P:(k + 1) * P])
                last_mm.then_inc(sem("x_turned"), 1)

            pe.wait_ge(sem("x_done"), KT)

            def ffn(l, f):
                pre, post = (0, 0) if f == 0 else (2, 2)
                hold(sem("hdn_high"), l * 24 + pre * 8 + 8)
                low_ready = [l * 6 + pre * 2 + 2]

                def pair(pos, tile0, j):
                    for n, done in enumerate(("gate_done", "up_done")):
                        slot_ready(l, pos + n, j)
                        for t in range(2):
                            hold(sem("h_done" if n else "silu_done"), tile0 + t + 1)
                            product(ps[:, 2 * t + n, 0:T], pos + n, t, KT, hdnR, yR,
                                    low_ready=low_ready.pop() if low_ready else None)\
                                .then_inc(sem(done), 1)

                base = POS_FFN[f]
                with pe.Fori(0, PAIRS // 2) as j:
                    for t in range(2):
                        pair(base + 2 * t, l * 44 + f * 22 + j * 4 + 2 * t, j)
                pair(base + 4 * (PAIRS // 2), l * 44 + f * 22 + 20, 0)
                pos = base + 2 * PAIRS
                hold(sem("h_done"), l * 44 + f * 22 + 22 + H_CREDIT)
                for mp in range(4):
                    for part, nk in enumerate(DOWN):
                        slot_ready(l, pos + 3 * mp + part)
                        ks = slice(8 * part, 8 * part + nk)
                        for t in range(2):
                            m = 2 * mp + t
                            if part == 0:
                                hold(sem("y_done"), l * 24 + post * 8 + m + 1)
                            d = product(ps[:, m % 4, 0:T], pos + 3 * mp + part, t, nk, bigR[:, ks], lowR[:, ks],
                                        part == 0, part == 2)
                            if part == 2:
                                d.then_inc(sem("post_product_done"), 1)
                        if part < 2:
                            d.then_inc(sem("down_part_done"), 1)

            def norm_post(l, post):
                pe.wait_ge(sem("squares_added"), l * 24 + post * 8 + 8)
                mm(ps[:, 4, 0:T], ones, ssum[:, :]).then_inc(sem("norm_sum"), 1)

            def norm_pre(l, pre):
                for k in range(KT):
                    pe.wait_ge(sem("x_squared"), l * 24 + pre * 8 + k + 1)
                    n = mm(ps[:, 4, 0:T], ones, y[:, k, :], k == 0, k == KT - 1)
                n.then_inc(sem("norm_sum"), 1)

            def mixers(l):
                l1 = l + 1
                hold(sem("hdn_high"), l * 24 + 16)
                for i in range(NPT):
                    if i >= 4:
                        hold(sem("proj_read"), l * NPT + i - 3)
                    if i % 2 == 0:
                        slot_ready(l, POS_IN + i // 2)
                    product(ps[:, i % 4, 0:T], POS_IN + i // 2, i % 2, KT, hdnR, yR,
                            low_ready=None if i else l * 6 + 4).then_inc(sem("proj_done"), 1)
                    if i == 1:
                        hold(sem("layer_params"), l1)
                        hR, lR = hdnf[:, :].bitcast(F32R), yfR
                        wh, wl = wgh[:, :, :].bitcast(F32R), wgR
                        for c in range(3):
                            for n, (a, w) in enumerate(((hR, wh), (hR, wl), (lR, wh))):
                                for k in range(KT):
                                    g = mm(ps[:, 5, 20 * c:20 * c + 20], a[:, k * T + c * P:k * T + (c + 1) * P],
                                           w[:, k, :], n == 0 and k == 0, n == 2 and k == KT - 1)
                        g.then_inc(sem("gates_done"), 1)
                        hold(sem("hist_loaded"), l1 * 32)
                        for t in range(NC):
                            g = tr(B(6, NC, NB * 3)[:, t, :], hist[:, t, :])
                        g.then_inc(sem("hist_turned"), 1)
                hold(sem("proj_read"), l * NPT + NPT)
                hold(sem("decays_ready"), l1)
                cb, tb = B(4, 3, 12), B(7, 3, 12)
                mm(cb[:, 0, :], C("tri"), G[:, 0, :])
                mm(cb[:, 1, :], C("tri"), G[:, 1, :], True, False)
                mm(cb[:, 1, 8:12], ones, G[:, 0, 8:12], False, True)
                mm(cb[:, 2, :], C("tri_s"), G[:, 2, :])
                mm(tb[:, 0, :], ones, G[:, 0, :])
                mm(tb[:, 1, :], ones, G[:, 1, :])
                mm(tb[:, 2, :], C("blk_s"), G[:, 2, :]).then_inc(sem("cum_done"), 1)
                hold(sem("decays_spread"), l1)
                for n in range(4):
                    e = ps[:, n // 2, 160 * (n % 2):160 * (n % 2) + 160]
                    mm(e[:, 0:P], Gb[:, 0, 2 * n:2 * n + 2, :].rearrange("p s d -> p (s d)"), C("tri"))
                    mm(e[:, P:], Gb[:, 1, 2 * n:2 * n + 2, :].rearrange("p s d -> p (s d)"),
                       C("tri_s")[:, 0:NS])
                    mm(ps[:, 2, n:n + 1], Gb[:, 0, 2 * n:2 * n + 2, :].rearrange("p s d -> p (s d)"),
                       ones[:, 0:1])
                mm(ps[:, 3, 0:16], C("blsel", NS), Gx[:, 0:16])
                mm(ps[:, 3, 16:48], ones[0:NS, :], Gx[:, 16:48]).then_inc(sem("erow_done"), 1)
                hold(sem("a_ready"), l1)
                for c, (o, L) in enumerate(CH):
                    g = tr(ps[0:H, 5, o:o + L], aT[0:L, c, :])
                g.then_inc(sem("a_turned"), 1)
                hold(sem("m_rows_ready"), l1)
                for n, row in enumerate((mH, mL, eD)):
                    for c, (o, L) in enumerate(CH):
                        g = tr(ps[0:L, 5, 300 + (3 * n + c) * H:300 + (3 * n + c) * H + H], row[:, o:o + L])
                for a in range(2):
                    mm(ps[:, 6, 160 * a:160 * a + 160], sel2[0:H, a, :], eI[:, P:T])
                for a in range(2):
                    g = mm(ps[:, 6, 320 + a:321 + a], sel2[0:H, a, :], eD[:, P:P + 1])
                g.then_inc(sem("m_tok_done"), 1)
                hold(sem("ml_decay_spread"), l1)
                mm(ps[:, 7, 64:80], C("blsel", NS), Gx[:, 48:64]).then_inc(sem("ml_decS_done"), 1)
                hold(sem("qk_squared"), l1)
                hold(sem("er_read"), l1)
                for n in range(4):
                    g = mm(ps[:, n, 0:T], bdones, DTf[:, n * T:(n + 1) * T])
                g.then_inc(sem("qk_norms_done"), 1)
                hold(sem("qk_norms_read"), l1)
                for n in range(4):
                    g = mm(ps[:, n, 0:T], C("rot"), big[:, RET_T + n, :])
                g.then_inc(sem("rotated"), 1)
                for a in range(2):
                    for c, (o, L) in enumerate(CH):
                        g = mm(ps[:, 4 + a, o:o + L],
                               Bb[0:L, c, 2 * a:2 * a + 2, :].rearrange("p h d -> p (h d)"), ident[0:L, 0:L])
                g.then_inc(sem("beta_rows_done"), 1)
                for mi, m in enumerate(MIX):
                    mixer(l, l1, mi, m)
                hold(sem("mixed_ready"), l * 4 + 4 + FREE)
                for t in range(NC):
                    g = tr(ps[0:27, 4 + t // 4, (t % 4) * P:(t % 4 + 1) * P], last[:, t, :])
                g.then_inc(sem("last_turned"), 1)

            def mixer(l, l1, mi, m):
                w = HW[m]
                Sx = SX[m]
                hold(sem("mixed_ready"), l * 4 + mi + FREE)
                hold(sem("qk_ready"), l * 4 + mi + 1)
                for c, (o, L) in enumerate(CH):
                    if c or mi:
                        hold(sem("kv_read"), l * 12 + 3 * mi + c)
                    kts = (KTL[m],) if m == "ssd" else (KTL[m], KTL[m] + 1)
                    for n, t in enumerate(kts):
                        tr(ps[0:L, 4, n * P:(n + 1) * P], big[:, t, o:o + L])
                    for n in range(2):
                        g = tr(ps[0:L, 4, GW + n * P:GW + (n + 1) * P], big[:, VTL[m] + n, o:o + L])
                    g.then_inc(sem("kv_turned"), 1)
                if m != "ret":
                    for c, (o, L) in enumerate(CH):
                        if c:
                            hold(sem("decay_arg"), l * 9 + 3 * [0, 1, 0, 2][mi] + c)
                        for s in range(H):
                            out = ps[0:L, 1, s * L:(s + 1) * L]
                            if m == "ml":
                                g = mm(out, C("nident", H)[:, s:s + 1].broadcast_to([H, L]), mH[:, o:o + L])
                            else:
                                h = head(m, s // 2, s % 2)
                                tri = C("tri") if c < 2 else C("tri_s")[0:NS, 0:NS]
                                g = mm(out, G[0:L, c, DC[m] + h:DC[m] + h + 1].broadcast_to([L, L]), tri)
                        g.then_inc(sem("decay_rows"), 1)
                for s in range(H):
                    g = mm(ps[:, 3, s * NS:(s + 1) * NS], dup[:, s % 2, :], qi[:, s // 2, P:])
                if m == "gdn":
                    for s in range(H):
                        g = mm(ps[:, 3, P + s * NS:P + (s + 1) * NS], dup[:, s % 2, :], ki[:, s // 2, P:])
                g.then_inc(sem("dup_done"), 1)
                if m == "ssd":
                    states_in(l1, m)
                    for bp in range(4):
                        if bp:
                            hold(sem("snat_read"), l * 4 + bp)
                        for s in range(H):
                            h = head(m, s // 2, s % 2)
                            g = tr(ps[:, 5, s * HD:(s + 1) * HD],
                                   Snat[:, h, 2 * bp:2 * bp + 2, :].rearrange("p b n -> p (b n)"))
                        g.then_inc(sem("snat_turned"), 1)
                if m == "gdn":
                    gdn_solve(l, l1)
                for c, (o, L) in enumerate(CH):
                    if c:
                        hold(sem("probs_ready"), l * 12 + 3 * mi + c)
                    if m == "ssd":
                        g = mm(ps[0:L, 0, 0:2 * L], big[:, KTL[m], o:o + L],
                               qbd[:, 0, :, o:o + L])
                    else:
                        for a in range(2):
                            g = mm(ps[0:L, 0, 2 * L * a:2 * L * (a + 1)], big[:, KTL[m] + a, o:o + L],
                                   qbd[:, a, :, o:o + L])
                    g.then_inc(sem("scores_done"), 1)
                    if m == "gdn":
                        if c:
                            if c == 1:
                                for a in range(2):
                                    g = mm(ps[:, 5, a * P:(a + 1) * P], ki[:, a, 0:P],
                                           Sbd[:, a, :, 0:HD])
                            else:
                                states_in(l1, m)
                                for s in range(H):
                                    for bp in range(4):
                                        g = mm(ps[0:NS, 5, s * HD:(s + 1) * HD], KQX[:, s, bp, :],
                                               Sx[:, bp, s, 0:HD], bp == 0, bp == 3)
                            g.then_inc(sem("ks_done"), 1)
                        hold(sem("resid_ready"), l * 3 + c + 1)
                        for s in range(H):
                            xt = XT[:, c, s, :] if c < 2 else XTs[:, s, :]
                            g = mm(ps[0:L, 6, s * HD:(s + 1) * HD], xt, VW[0:L, c, s, 0:HD])
                        g.then_inc(sem("vnew_done"), 1)
                    hold(sem("probs_ready"), l * 12 + 3 * mi + c + 1)
                    hold(sem("values_ready"), l * 12 + 3 * mi + c + 1)
                    if c or mi:
                        hold(sem("on_ready"), l * 12 + 3 * mi + c)
                    if c == 2:
                        states_in(l1, m)
                        hold(sem("qx_ready"), l * 4 + mi + 1)
                    for s in range(H):
                        out = ps[0:L, 2, s * w:(s + 1) * w]
                        if c == 1:
                            b = s % 2
                            mm(out, qi[:, s // 2, 0:P], Sbd[:, s // 2, b, 0:w], True, False)
                        if c == 2:
                            for bp in range(4):
                                mm(out, QX[:, s, bp, :], Sx[:, bp, s, 0:w], bp == 0, False)
                        g = mm(out, PT[0:L, c, s, 0:L], V[0:L, c, s, 0:w], c == 0, True)
                    g.then_inc(sem("out_done"), 1)
                    hold(sem("vw_ready"), l * 12 + 3 * mi + c + 1)
                    if c < 2:
                        if c:
                            hold(sem("state_read"), l * 8 + 2 * mi + c)
                        for s in range(H):
                            a, b = s // 2, s % 2
                            kc = b if m == "ssd" else s
                            g = mm(ps[b * HD:(b + 1) * HD, 7, a * w:(a + 1) * w],
                                   K[:, c, kc * HD:(kc + 1) * HD], VW[:, c, s, 0:w])
                        g.then_inc(sem("state_add"), 1)
                        if c == 0:
                            hold(sem("state_read"), l * 8 + 2 * mi + 1)
                    elif m == "ssd":
                        hold(sem("kx_ready"), l * 4 + mi + 1)
                        for s in range(H):
                            if s:
                                hold(sem("sadd_read"), l * 16 + 4 * mi + s)
                            mm(ps[0:HD, 3, :], VW[0:NS, 2, s, 0:HD],
                               KX[:, s % 2, :, :].rearrange("p b n -> p (b n)")).then_inc(sem("sadd_done"), 1)
                    else:
                        hold(sem("kx_ready"), l * 4 + mi + 1)
                        for bp in range(4):
                            if bp:
                                hold(sem("sadd_read"), l * 16 + 4 * mi + bp)
                            for s in range(H):
                                g = mm(ps[:, 3, s * w:(s + 1) * w],
                                       KX[:, s, 2 * bp:2 * bp + 2, :].rearrange("p b d -> p (b d)"),
                                       VW[0:NS, 2, s, 0:w])
                            g.then_inc(sem("sadd_done"), 1)
                    hold(sem("on_ready"), l * 12 + 3 * mi + c + 1)
                    for n in range(2):
                        g = tr(outT(m, n)[:, o:o + L], on[0:L, c, n * P:(n + 1) * P])
                    g.then_inc(sem("on_turned"), 1)
                if m == "ssd":
                    hold(sem("ssd_squared"), l1)
                    for n in range(2):
                        g = mm(ps[:, 0, 0:T], ones, tiny[:, n, :], n == 0, n == 1)
                    g.then_inc(sem("ssd_sum"), 1)
                    hold(sem("state_read"), l * 8 + 2 * mi + 2)
                    for a in range(2):
                        g = tr(ps[0:HD, 7, a * P:(a + 1) * P], S1[:, a, 0:HD])
                    g.then_inc(sem("ssd_state_turned"), 1)

            def states_in(l1, m):
                hold(sem("states_loaded_" + m), l1 * (256 if m == "ml" else 128))

            def outT(m, n):
                return ps[:, OUTB[m][n], :]

            def gdn_solve(l, l1):
                hold(sem("kbd_ready"), l1)
                for c, (o, L) in enumerate(CH):
                    if c:
                        hold(sem("at_ready"), l * 3 + c)
                    for a in range(2):
                        g = mm(ps[0:L, 0, 2 * L * a:2 * L * (a + 1)], big[:, KTL["gdn"] + a, o:o + L],
                               kbd[:, a, :, o:o + L])
                    g.then_inc(sem("gram_done"), 1)
                hold(sem("at_ready"), l * 3 + 3)
                for k in range(7):
                    cs = (0, 1, 2) if k < 2 else (0, 1)
                    for c in cs:
                        L = CH[c][1]
                        n = k * 3 + c if k < 2 else 6 + (k - 2) * 2 + c
                        if k:
                            hold(sem("x_level"), l * 16 + ([0, 3, 6, 8, 10, 12, 14][k - 1]) + c + 1)
                        for s in range(H):
                            at = AT[:, c, s, :] if c < 2 else ATs[:, s, :]
                            xx = X[:, 4 * c + s, :] if c < 2 else Xs[:, s, :]
                            g = mm(LB(0, c, L)[:, s, :], at, xx)
                        g.then_inc(sem("level_t"), 1)
                    for c in cs:
                        L = CH[c][1]
                        hold(sem("t_masked"), l * 16 + [0, 3, 6, 8, 10, 12, 14][k] + c + 1)
                        for s in range(H):
                            xt = XT[:, c, s, :] if c < 2 else XTs[:, s, :]
                            tm = Tm[:, c, s, :] if c < 2 else Tms[:, s, :]
                            mm(LB(1, c, L)[:, s, :], xt, tm)
                            g = mm(LB(2, c, L)[:, s, :], tm, xt)
                        g.then_inc(sem("level_y"), 1)
                hold(sem("x_level"), l * 16 + 16)

            with pe.Fori(0, DEPTH) as l:
                norm_pre(l, 0)
                ffn(l, 0)
                norm_post(l, 0)
                norm_pre(l, 1)
                mixers(l)
                hold(sem("last_read"), l + 1)
                for i in range(4):
                    slot_ready(l, POS_OUT + i)
                    for t in range(2):
                        m = 2 * i + t
                        hold(sem("y_done"), l * 24 + 8 + m + 1)
                        product(ps[:, m % 4, 0:T], POS_OUT + i, t, KT, hdnR, bigR)\
                            .then_inc(sem("post_product_done"), 1)
                norm_post(l, 1)
                norm_pre(l, 2)
                ffn(l, 1)
                norm_post(l, 2)
            pe.wait_ge(sem("x_done"), 24 * DEPTH + KT)
            for c, (o, L) in enumerate(CH):
                if c:
                    pe.wait_ge(sem("x_out_read"), c)
                for k in range(KT):
                    g = tr(ps[0:L, k // 4, (k % 4) * P:(k % 4 + 1) * P], x[:, k, o:o + L])
                g.then_inc(sem("x_back"), 1)

        @block.scalar
        def _(act):
            A = act.activation
            n_chain = [0]

            def link(l, ins):
                n_chain[0] += 1
                ins.then_inc(sem("act_chain"), 1)
                act.wait_ge(sem("act_chain"), l * CHAIN["act"] + n_chain[0])

            act.sem_inc(sem("y_done"), Y_CREDIT)
            act.sem_inc(sem("silu_done"), H_CREDIT)
            act.dma_start(cst[:, :], I["const"]).then_inc(sem("const_loaded"), 16)

            def rsqrt(l, out, src, scale, eps=True):
                link(l, A(out, src, ACT.Ln, bias=epsc[0:out.shape[0], :], scale=scale))
                return A(out, out, ACT.Exp, scale=-0.5)

            def upper(l, pos, rows=KT, free=None, j=0):
                s, v = ring_pos(l, pos)
                act.wait_ge(w_in_s[s], v + j * 16)
                if free:
                    act.wait_ge(*free)
                A(whighR[:, pos % 2, 0:rows * 256], ring[:, s, 0:rows * 256], ACT.Copy)\
                    .then_inc(sem("weights_high"), 1)

            def next_upper(l, pos):
                upper(l, pos, free=used(l, pos - 2) if pos >= 2 else None)

            def upper_hdn(l, n):
                for k in range(KT):
                    act.wait_ge(sem("hdn_full"), l * 24 + n * 8 + k + 1)
                    A(hdn[:, k, :].bitcast(F32R), y[:, k, :], ACT.Copy).then_inc(sem("hdn_high"), 1)

            def norm(l, i):
                act.wait_ge(sem("norm_sum"), l * 6 + i + 1)
                act.wait_ge(sem("rrow_used"), l * 6 + i + FREE)
                link(l, A(lnr[:, :], ps[:, 4, 0:T], ACT.Ln, bias=epsc[:, :], scale=1.0 / D))
                A(rrow[:, :], lnr[:, :], ACT.Exp, scale=-0.5).then_inc(sem("rrow_ready"), 1)

            def squares(l, pre, post_done, during):
                for k in range(KT):
                    if k == 3:
                        for pos in during:
                            next_upper(l, pos)
                    act.wait_ge(sem("x_done"), post_done + k + 1)
                    A(y[:, k, :], x[:, k, :], ACT.Square).then_inc(sem("x_squared"), 1)

            def products(l, post, ms):
                for m in ms:
                    act.wait_ge(sem("post_product_done"), l * 24 + post * 8 + m + 1)
                    if m >= 2:
                        act.wait_ge(sem("squares_added"), l * 24 + post * 8 + m - 1)
                    A(sq[:, m % 2, :], ps[:, m % 4, 0:T], ACT.Square)
                    A(y[:, m, :], ps[:, m % 4, 0:T], ACT.Copy).then_inc(sem("y_done"), 1)

            def ffn(l, f):
                base = POS_FFN[f]

                def silus(i0):
                    for t in range(2):
                        act.wait_ge(sem("gate_done"), i0 + t + 1)
                        act.wait_ge(sem("h_done"), i0 + t - 1 + H_CREDIT)
                        A(sg[:, t, :], ps[:, 2 * t, 0:T], ACT.Silu).then_inc(sem("silu_done"), 1)

                with act.Fori(0, PAIRS // 2) as j:
                    for t in range(2):
                        silus(l * 2 * FT + f * FT + j * 4 + 2 * t)
                        upper(l, base + 2 * t + 2, free=gate_used(l, f, j * 2 + t), j=j)
                        upper(l, base + 2 * t + 3, free=up_used(l, f, j * 2 + t), j=j)
                silus(l * 2 * FT + f * FT + FT - 2)
                pos = base + 2 * PAIRS
                upper(l, pos, free=used(l, pos - 2))
                upper(l, pos + 1, free=used(l, pos - 1))
                for mp in range(4):
                    for part, rows in enumerate(DOWN):
                        n = 3 * mp + part
                        if n >= 2:
                            upper(l, pos + n, rows, used(l, pos + n - 2))
                    if mp:
                        products(l, 2 * f, (2 * mp - 2, 2 * mp - 1))
                if f == 0:
                    next_upper(l, POS_IN)
                products(l, 2 * f, (KT - 2, KT - 1))

            def mixers(l):
                l1 = l + 1
                def conv_silu(ct):
                    act.wait_ge(sem("conv_done"), l * NC + ct + 1)
                    A(big[:, CONV_T[ct], 0:SEQ], big[:, CONV_T[ct], 0:SEQ], ACT.Silu)\
                        .then_inc(sem("conv_silu"), 1)

                for i in range(NPT):
                    act.wait_ge(sem("proj_done"), l * NPT + i + 1)
                    src = ps[:, i % 4, 0:T]
                    if i % 2 and i < NPT - 3:
                        next_upper(l, POS_IN + (i + 3) // 2)
                    if i in CONV_T:
                        ct = CONV_T.index(i)
                        A(xP[:, ct, 3:], src[:, 0:SEQ], ACT.Copy)
                        g = A(xS[:, ct, :, 3:], src[:, SEQ:].rearrange("p (b t) -> p b t", t=LS), ACT.Copy)
                    elif i in SILU_T:
                        g = A(big[:, i, :], src, ACT.Silu)
                    elif i >= 28:
                        g = A(big[:, i, :], src, ACT.Tanh, scale=0.5)
                    elif i in (16, 17, 24, 25):
                        g = A(big[:, i, :], src, ACT.Copy, scale=HD ** -0.5)
                    else:
                        g = A(big[:, i, :], src, ACT.Copy)
                    g.then_inc(sem("proj_read"), 1)
                    if i >= 5 and i % 2 and (i - 5) // 2 < NC:
                        conv_silu((i - 5) // 2)
                    if i == 26:
                        act.wait_ge(sem("conv_s_done"), l1)
                        for ct in range(NC):
                            g = A(big[:, CONV_T[ct], SEQ:T],
                                  ctmp[:, ct, :, :].rearrange("p b t -> p (b t)"), ACT.Silu)
                        g.then_inc(sem("conv_s_silu"), 1)
                        act.wait_ge(sem("u_ready"), l1)
                        link(l, A(AB[:, :, :], U[:, :, 0:12], ACT.Abs))
                        link(l, A(AB[:, :, :], AB[:, :, :], ACT.Exp, scale=-1.0))
                        A(AB[:, :, :], AB[:, :, :], ACT.Ln, bias=1.0)
                        A(alog[:, 0:8], alog[:, 0:8], ACT.Exp)
                        A(beta[:, :, :], U[:, :, 12:16], ACT.Exp).then_inc(sem("gate_exps"), 1)
                act.wait_ge(sem("act_chain"), l * CHAIN["act"] + n_chain[0])
                act.wait_ge(sem("conv_s_silu"), l1)
                link(l, A(DTf[:, 0:4 * T], big[:, 0:4, :].rearrange("p k t -> p (k t)"), ACT.Square))
                A(sml[0:1, 0, 0:1], epsc[0:1, :], ACT.Copy).then_inc(sem("qk_squared"), 1)
                act.wait_ge(sem("w_arg"), l1)
                A(wexp[:, :, 0:8], wexp[:, :, 0:8], ACT.Exp).then_inc(sem("wexp_ready"), 1)
                act.wait_ge(sem("erow_done"), l1)
                for n in range(2):
                    A(er[:, 2 * n:2 * n + 2, :], B(n, 2, 160), ACT.Exp)
                A(decP[:, 0:4], ps[:, 2, 0:4], ACT.Exp)
                A(decS[:, 0:48], ps[:, 3, 0:48], ACT.Exp).then_inc(sem("er_read"), 1)
                act.wait_ge(sem("m_rows_arg"), l1)
                A(eI[:, :], eI[:, :], ACT.Exp)
                A(eD[:, :], eD[:, :], ACT.Exp).then_inc(sem("m_rows_ready"), 1)
                act.wait_ge(sem("ml_arg"), l1)
                for rows, cc in ((P, slice(0, 2)), (NS, slice(2, 3))):
                    A(emt[0:rows, cc, :], mt[0:rows, cc, :], ACT.Exp, scale=-1.0)
                    g = A(wexp[0:rows, cc, 8:12], wexp[0:rows, cc, 8:12], ACT.Exp)
                g.then_inc(sem("ml_exps"), 1)
                act.wait_ge(sem("qk_norms_done"), l1)
                for n in range(4):
                    g = A(DTf[:, n * T:(n + 1) * T], ps[:, n, 0:T], ACT.Ln, bias=epsc[:, :])
                link(l, g)
                A(DTf[:, 0:4 * T], DTf[:, 0:4 * T], ACT.Exp, scale=-0.5).then_inc(sem("qk_norms_read"), 1)
                for mi, m in enumerate(MIX):
                    if m == "ml":
                        act.wait_ge(sem("ssm_samples_stored"), l1 * NB * 16)
                        upper(l, POS_OUT)
                    if m != "ret":
                        for c, (o, L) in enumerate(CH):
                            act.wait_ge(sem("decay_arg"), l * 9 + 3 * [0, 1, 0, 2][mi] + c + 1)
                            A(DT[0:L, c, :, 0:L], DT[0:L, c, :, 0:L], ACT.Exp).then_inc(sem("decay_ready"), 1)
                    if m == "ssd":
                        act.wait_ge(sem("ssd_gated"), l1)
                        for n in range(2):
                            g = A(tiny[:, n, :], big[:, 8 + n, :], ACT.Square)
                        g.then_inc(sem("ssd_squared"), 1)
                        act.wait_ge(sem("ssd_sum"), l1)
                        link(l, A(lnr[:, :], ps[:, 0, 0:T], ACT.Ln, bias=epsc[:, :], scale=1.0 / GW))
                        A(lnr[:, :], lnr[:, :], ACT.Exp, scale=-0.5).then_inc(sem("ssd_rrow"), 1)
                        continue
                    for c, (o, L) in enumerate(CH):
                        i3 = l * 9 + 3 * [0, 0, 1, 2][mi] + c + 1
                        if m == "ml":
                            act.wait_ge(sem("hout_ready"), l * 3 + c + 1)
                            src = hout[0:L, :]
                        else:
                            act.wait_ge(sem("out_done"), l * 12 + 3 * mi + c + 1)
                            src = ps[0:L, 2, 0:GW]
                        A(osq[0:L, :], src, ACT.Square).then_inc(sem("out_sq"), 1)
                        act.wait_ge(sem("out_ss"), i3)
                        link(l, A(sml[0:L, 1, :], sml[0:L, 0, :], ACT.Ln, bias=epsc[0:L, :], scale=1.0 / HD))
                        A(sml[0:L, 2, :], sml[0:L, 1, :], ACT.Exp, scale=-0.5).then_inc(sem("out_rn"), 1)
                act.wait_ge(sem("sadd_done"), l * 16 + 16 + FREE)
                upper(l, POS_OUT + 1)

            with act.Fori(0, DEPTH) as l:
                n_chain[0] = 0
                squares(l, 0, l * 24, (0, 1))
                norm(l, 0)
                upper_hdn(l, 0)
                ffn(l, 0)
                norm(l, 1)
                squares(l, 1, l * 24 + 8, (POS_IN + 1,))
                norm(l, 2)
                upper_hdn(l, 1)
                mixers(l)
                for i in (2, 3):
                    next_upper(l, POS_OUT + i)
                    products(l, 1, (2 * i - 4, 2 * i - 3))
                products(l, 1, (4, 5))
                next_upper(l, POS_FFN[1])
                products(l, 1, (6, 7))
                norm(l, 3)
                squares(l, 2, l * 24 + 16, (POS_FFN[1] + 1,))
                norm(l, 4)
                upper_hdn(l, 2)
                ffn(l, 1)
                norm(l, 5)
            print("act chain", n_chain[0])
            assert n_chain[0] == CHAIN["act"] or not STRICT

        @block.vector
        def _(dve):
            TT, TS, STT, CP = dve.tensor_tensor, dve.tensor_scalar, dve.scalar_tensor_tensor, dve.tensor_copy
            n_chain = [0]

            def link(l, ins):
                n_chain[0] += 1
                ins.then_inc(sem("dve_chain"), 1)
                dve.wait_ge(sem("dve_chain"), l * CHAIN["dve"] + n_chain[0])

            dve.sem_inc(sem("h_done"), H_CREDIT)
            dve.sem_inc(sem("rrow_used"), FREE)
            dve.sem_inc(sem("mixed_ready"), FREE)
            dve.memset(epsc[:, :], EPS)
            dve.memset(gb2[:, :, 12:16], 0.0)
            dve.memset(ssum[:, :], 0.0).then_inc(sem("zeros_set"), 1)
            dve.wait_ge(sem("zeros_set"), 1)
            for tile in (hdnf[:, KT * T:].bitcast(F32R), yfR[:, KT * T:]):
                CP(tile, ssum[:, 0:3 * P - T])
            dve.memset(V[:, :, :, HD:], 1.0)
            dve.memset(Sbd[:, :, :, :], 0.0)
            dve.memset(qbd[:, :, :, :], 0.0)
            dve.memset(cbias[:, 0:6], 0.0)
            dve.memset(al2[:, :, 8:12], -1.0).then_inc(sem("dve_set"), 1)
            dve.wait_ge(sem("gains_turned"), 1)
            CP(gn[:, :, :, :].rearrange("p l i k -> p (l i k)"), B(0, 96)).then_inc(sem("params_placed"), 1)
            dve.wait_ge(sem("params_turned"), 1)
            CP(p2[:, :, :].rearrange("p l n -> p (l n)"), B(1, 104)).then_inc(sem("params_placed"), 1)
            for k in range(KT):
                dve.wait_ge(sem("x_turned"), k + 1)
                CP(x[:, k, :], ps[:, k, 0:T]).then_inc(sem("x_done"), 1)
            dve.wait_ge(sem("x_done"), KT)
            dve.wait_ge(sem("params_placed"), 2)
            dve.wait_ge(sem("dve_set"), 1)

            def upper(out, in_):
                return CP(out, in_)

            def lower(out, in_, high):
                return TT(out, in_, high, ALU.subtract)

            def lower_weights(l, pos, rows=KT, j=0):
                dve.wait_ge(sem("weights_high"), l * N_POS + pos + 1 + j * 4)
                n = rows * 256
                lower(ringR[:, pos % RING, 0:n], ring[:, pos % RING, 0:n], whighR[:, pos % 2, 0:n].bitcast(F32)).then_inc(sem("weights_split"), 1)

            def pre(l, i):
                if i == 0:
                    lower_weights(l, 0)
                lower_weights(l, (POS_FFN[0], None, POS_IN, None, POS_FFN[1])[i] + 1)
                dve.wait_ge(sem("rrow_ready"), l * 6 + i + 1)
                for k in range(KT):
                    STT(y[:, k, :], x[:, k, :], gcol[:, i, k:k + 1], rrow[:, :], ALU.mult, ALU.mult)\
                        .then_inc(sem("hdn_full"), 1)
                for n in range(2):
                    ks = slice(4 * n, 4 * n + 4)
                    dve.wait_ge(sem("hdn_high"), l * 24 + i * 4 + 4 * n + 4)
                    lower(yR[:, ks, :], y[:, ks, :], hdn[:, ks, :]).then_inc(sem("hdn_low"), 1)
                TS(ssum[:, 0:1], rrow[:, 0:1], 1.0, None, ALU.mult).then_inc(sem("rrow_used"), 1)

            def add_squares(l, p, m):
                dve.wait_ge(sem("y_done"), l * 24 + 8 * p + m + 1 + Y_CREDIT)
                if m == 0:
                    g = CP(ssum[:, :], sq[:, 0, :])
                else:
                    dve.wait_ge(sem("squares_added"), l * 24 + 8 * p + m)
                    g = TT(ssum[:, :], ssum[:, :], sq[:, m % 2, :], ALU.add)
                g.then_inc(sem("squares_added"), 1)

            def post(l, p, half):
                i = 2 * p + 1
                g_ = ghalf if half else gcol
                if p < 2:
                    lower_weights(l, (POS_IN, POS_FFN[1])[p])
                dve.wait_ge(sem("rrow_ready"), l * 6 + i + 1)
                for k in range(KT):
                    link(l, STT(y[:, k, :], y[:, k, :], g_[:, i, k:k + 1], rrow[:, :], ALU.mult, ALU.mult))
                    TT(x[:, k, :], x[:, k, :], y[:, k, :], ALU.add).then_inc(sem("x_done"), 1)
                TS(ssum[:, 0:1], rrow[:, 0:1], 1.0, None, ALU.mult).then_inc(sem("rrow_used"), 1)

            def ffn(l, f):
                base = POS_FFN[f]

                def hidden(i, tile, t):
                    dve.wait_ge(sem("silu_done"), i + 1 + H_CREDIT)
                    dve.wait_ge(sem("up_done"), i + 1)
                    h, hR, highR = (v[:, bass.ds(tile, 1), :].rearrange("p o t -> p (o t)")
                                    for v in (low, lowR, bigR))
                    TT(h, sg[:, t, :], ps[:, 2 * t + 1, 0:T], ALU.mult).then_inc(sem("h_product"), 1)
                    dve.wait_ge(sem("h_product"), i + 1)
                    upper(highR, h).then_inc(sem("h_high"), 1)
                    dve.wait_ge(sem("h_high"), i + 1)
                    lower(hR, h, highR.bitcast(F32)).then_inc(sem("h_done"), 1)

                with dve.Fori(0, PAIRS // 2) as j:
                    for t in range(2):
                        i = l * 2 * FT + f * FT + j * 4 + 2 * t
                        lower_weights(l, base + 2 * t + 2, j=j)
                        hidden(i, j * 4 + 2 * t, 0)
                        hidden(i + 1, j * 4 + 2 * t + 1, 1)
                        lower_weights(l, base + 2 * t + 3, j=j)
                i = l * 2 * FT + f * FT + FT - 2
                pos = base + 2 * PAIRS
                lower_weights(l, pos)
                hidden(i, FT - 2, 0)
                hidden(i + 1, FT - 1, 1)
                lower_weights(l, pos + 1)
                for mp in range(4):
                    for part, rows in enumerate(DOWN):
                        n = 3 * mp + part
                        if n >= 2:
                            lower_weights(l, pos + n, rows)
                    if mp:
                        add_squares(l, 2 * f, 2 * mp - 2)
                        add_squares(l, 2 * f, 2 * mp - 1)
                add_squares(l, 2 * f, KT - 2)
                add_squares(l, 2 * f, KT - 1)
                post(l, 2 * f, True)

            def mixers(l):
                l1 = l + 1
                dve.memset(xP[:, :, 0:3], 0.0)
                dve.wait_ge(sem("layers_stored"), l + FREE)

                def weights(n):
                    lower_weights(l, POS_IN + n)

                weights(2)
                dve.wait_ge(sem("gates_done"), l1)
                link(l, TT(U[:, :, :], B(5, 3, 20), bc(gbias[:, :], 1, 3), ALU.add))
                TT(U[:, :, :], U[:, :, :], bc(sign, 1, 3), ALU.mult).then_inc(sem("u_ready"), 1)
                dve.wait_ge(sem("hist_turned"), l1)
                CP(xS[:, :, :, 0:3], B(6, NC, NB * 3).rearrange("p c (b j) -> p c b j", j=3))\
                    .then_inc(sem("hist_placed"), 1)
                for ct in range(NC):
                    i = CONV_T[ct]
                    if ct:
                        weights(ct + 2)
                    dve.wait_ge(sem("proj_read"), l * NPT + i + 1)
                    out = big[:, i, 0:SEQ]
                    link(l, TS(out, xP[:, ct, 0:SEQ], taps[:, ct, 0:1], cbias[:, ct:ct + 1], ALU.mult, ALU.add))
                    for j in (1, 2, 3):
                        g = STT(out, xP[:, ct, j:j + SEQ], taps[:, ct, j:j + 1], out, ALU.mult, ALU.add)
                        if j < 3:
                            link(l, g)
                        else:
                            g.then_inc(sem("conv_done"), 1)
                weights(12)
                dve.wait_ge(sem("hist_placed"), l1)
                bcw = lambda j: taps[:, :, j:j + 1].unsqueeze(3).broadcast_to([P, NC, NB, LS])
                cs = C4[:, :, :, :]
                link(l, TT(ctmp[:, :, :, :], xS[:, :, :, 0:LS], bcw(0), ALU.mult))
                for j in (1, 2, 3):
                    link(l, TT(cs, xS[:, :, :, j:j + LS], bcw(j), ALU.mult))
                    link(l, TT(ctmp[:, :, :, :], ctmp[:, :, :, :], cs, ALU.add))
                TT(ctmp[:, :, :, :], ctmp[:, :, :, :],
                   cbias[:, :].unsqueeze(2).unsqueeze(3).broadcast_to([P, NC, NB, LS]), ALU.add)\
                    .then_inc(sem("conv_s_done"), 1)
                CP(last[:, :, 0:3], xP[:, :, SEQ:SEQ + 3])
                CP(last[:, :, 3:27].rearrange("p c (b j) -> p c b j", j=3), xS[:, :, :, LS:LS + 3])\
                    .then_inc(sem("last_ready"), 1)
                weights(13)
                dve.wait_ge(sem("gate_exps"), l1)
                link(l, STT(SP[:, :, :], U[:, :, 0:12], 0.0, AB[:, :, :], ALU.max, ALU.add))
                TS(alog[:, 0:8], alog[:, 0:8], -1.0, None, ALU.mult)
                link(l, TS(beta[:, :, :], beta[:, :, :], 1.0, None, ALU.add))
                link(l, dve.reciprocal(beta[:, :, :], beta[:, :, :]))
                TT(G[:, :, :], SP[:, :, :], bc(alog[:, :], 1, 3), ALU.mult).then_inc(sem("decays_ready"), 1)
                dve.wait_ge(sem("decays_ready"), l1)
                weights(14)
                CP(Bb[:, :, :, :], bc(beta[:, :, :], 3, HD))
                CP(Gb[:, :, 0:4, :].rearrange("p c (a b) d -> p c a b d", a=2)[:, 0],
                   bc(slots1(G[:, 1, 0:4], "ssd"), 3, HD))
                CP(Gb[:, :, 0:4, :].rearrange("p c (a b) d -> p c a b d", a=2)[:, 1],
                   bc(slots1(G[:, 2, 0:4], "ssd"), 3, HD))
                CP(Gb[:, :, 4:8, :], bc(G[:, 1:3, 4:8], 3, HD))
                TT(Gx[:, 0:16].rearrange("p (a h) -> p a h", h=H), bc(G[0:NS, 2, 4:8], 1, 4),
                   bc(C("obp", NS), 2, H), ALU.mult)
                TT(Gx[:, 16:48].rearrange("p (a h) -> p a h", h=H), bc(G[0:NS, 2, 0:4], 1, NB),
                   bc(C("onehot", NS), 2, H), ALU.mult).then_inc(sem("decays_spread"), 1)
                dve.wait_ge(sem("cum_done"), l1)
                link(l, CP(cum[:, :, :], B(4, 3, 12)))
                TT(wexp[:, :, 0:8], B(7, 3, 12)[:, :, 0:8], cum[:, :, 0:8], ALU.subtract).then_inc(sem("w_arg"), 1)
                TT(aT[:, :, :], U[:, :, 16:20], cum[:, :, 8:12], ALU.subtract).then_inc(sem("a_ready"), 1)
                dve.wait_ge(sem("a_turned"), l1)
                link(l, CP(aH[:, :], ps[0:H, 5, 0:T]))
                link(l, TT(aH[:, SEQ::LS], aH[:, SEQ::LS], mmc[:, :], ALU.max))
                link(l, dve.tensor_tensor_scan(mH[:, :], C("reset", H), aH[:, :], 0.0, ALU.add, ALU.max))
                CP(mL[:, 0:SEQ].rearrange("p (c n) -> p c n", c=2), bc(mH[:, P - 1:SEQ:P], 2, P))
                CP(mL[:, SEQ:].rearrange("p (b t) -> p b t", t=LS), bc(mH[:, SEQ + LS - 1::LS], 2, LS))
                dve.memset(mPv[:, 0:P], 0.0)
                CP(mPv[:, P:SEQ], mH[:, P - 1:P].broadcast_to([H, P]))
                link(l, CP(mPv[:, SEQ:].rearrange("p (b t) -> p b t", t=LS), bc(mmc[:, :], 2, LS)))
                TT(eI[:, :], mPv[:, :], mH[:, :], ALU.subtract)
                TT(eD[:, :], mPv[:, :], mL[:, :], ALU.subtract).then_inc(sem("m_rows_arg"), 1)
                dve.wait_ge(sem("m_tok_done"), l1)
                mtk = lambda n: ps[:, 5, 300 + 12 * n:312 + 12 * n].rearrange("p (c h) -> p c h", h=H)
                for rows, cc in ((P, slice(0, 2)), (NS, slice(2, 3))):
                    TT(mt[0:rows, cc, :], mtk(0)[0:rows, cc, :], cum[0:rows, cc, 8:12], ALU.add)
                    g = TT(wexp[0:rows, cc, 8:12], aT[0:rows, cc, :], mtk(1)[0:rows, cc, :], ALU.subtract)
                g.then_inc(sem("ml_arg"), 1)
                CP(er[:, 4:6, :], B(6, 2, 160))
                CP(decP[:, 4:6], ps[:, 6, 320:322])
                link(l, CP(sml[0:NS, 3, :], mtk(2)[0:NS, 2, :]))
                TT(Gx[:, 48:64].rearrange("p (a h) -> p a h", h=H), bc(sml[0:NS, 3, :], 1, 4),
                   bc(C("first", NS), 2, H), ALU.mult).then_inc(sem("ml_decay_spread"), 1)
                dve.wait_ge(sem("ml_decS_done"), l1)
                CP(decS[:, 48:64], ps[:, 7, 64:80])
                dve.wait_ge(sem("qk_norms_read"), l1)
                STT(big[:, 0:2, :].rearrange("p k t -> p (k t)"), big[:, 0:2, :].rearrange("p k t -> p (k t)"),
                    HD ** -0.5, DTf[:, 0:2 * T], ALU.mult, ALU.mult)
                link(l, TT(big[:, 2:4, :].rearrange("p k t -> p (k t)"),
                           big[:, 2:4, :].rearrange("p k t -> p (k t)"), DTf[:, 2 * T:4 * T], ALU.mult))
                dve.wait_ge(sem("beta_rows_done"), l1)
                dve.wait_ge(sem("kbd_clear"), l1)
                for b in range(2):
                    r = slice(b * HD, (b + 1) * HD)
                    g = TT(kbd[r, :, b, :], big[r, 2:4, :], ps[r, 4:6, 0:T], ALU.mult)
                g.then_inc(sem("kbd_ready"), 1)
                TT(ki[:, :, :], big[:, 2:4, P:T], er[:, 2:4, :], ALU.mult)
                dve.wait_ge(sem("rotated"), l1)
                rq = big[:, RET_T:RET_T + 4, :]
                tmp = DTf[:, 0:4 * T].rearrange("p (k t) -> p k t", k=4)
                TT(tmp, ps[:, 0:4, 0:T], bc(C("sin"), 1, 4), ALU.mult)
                link(l, TT(rq, rq, bc(C("cos"), 1, 4), ALU.mult))
                link(l, TT(rq, rq, tmp, ALU.add))
                link(l, TS(big[:, 28:30, :].rearrange("p k t -> p (k t)"),
                           big[:, 28:30, :].rearrange("p k t -> p (k t)"), 0.5, 0.5, ALU.mult, ALU.add))
                for mi, m in enumerate(MIX):
                    mixer(l, l1, mi, m)
                dve.wait_ge(sem("last_turned"), l1)
                dve.wait_ge(sem("layers_stored"), l + FREE)
                for n in range(3):
                    w = min(4, NC - 4 * n)
                    g = CP(lastT[:, 4 * n:4 * n + w, :].rearrange("p c n -> p (c n)"), ps[0:27, 4 + n, 0:w * P])
                g.then_inc(sem("last_read"), 1)

            def mixer(l, l1, mi, m):
                w = HW[m]
                Sx = SX[m]
                i12 = l * 12 + 3 * mi
                q = QT[m]
                for b in range(2):
                    r = slice(b * HD, (b + 1) * HD)
                    if m == "ssd":
                        CP(qbd[r, 0, b, :], big[r, q, :])
                    else:
                        CP(qbd[r, :, b, :], big[r, q:q + 2, :])
                if m == "ssd":
                    g = TT(qi[:, :, :], bc(big[:, q, P:T], 1, 2), er[:, 0:2, :], ALU.mult)
                else:
                    e = retI if m == "ret" else er[:, 2:4, :] if m == "gdn" else er[:, 4:6, :]
                    g = TT(qi[:, :, :], big[:, q:q + 2, P:T], e, ALU.mult)
                g.then_inc(sem("qk_ready"), 1)
                for c, (o, L) in enumerate(CH):
                    dve.wait_ge(sem("kv_turned"), i12 + c + 1)
                    nk = P if m == "ssd" else GW
                    CP(K[0:L, c, 0:nk], ps[0:L, 4, 0:nk])
                    vsrc = slots(B(4, H, HD, rows=L, off=GW), m)
                    vdst = V[0:L, c, :, 0:HD].rearrange("p (a b) d -> p a b d", a=2)
                    if m == "ssd":
                        TT(Dx[0:L, c].rearrange("p (a b) d -> p a b d", a=2), vsrc,
                           bc(slots1(sD[0:L, :], m), 3, HD), ALU.mult)
                        g = TT(vdst, vsrc, bc(slots1(SP[0:L, c, 0:4], m), 3, HD), ALU.mult)
                    else:
                        g = CP(vdst, vsrc)
                    g.then_inc(sem("kv_read"), 1)
                if m != "ret":
                    neg = (C("neg"), C("neg"), C("neg_s", NS))
                    for c, (o, L) in enumerate(CH):
                        dve.wait_ge(sem("decay_rows"), l * 9 + 3 * [0, 1, 0, 2][mi] + c + 1)
                        for s in range(H):
                            h = head(m, s // 2, s % 2)
                            if m == "ml":
                                col, op = aT[0:L, c, s:s + 1], ALU.add
                            else:
                                col, op = cum[0:L, c, DC[m] + h:DC[m] + h + 1], ALU.subtract
                            g = STT(DT[0:L, c, s, 0:L], ps[0:L, 1, s * L:(s + 1) * L], col, neg[c], op, ALU.add)
                        g.then_inc(sem("decay_arg"), 1)
                dve.wait_ge(sem("dup_done"), l * 4 + mi + 1)
                spread = lambda off: bc(B(3, H, NS, off=off), 2, 4)
                g = TT(QX[:, :, :, :], spread(0), bc(bmask, 1, H), ALU.mult)
                if m == "gdn":
                    g = TT(KQX[:, :, :, :], spread(P), bc(bmask, 1, H), ALU.mult)
                g.then_inc(sem("qx_ready"), 1)
                if m == "ssd":
                    for bp in range(4):
                        dve.wait_ge(sem("snat_turned"), l * 4 + bp + 1)
                        CP(Sx[:, bp, :, 0:HD], B(5, H, HD)).then_inc(sem("snat_read"), 1)
                if m == "gdn":
                    gdn_solve(l, l1)
                for c, (o, L) in enumerate(CH):
                    dve.wait_ge(sem("scores_done"), i12 + c + 1)
                    if m == "ret":
                        d = retD if c < 2 else retDs[0:NS]
                    else:
                        dve.wait_ge(sem("decay_ready"), l * 9 + 3 * [0, 1, 0, 2][mi] + c + 1)
                        d = DT[0:L, c, :, 0:L]
                    if m == "ssd":
                        g = TT(PT[0:L, c, :, 0:L].rearrange("p (a b) n -> p a b n", a=2),
                               bc(B(0, 2, L, rows=L), 1, 2), d.rearrange("p (a b) n -> p a b n", a=2), ALU.mult)
                    else:
                        g = TT(PT[0:L, c, :, 0:L], B(0, H, L, rows=L), d, ALU.mult)
                    g.then_inc(sem("probs_ready"), 1)
                    if m == "gdn":
                        bt = bc(beta[0:L, c, :], 2, HD)
                        if c:
                            dve.wait_ge(sem("ks_done"), l * 2 + c)
                            link(l, TT(VW[0:L, c, :, 0:HD], V[0:L, c, :, 0:HD], B(5, H, HD, rows=L), ALU.subtract))
                            TT(VW[0:L, c, :, 0:HD], VW[0:L, c, :, 0:HD], bt, ALU.mult)\
                                .then_inc(sem("resid_ready"), 1)
                        else:
                            TT(VW[0:L, c, :, 0:HD], V[0:L, c, :, 0:HD], bt, ALU.mult)\
                                .then_inc(sem("resid_ready"), 1)
                        dve.wait_ge(sem("vnew_done"), l * 3 + c + 1)
                        g = CP(V[0:L, c, :, 0:HD], B(6, H, HD, rows=L))
                    else:
                        g = TS(sml[0:1, 0, 0:1], epsc[0:1, :], 1.0, None, ALU.mult)
                    g.then_inc(sem("values_ready"), 1)
                    dve.wait_ge(sem("values_ready"), i12 + c + 1)
                    if m == "ret":
                        wt = bc(tail[0:L, c, :], 2, w)
                    elif m == "ssd":
                        wt = bc(slots1(wexp[0:L, c, 0:4], m), 3, w)
                    else:
                        wt = bc(wexp[0:L, c, DC[m]:DC[m] + 4], 2, w)
                    dst, src = VW[0:L, c, :, 0:w], V[0:L, c, :, 0:w]
                    if m == "ssd":
                        dst, src = (v.rearrange("p (a b) n -> p a b n", a=2) for v in (dst, src))
                    TT(dst, src, wt, ALU.mult).then_inc(sem("vw_ready"), 1)
                    if c < 2:
                        dve.wait_ge(sem("state_add"), l * 8 + 2 * mi + c + 1)
                        sp_ = B(7, 2, w)
                        if c == 0:
                            if mi:
                                dve.wait_ge(sem("prompt_stored"), l * PSTORES + PS_BEFORE[m])
                            for b in range(2):
                                r = slice(b * HD, (b + 1) * HD)
                                CP(Sbd[r, :, b, 0:w], sp_[r])
                            g = CP(S1[:, :, 0:w], sp_)
                        else:
                            dec = C("ret_dec") if m == "ret" else decP[:, {"ssd": 0, "gdn": 2, "ml": 4}[m]:][:, 0:2]
                            for a in range(2):
                                g = STT(S1[:, a, 0:w], S1[:, a, 0:w], dec[:, a:a + 1], sp_[:, a, :],
                                        ALU.mult, ALU.add)
                        g.then_inc(sem("state_read"), 1)
                        dve.wait_ge(sem("state_read"), l * 8 + 2 * mi + c + 1)
                    finish(l, l1, mi, m, c, L)
                    if c == 2:
                        sample_states(l, l1, mi, m)
                gt, ot, nb = GATE[m], OUT_T[m], NORM[m]
                dve.wait_ge(sem("on_turned"), i12 + 3)
                if m == "ssd":
                    for n in range(2):
                        g = TT(big[:, 8 + n, :], ps[:, OUTB[m][n], 0:T], big[:, gt + n, :], ALU.mult)
                    g.then_inc(sem("ssd_gated"), 1)
                    dve.wait_ge(sem("ssd_state_turned"), l1)
                    CP(fin[:, :, :], B(7, 2, P, rows=HD)).then_inc(sem("ssd_state_read"), 1)
                    dve.wait_ge(sem("ssd_rrow"), l1)
                    for n in range(2):
                        g = STT(big[:, ot + n, :], big[:, 8 + n, :], pcol[:, nb + n:nb + n + 1], lnr[:, :],
                                ALU.mult, ALU.mult)
                else:
                    for n in range(2):
                        g = STT(big[:, ot + n, :], ps[:, OUTB[m][n], 0:T], pcol[:, nb + n:nb + n + 1],
                                big[:, gt + n, :], ALU.mult, ALU.mult)
                link(l, g)
                link(l, upper(hdn[:, ot:ot + 2, :].bitcast(F32R), big[:, ot:ot + 2, :]))
                lower(bigR[:, ot:ot + 2, :], big[:, ot:ot + 2, :], hdn[:, ot:ot + 2, :])\
                    .then_inc(sem("mixed_ready"), 1)

            def finish(l, l1, mi, m, c, L):
                i12 = l * 12 + 3 * mi
                w = HW[m]
                o4 = B(2, H, w, rows=L)
                on4 = on[0:L, c, :].rearrange("p (h d) -> p h d", h=H)
                dve.wait_ge(sem("out_done"), i12 + c + 1)
                if m == "ssd":
                    TT(slots(on4, m), o4.rearrange("p (a b) d -> p a b d", a=2),
                       Dx[0:L, c].rearrange("p (a b) d -> p a b d", a=2), ALU.add).then_inc(sem("on_ready"), 1)
                    return
                i3 = l * 9 + 3 * [0, 0, 1, 2][mi] + c
                if m == "ml":
                    den = o4[:, :, HD:HE].rearrange("p h o -> p (h o)")
                    link(l, CP(sml[0:L, 3, :], den))
                    link(l, STT(sml[0:L, 3, :], sml[0:L, 3, :], -1.0, sml[0:L, 3, :], ALU.mult, ALU.max))
                    link(l, TT(sml[0:L, 3, :], sml[0:L, 3, :], emt[0:L, c, :], ALU.max))
                    link(l, dve.reciprocal(sml[0:L, 3, :], sml[0:L, 3, :]))
                    TT(hout[0:L, :].rearrange("p (h d) -> p h d", h=H), o4[:, :, 0:HD],
                       bc(sml[0:L, 3, :], 2, HD), ALU.mult).then_inc(sem("hout_ready"), 1)
                dve.wait_ge(sem("out_sq"), i3 + 1)
                dve.tensor_reduce(sml[0:L, 0, :], osq[0:L, :].rearrange("p (h d) -> p h d", h=H), AX, ALU.add)\
                    .then_inc(sem("out_ss"), 1)
                dve.wait_ge(sem("out_rn"), i3 + 1)
                src = hout[0:L, :].rearrange("p (h d) -> p h d", h=H) if m == "ml" else o4
                TT(on4, src, bc(sml[0:L, 2, :], 2, HD), ALU.mult).then_inc(sem("on_ready"), 1)

            def sample_states(l, l1, mi, m):
                w = HW[m]
                if m == "ssd":
                    d = decS[0:HD, 16:48].rearrange("p (b h) -> p h b", h=H)
                    v = Snat[:, :, :, :]
                    link(l, TT(v, v, bc(d, 3, HD), ALU.mult))
                    for s in range(H):
                        dve.wait_ge(sem("sadd_done"), l * 16 + 4 * mi + s + 1 + FREE)
                        h = head(m, s // 2, s % 2)
                        TT(Snat[:, h], Snat[:, h], B(3, NB, HD, rows=HD), ALU.add).then_inc(sem("sadd_read"), 1)
                    return
                Sx = SX[m]
                if m == "ret":
                    d = bc(bc(C("ret_decs"), 1, 4), 3, w)
                else:
                    at = 0 if m == "gdn" else 48
                    d = bc(decS[:, at:at + 16].rearrange("p (a h) -> p a h", h=H), 3, w)
                link(l, TT(Sx[:, :, :, 0:w], Sx[:, :, :, 0:w], d, ALU.mult))
                for bp in range(4):
                    dve.wait_ge(sem("sadd_done"), l * 16 + 4 * mi + bp + 1 + FREE)
                    TT(Sx[:, bp, :, 0:w], Sx[:, bp, :, 0:w], B(3, H, w), ALU.add).then_inc(sem("sadd_read"), 1)

            def gdn_solve(l, l1):
                for c, (o, L) in enumerate(CH):
                    dve.wait_ge(sem("gram_done"), l * 3 + c + 1)
                    dve.wait_ge(sem("decay_ready"), l * 9 + c + 1)
                    at = AT[:, c] if c < 2 else ATs[:, :, :]
                    TT(at, B(0, H, L, rows=L), DT[0:L, c, :, 0:L], ALU.mult)
                    idb = bc(ident[0:L, 0:L], 1, H)
                    CP(X[:, 4 * c:4 * c + 4, :] if c < 2 else Xs[:, :, :], idb)
                    CP(XT[:, c] if c < 2 else XTs[:, :, :], idb).then_inc(sem("at_ready"), 1)
                for k in range(7):
                    cs = (0, 1, 2) if k < 2 else (0, 1)
                    i0 = l * 16 + [0, 3, 6, 8, 10, 12, 14][k]
                    for c in cs:
                        L = CH[c][1]
                        dve.wait_ge(sem("level_t"), i0 + c + 1)
                        tm = Tm[:, c] if c < 2 else Tms[:, :, :]
                        TT(tm, LB(0, c, L), bc(level[0:L, k, 0:L], 1, H), ALU.mult).then_inc(sem("t_masked"), 1)
                    for c in cs:
                        L = CH[c][1]
                        dve.wait_ge(sem("level_y"), i0 + c + 1)
                        xx = X[:, 4 * c:4 * c + 4, :] if c < 2 else Xs[:, :, :]
                        xt = XT[:, c] if c < 2 else XTs[:, :, :]
                        TT(xx, xx, LB(1, c, L), ALU.subtract)
                        TT(xt, xt, LB(2, c, L), ALU.subtract).then_inc(sem("x_level"), 1)

            with dve.Fori(0, DEPTH) as l:
                n_chain[0] = 0
                l1 = l + 1
                CP(gcol[:, :, :], gn[:, bass.ds(l, 1), :, :].rearrange("p o i k -> p (o i) k"))
                link(l, CP(pcol[:, :], p2[:, bass.ds(l, 1), :].rearrange("p o n -> p (o n)")))
                TS(ghalf[:, :, :], gcol[:, :, :], 0.5, None, ALU.mult)
                CP(taps[:, 0:6, :], pcol[:, 28:52].rearrange("p (j t) -> p t j", j=4))
                CP(taps[:, 6:10, :], pcol[:, 12:28].rearrange("p (j t) -> p t j", j=4))
                CP(cbias[:, 6:10], pcol[:, 8:12])
                dve.wait_ge(sem("gate_params_loaded"), 16 * 18)
                CP(gbias[:, :], gb2[:, bass.ds(l, 1), :].rearrange("p o n -> p (o n)"))
                CP(alog[:, :], al2[:, bass.ds(l, 1), :].rearrange("p o n -> p (o n)"))
                CP(sD[:, :], sd2[:, bass.ds(l, 1), :].rearrange("p o n -> p (o n)"))
                CP(mmc[:, :], mm[:, bass.ds(l, 1), :].rearrange("p o n -> p (o n)"))
                link(l, CP(wg[:, :, :], wg2[:, bass.ds(l, 1), :, :].rearrange("p o k n -> p (o k) n")))
                link(l, upper(wgh[:, :, :].bitcast(F32R), wg[:, :, :]))
                lower(wgR[:, :, :], wg[:, :, :], wgh[:, :, :]).then_inc(sem("layer_params"), 1)
                dve.wait_ge(sem("layer_params"), l1)
                pre(l, 0)
                ffn(l, 0)
                pre(l, 2)
                mixers(l)
                for i in range(4):
                    lower_weights(l, POS_OUT + i)
                for m in range(KT):
                    add_squares(l, 1, m)
                post(l, 1, False)
                pre(l, 4)
                ffn(l, 1)
            print("dve chain", n_chain[0])
            assert n_chain[0] == CHAIN["dve"] or not STRICT
            for c, (o, L) in enumerate(CH):
                dve.wait_ge(sem("x_back"), c + 1)
                for n in range(2):
                    g = CP(xtok_s[0:L, c, 512 * n:512 * n + 512], ps[0:L, n, :])
                g.then_inc(sem("x_out_read"), 1)

        @block.gpsimd
        def _(pool):
            dma = pool.dma_start

            def hold(s, v):
                pool.wait_ge(s, v)
                pool.sem_inc(sem("pool_held"), 1)

            pool.sem_inc(sem("layers_stored"), FREE)
            xp, xs = I["x_prompt"], I["x_sample"].rearrange("b t d -> (b t) d")
            dma(stage[0:96, :], I["norm_sandwich"].rearrange("l i (k p) -> (l i k) p", p=P))\
                .then_inc(sem("gain_rows_loaded"), 16)
            dma(xtok_s[:, 0:2, :], xp.rearrange("o (c p) d -> p (o c) d", p=P)).then_inc(sem("x_loaded"), 16)
            dma(xtok_s[0:NS, 2, :], xs).then_inc(sem("x_loaded"), 16)
            gl = sem("gate_params_loaded")
            win = I["w_in"].rearrange("l (k p) n -> p l k n", p=P)
            for n, c0 in enumerate((DT0, GAB0, MIF0 + H, GAB0 + H, MIF0)):
                for l in range(DEPTH):
                    dma(wg2[:, l, :, 4 * n:4 * n + 4], win[:, l, :, c0:c0 + 4]).then_inc(gl, 16)
            for n, v in enumerate(("ssm_dt_bias", "gdn_dt_bias", "mlstm_f_bias", None, "mlstm_i_bias")):
                if v:
                    dma(gb2[:, :, 4 * n:4 * n + 4], I[v].partition_broadcast(P)).then_inc(gl, 16)
            dma(al2[:, :, 0:4], I["ssm_A_log"].partition_broadcast(P)).then_inc(gl, 16)
            dma(al2[:, :, 4:8], I["gdn_A_log"].partition_broadcast(P)).then_inc(gl, 16)
            dma(sd2[:, :, :], I["ssm_D"].partition_broadcast(P)).then_inc(gl, 16)
            dma(mm[:, :, :], I["state_mlstm_m"].rearrange("l b h -> h l b")).then_inc(gl, 16)
            pool.wait_ge(sem("gains_turned"), 1)
            pr = sem("param_rows_loaded")
            for l in range(DEPTH):
                r = 52 * l
                for n, v in enumerate(("ret_norm", "ssm_norm", "gdn_norm", "mlstm_norm")):
                    dma(stage[r + 2 * n:r + 2 * n + 2, :], I[v][l].rearrange("(k p) -> k p", p=P)).then_inc(pr, 16)
                dma(stage[r + 8:r + 12, :], I["ssm_conv_b"][l].rearrange("(k p) -> k p", p=P)).then_inc(pr, 16)
                dma(stage[r + 12:r + 28, :], I["ssm_conv_w"][l].rearrange("j (k p) -> (j k) p", p=P)).then_inc(pr, 16)
                dma(stage[r + 28:r + 52, :], I["gdn_conv_w"][l].rearrange("j (k p) -> (j k) p", p=P)).then_inc(pr, 16)

            def at(name, l):
                return I[name][bass.ds(l, 1)]

            with pool.Fori(0, DEPTH) as l:
                l1 = l + 1
                dma(hist[:, 0:6, :], at("state_gdn_conv", l).rearrange("o b j (k p) -> (o b j) k p", p=P))\
                    .then_inc(sem("hist_loaded"), 16)
                dma(hist[:, 6:10, :], at("state_ssm_conv", l).rearrange("o b j (k p) -> (o b j) k p", p=P))\
                    .then_inc(sem("hist_loaded"), 16)
                def load_states(m):
                    name = {"gdn": "state_gdn", "ret": "state_ret", "ml": "state_mlstm_C", "ssd": "state_ssm"}[m]
                    for b in range(NB):
                        src = at(name, l)[:, b].rearrange("o h d e -> d (o h) e")
                        dst = Snat[:, :, b, :] if m == "ssd" else \
                            SX[m][(b % 2) * HD:(b % 2 + 1) * HD, b // 2, :, 0:HD]
                        dma(dst, src).then_inc(sem("states_loaded_" + m), 16)
                    if m == "ml":
                        for b in range(NB):
                            dma(SX["ml"][(b % 2) * HD:(b % 2 + 1) * HD, b // 2, :, HD:],
                                at("state_mlstm_n", l)[:, b].rearrange("o h d -> d (o h)").unsqueeze(2))\
                                .then_inc(sem("states_loaded_ml"), 16)

                load_states("gdn")
                hold(sem("proj_done"), l1 * NPT)
                pool.memset(kbd, 0.0).then_inc(sem("kbd_clear"), 1)
                for mi, m in enumerate(MIX):
                    if m == "gdn":
                        hold(sem("x_level"), l * 16 + 16)
                    hold(sem("kv_read"), l * 12 + 3 * mi + 3)
                    hold(sem("sadd_done"), l * 16 + 4 * mi + FREE)
                    for s in range(2 if m == "ssd" else H):
                        g = pool.tensor_tensor(KX[:, s], bc(K[0:NS, 2, s * HD:(s + 1) * HD], 1, NB),
                                               bc(C("onehot", NS), 2, HD), ALU.mult)
                    g.then_inc(sem("kx_ready"), 1)
                    pstored = sem("prompt_stored")
                    hold(sem("state_read"), l * 8 + 2 * mi + 2)
                    if m == "ssd":
                        hold(sem("ssd_state_read"), l1)
                        for a in range(2):
                            dma(O["p_ssm"][bass.ds(l, 1), 0].rearrange("o (g a) p n -> a p (o g) n", a=2)[a],
                                fin[:, a, :].rearrange("p (g n) -> p g n", g=2)).then_inc(pstored, 16)
                    else:
                        out = {"gdn": "p_gdn", "ret": "p_ret", "ml": "p_mC"}[m]
                        for a in range(2):
                            dma(O[out][bass.ds(l, 1), 0, 2 * a:2 * a + 2].rearrange("o h d e -> (o h d) e"),
                                S1[:, a, 0:HD]).then_inc(pstored, 16)
                            if m == "ml":
                                dma(O["p_mn"][bass.ds(l, 1), 0, 2 * a:2 * a + 2].rearrange("o h d -> (o h d)").unsqueeze(1),
                                    S1[:, a, HD:]).then_inc(pstored, 16)
                    stored = sem("sample_stored")
                    hold(sem("sadd_read"), l * 16 + 4 * mi + 4)
                    out = {"gdn": "s_gdn", "ret": "s_ret", "ml": "s_mC", "ssd": "s_ssm"}[m]
                    for b in range(NB):
                        dst = O[out][bass.ds(l, 1), b].rearrange("o h d e -> d (o h) e")
                        src = Snat[:, :, b, :] if m == "ssd" else \
                            SX[m][(b % 2) * HD:(b % 2 + 1) * HD, b // 2, :, 0:HD]
                        dma(dst, src).then_inc(sem("ssm_samples_stored") if m == "ssd" else stored, 16)
                        if m == "ml":
                            dma(O["s_mn"][bass.ds(l, 1), b].rearrange("o h d -> d (o h)").unsqueeze(2),
                                SX[m][(b % 2) * HD:(b % 2 + 1) * HD, b // 2, :, HD:]).then_inc(stored, 16)
                    if m == "gdn":
                        hold(sem("mixed_ready"), l * 4 + 1 + FREE)
                        load_states("ssd")
                        hold(stored, l * SSTORES + NB * 16)
                        load_states("ret")
                    if m == "ssd":
                        load_states("ml")
                dma(O["p_mm"][bass.ds(l, 1), 0], mt[P - 1:P, 1, :]).then_inc(stored, 16)
                for b in range(NB):
                    dma(O["s_mm"][bass.ds(l, 1), b], mt[LS * b + LS - 1:LS * b + LS, 2, :]).then_inc(stored, 16)
                hold(sem("last_read"), l1)
                ls = sem("last_stored")
                gc = lastT[:, 0:6, :].rearrange("p c n -> p (c n)")
                sc = lastT[:, 6:10, :].rearrange("p c n -> p (c n)")
                dma(O["p_gdn_conv"][bass.ds(l, 1), 0].rearrange("o j c -> (o j) c"), gc[0:3]).then_inc(ls, 16)
                dma(O["p_ssm_conv"][bass.ds(l, 1), 0].rearrange("o j c -> (o j) c"), sc[0:3]).then_inc(ls, 16)
                dma(O["s_gdn_conv"][bass.ds(l, 1)].rearrange("o b j c -> (o b j) c"), gc[3:27]).then_inc(ls, 16)
                dma(O["s_ssm_conv"][bass.ds(l, 1)].rearrange("o b j c -> (o b j) c"), sc[3:27]).then_inc(ls, 16)
                hold(sem("prompt_stored"), l1 * PSTORES)
                hold(stored, l1 * SSTORES)
                hold(sem("ssm_samples_stored"), l1 * NB * 16)
                pool.wait_ge(ls, l1 * 64)
                pool.sem_inc(sem("layers_stored"), 1)
            yp = O["y_prompt"].rearrange("o (c p) d -> c p (o d)", p=P)
            ys = O["y_sample"].rearrange("b t d -> (b t) d")
            for c in range(3):
                pool.wait_ge(sem("x_out_read"), c + 1)
                dma(yp[c] if c < 2 else ys, xtok_s[0:CH[c][1], c, :]).then_inc(sem("y_stored"), 16)
            pool.wait_ge(sem("y_stored"), 48)


_INS = ["x_prompt", "x_sample", "state_ret", "state_ssm", "state_ssm_conv", "state_gdn", "state_gdn_conv",
        "state_mlstm_C", "state_mlstm_n", "state_mlstm_m", "w_in", "w_out", "norm_sandwich", "ffn_w_gate",
        "ffn_w_up", "ffn_w_down", "ret_norm", "ssm_conv_w", "ssm_conv_b", "ssm_dt_bias", "ssm_A_log", "ssm_D",
        "ssm_norm", "gdn_conv_w", "gdn_dt_bias", "gdn_A_log", "gdn_norm", "mlstm_i_bias", "mlstm_f_bias",
        "mlstm_norm"]
_OUTS = {"y_prompt": (1, SEQ, D), "y_sample": (NB, LS, D)}
for _p, _b in (("p", 1), ("s", NB)):
    _OUTS |= {f"{_p}_ret": (DEPTH, _b, H, HD, HD), f"{_p}_ssm": (DEPTH, _b, H, HD, HD),
              f"{_p}_ssm_conv": (DEPTH, _b, 3, SSM_CH), f"{_p}_gdn": (DEPTH, _b, H, HD, HD),
              f"{_p}_gdn_conv": (DEPTH, _b, 3, GDN_CH), f"{_p}_mC": (DEPTH, _b, H, HD, HD),
              f"{_p}_mn": (DEPTH, _b, H, HD), f"{_p}_mm": (DEPTH, _b, H)}


def kernel(**inputs):
    import concourse.bacc as bacc
    from concourse.bass_utils import run_bass_kernel_spmd

    nc = bacc.Bacc("TRN2", target_bir_lowering=False, num_devices=1)
    arrays, ins, outs = {}, {}, {}
    for name in _INS:
        a = np.ascontiguousarray(inputs[name])
        arrays["in_" + name] = a
        ins[name] = nc.dram_tensor("in_" + name, a.shape, mybir.dt.from_np(a.dtype), kind="ExternalInput").ap()
    table = np.ascontiguousarray(np.concatenate(list(CONST.values()), axis=1))
    arrays["in_const"] = table
    ins["const"] = nc.dram_tensor("in_const", table.shape, F32, kind="ExternalInput").ap()
    for name, shape in _OUTS.items():
        outs[name] = nc.dram_tensor("out_" + name, shape, F32, kind="ExternalOutput").ap()
    trunk_kernel(nc, ins, outs)
    r = run_bass_kernel_spmd(nc, [arrays], core_ids=[0])
    return tuple(r.results[0]["out_" + name] for name in _OUTS)
```

```python
from contextlib import ExitStack

import numpy as np

import concourse.bass as bass
from concourse import mybir

F32 = mybir.dt.float32
F32R = mybir.dt.float32r
ALU = mybir.AluOpType
ACT = mybir.ActivationFunctionType
AX = mybir.AxisListType.X
P = 128

D = 1024
KT = D // P
SEQ = 256
DEPTH = 2
NB, LS = 8, 4
PAST = 2048
NS = NB * LS
T = SEQ + NS
H, HD = 4, 64
GW = 256
FF = 2816
FT = FF // P
RET_IN = 4 * GW
SSM_CH = GW + 4 * HD
GDN_CH = 3 * GW
Z0 = RET_IN
XBC0 = Z0 + GW
DT0 = XBC0 + SSM_CH
GDN0 = DT0 + H
GG0 = GDN0 + GDN_CH
GAB0 = GG0 + GW
ML0 = GAB0 + 2 * H
MIF0 = ML0 + 4 * GW
IN_DIM = MIF0 + 2 * H
EPS = 1e-6
NEG = -1.0e30
HE = HD + 1

CH = [(0, 128), (128, 128), (256, 32)]
GDN_T, SSD_T, RET_T, ML_T = 0, 8, 14, 22
NPT = 30
BLOCKS = ([GDN0 + GW * i for i in range(4)] + [XBC0, XBC0 + GW, Z0] + [GW * i for i in range(4)]
          + [ML0 + GW * i for i in range(4)])
CONV_T = [0, 1, 2, 3, 4, 5, 8, 9, 10, 11]
NC = len(CONV_T)
SILU_T = (6, 7, 12, 13, 20, 21)
MIX = ("gdn", "ret", "ssd", "ml")
OUT_T = {"ret": 0, "ssd": 2, "gdn": 4, "ml": 6}

RING = 4
SLOT = KT * 256
DOWN = (8, 8, 6)
PAIRS = FT // 2
FFN_SLOTS = 2 * PAIRS + 4 * len(DOWN)
N_IN = len(BLOCKS)
POS_FFN = (0, FFN_SLOTS + N_IN + 4)
POS_IN = FFN_SLOTS
POS_OUT = POS_IN + N_IN
N_POS = 2 * FFN_SLOTS + N_IN + 4
POSITIONS = N_POS + 1
assert POSITIONS % RING == 0
PER_SLOT = POSITIONS // RING
H_CREDIT = 2
Y_CREDIT = 4
FREE = 1


def constants():
    i = np.arange(P)
    same = (i[:, None] // LS == i[None, :] // LS) & (i[:, None] < NS) & (i[None, :] < NS)
    lg = np.log(1.0 - np.exp2(-5.0 - np.arange(H)))
    c = {}
    c["ident"] = np.eye(P)
    c["ones"] = np.ones((P, P))
    c["bdones"] = (i[:, None] // HD == i[None, :] // HD)
    rot = np.zeros((P, P))
    for d in range(P):
        if d % HD < HD // 2:
            rot[d + HD // 2, d] = -1
        else:
            rot[d - HD // 2, d] = 1
    c["rot"] = rot
    le = i[:, None] <= i[None, :]
    c["tri"] = le
    c["tri_s"] = le & same
    c["blk_s"] = same
    c["neg"] = np.where(le, 0, NEG)
    c["neg_s"] = np.where(le & same, 0, NEG)[:, :NS]
    lv = np.zeros((P, 7, P))
    for k in range(7):
        s = 1 << k
        t, u = i[:, None], i[None, :]
        lv[:, k] = (t // (2 * s) == u // (2 * s)) & (t % (2 * s) >= s) & (u % (2 * s) < s)
    c["level"] = lv.reshape(P, -1)
    pos = np.concatenate([np.arange(SEQ), PAST + np.arange(NS) % LS]).astype(np.float32)
    inv = np.float32(10000.0) ** (-np.arange(HD // 2, dtype=np.float32) / np.float32(HD // 2))
    ang = (inv[i % (HD // 2)][:, None] * pos[None, :]).astype(np.float32).astype(np.float64)
    c["cos"], c["sin"] = np.cos(ang), np.sin(ang)
    dp = np.zeros((P, H, P))
    ds = np.zeros((P, H, NS))
    for h in range(H):
        dp[:, h] = np.where(le, np.exp(np.where(le, i[None, :] - i[:, None], 0) * lg[h]), 0)
        ds[:, h] = np.where(le & same, np.exp(np.where(le, i[None, :] - i[:, None], 0) * lg[h]), 0)[:, :NS]
    c["ret_d"], c["ret_ds"] = dp.reshape(P, -1), ds.reshape(P, -1)
    inter = np.zeros((P, 2, P + NS))
    for a in range(2):
        for b in range(2):
            inter[b * HD:(b + 1) * HD, a] = np.exp(
                np.concatenate([i + 1, np.arange(NS) % LS + 1]) * lg[2 * a + b])
    c["ret_inter"] = inter.reshape(P, -1)
    tail = np.zeros((P, 3, H))
    tail[:, 0] = tail[:, 1] = np.exp((P - 1 - i)[:, None] * lg)
    tail[:, 2] = np.where(i[:, None] < NS, np.exp((LS - 1 - i % LS)[:, None] * lg), 0)
    c["ret_tail"] = tail.reshape(P, -1)
    c["ret_dec"] = np.exp(P * lg)[2 * np.arange(2)[None, :] + i[:, None] // HD]
    c["ret_decs"] = np.broadcast_to(np.exp(LS * lg), (P, H))
    dup = np.zeros((P, 2, P))
    for b in range(2):
        dup[:, b] = (i[:, None] // HD == b) & (i[:, None] % HD == i[None, :] % HD)
    c["dup"] = dup.reshape(P, -1)
    tok = np.arange(NS)
    bm = (tok[None, None, :] // LS == 2 * np.arange(4)[None, :, None] + i[:, None, None] // HD)
    c["bmask"] = bm.reshape(P, -1)
    c["onehot"] = (i[:, None] // LS == np.arange(NB)[None, :])
    c["blsel"] = ((i[:, None] // LS) % 2 == i[None, :] // HD) & (i[:, None] < NS)
    c["obp"] = (i[:, None] // (2 * LS) == np.arange(4)[None, :])
    c["first"] = (i[:, None] // (2 * LS) == np.arange(4)[None, :]) & (i[:, None] % LS == 0)
    s2 = np.zeros((P, 2, P))
    for h in range(H):
        s2[h, h // 2, (h % 2) * HD:(h % 2 + 1) * HD] = 1
    c["nident"], c["sel2"] = -np.eye(P)[:, :H], s2.reshape(P, -1)
    reset = np.zeros((P, T))
    reset[:, SEQ::LS] = NEG
    c["reset"] = reset
    sign = np.ones((P, 5, H))
    sign[:, 2:4] = -1
    c["sign"] = sign.reshape(P, -1)
    return {k: np.ascontiguousarray(v, dtype=np.float32) for k, v in c.items()}


CONST = constants()
CONST_AT, _at = {}, 0
for _n, _v in CONST.items():
    CONST_AT[_n] = (_at, _v.shape[1])
    _at += _v.shape[1]
CONST_W = _at

CHAIN = {"dve": 105, "act": 13}
PS_BEFORE = {"gdn": 0, "ret": 32, "ssd": 64, "ml": 96}
PSTORES = 96 + 64
SSTORES = 16 * (4 * NB + 2)


def trunk_kernel(nc, I, O):
    ctx = ExitStack()
    with ctx:
        named = {}

        def sb(name, shape):
            return ctx.enter_context(nc.sbuf_tensor(name, shape, F32))

        def sb2(name, shape):
            offset = (nc.sbuf_base + 31) // 32 * 32
            return sb(name, shape), nc.alloc_sbuf_tensor_at(name + "_r", shape, F32R, offset=offset)

        def sem(name):
            if name not in named:
                named[name] = ctx.enter_context(nc.semaphore(name))
            return named[name]

        cst = sb("cst", [P, CONST_W])
        x = sb("x", [P, KT, T])
        hdn = sb("hdn", [P, KT, T])
        big, bigR = sb2("big", [P, NPT, T])
        y, yR = sb2("y", [P, KT, T])
        ring, ringR = sb2("ring", [P, RING, SLOT])
        rrow = sb("rrow", [P, T])
        lnr = sb("lnr", [P, T])
        ssum = sb("ssum", [P, T])
        sq = sb("sq", [P, 2, T])
        sg = sb("sg", [P, 2, T])
        gn = sb("gn", [P, DEPTH, 6, KT])
        p2 = sb("p2", [P, DEPTH, 52])
        gcol = sb("gcol", [P, 6, KT])
        ghalf = sb("ghalf", [P, 6, KT])
        pcol = sb("pcol", [P, 52])
        taps = sb("taps", [P, NC, 4])
        cbias = sb("cbias", [P, NC])
        wg2 = sb("wg2", [P, DEPTH, KT, 20])
        wgf, wgfR = sb2("wg", [P, KT * 20 + P - 20])
        wghf = sb("wgh", [P, KT * 20 + P - 20])
        wg, wgR, wgh = (v[:, 0:KT * 20].rearrange("p (k n) -> p k n", k=KT) for v in (wgf, wgfR, wghf))
        gb2 = sb("gb2", [P, DEPTH, 20])
        al2 = sb("al2", [P, DEPTH, 12])
        sd2 = sb("sd2", [P, DEPTH, H])
        gbias = sb("gbias", [P, 20])
        alog = sb("alog", [P, 12])
        sD = sb("sD", [P, H])
        epsc = sb("epsc", [P, 1])
        stage = sb("stage", [104, P])
        gain_rows = rrow[0:96, 0:P]
        lastT = sb("lastT", [27, NC, P])
        hist = lastT[0:NB * 3]
        arena, arenaR = sb2("arena", [P, NC * (3 + SEQ) + NC * NB * (3 + LS) + 3 * H * P + 3 * GW + 3 * H * HE + 2 * (P + NS)])
        at_ = [0]

        def carve(*shape):
            n = int(np.prod(shape))
            v = arena[:, at_[0]:at_[0] + n]
            at_[0] += n
            names = "abcd"[:len(shape)]
            return v.rearrange(f"p ({' '.join(names)}) -> p {' '.join(names)}", **dict(zip(names, shape)))

        low, lowR = (v[:, 0:FT * T].rearrange("p (k t) -> p k t", k=FT) for v in (arena, arenaR))
        xP = carve(NC, 3 + SEQ)
        xS = carve(NC, NB, 3 + LS)
        DT = carve(3, H, P)
        K = carve(3, GW)
        VW = carve(3, H, HE)
        ki = carve(2, P + NS)
        last = sb("last", [P, NC, 27])
        U = sb("U", [P, 3, 20])
        AB = sb("AB", [P, 3, 12])
        SP = sb("SP", [P, 3, 12])
        G = sb("G", [P, 3, 12])
        beta = sb("beta", [P, 3, H])
        cum = sb("cum", [P, 3, 12])
        wexp = sb("wexp", [P, 3, 12])
        onfin = sb("onfin", [P, 3 * GW + 2 * P])
        on = onfin[:, 0:3 * GW].rearrange("p (c n) -> p c n", c=3)
        fin = onfin[0:HD, 3 * GW:].rearrange("p (a n) -> p a n", a=2)
        Gb = onfin[:, :].rearrange("p (c s d) -> p c s d", c=2, s=8)
        er = sb("er", [P, 6, P + NS])
        decP = sb("decP", [P, 6])
        Gx = sb("Gx", [NS, 64])
        decS = sb("decS", [P, 64])
        aT = sb("aT", [P, 3, H])
        aH = sb("aH", [H, T])
        mH = sb("mH", [H, T])
        mL = sb("mL", [H, T])
        mPv = sb("mPv", [H, T])
        eI = aH
        eD = mPv
        mm = sb("mm", [H, DEPTH, NB])
        mmc = sb("mmc", [H, NB])
        mTok = sb("mTok", [P, 3, 3, H])
        mt = sb("mt", [P, 3, H])
        emt = sb("emt", [P, 3, H])
        qbd = sb("qbd", [P, 2, 2, T])
        qi = sb("qi", [P, 2, P + NS])
        V = sb("V", [P, 3, H, HE])
        ctmp = K[:, :, :].rearrange("p c n -> p (c n)")[:, 0:NC * NS].rearrange("p (c b t) -> p c b t", c=NC, b=NB)
        Bb = VW[:, :, :, :].rearrange("p c h e -> p (c h e)")[:, 0:3 * GW]\
            .rearrange("p (c h d) -> p c h d", c=3, h=H)
        xPf = xP[:, :, :].rearrange("p c n -> p (c n)")
        PT = xPf[:, 0:3 * H * P].rearrange("p (c h n) -> p c h n", c=3, h=H)
        DTf = DT[:, :, :, :].rearrange("p c h n -> p (c h n)")
        Dx = xPf[:, 3 * H * P:3 * H * P + 3 * GW].rearrange("p (c h n) -> p c h n", c=3, h=H)
        xtok_s = big[:, 0:11, :].rearrange("p k t -> p (k t)")[:, 0:3 * D].rearrange("p (c n) -> p c n", c=3)
        Sbd = sb("Sbd", [P, 2, 2, HE])
        S1 = sb("S1", [P, 2, HE])
        SX = [sb(f"Sx{n}", [P, 4, H, HE]) for n in range(2)]
        SX = {m: SX[n % 2] for n, m in enumerate(MIX)}
        whigh, whighR = sb2("whigh", [P, 2, SLOT])
        snat = whigh[:, 1, :]
        Snat = snat[0:HD, :].rearrange("p (h b n) -> p h b n", h=H, b=NB)
        kbd = snat[:, 0:4 * T].rearrange("p (a b t) -> p a b t", a=2, b=2)
        KQX = snat[:, 4 * T:4 * T + 16 * NS].rearrange("p (h b n) -> p h b n", h=H, b=4)
        atm = whigh[:, 0, :]
        AT = atm[:, 0:2 * H * P].rearrange("p (c h n) -> p c h n", c=2, h=H)
        Tm = atm[:, 2 * H * P:].rearrange("p (c h n) -> p c h n", c=2, h=H)
        KX = atm[0:NS, :].rearrange("p (h b n) -> p h b n", h=H, b=NB)
        QX = xS[:, :, :, :].rearrange("p c b j -> p (c b j)")[:, 0:H * 4 * NS]\
            .rearrange("p (h b n) -> p h b n", h=H, b=4)
        osq = DTf[:, 0:3 * GW].rearrange("p (c n) -> p c n", c=3)
        C4 = sg[:, :, :].rearrange("p a t -> p (a t)")[:, 0:NC * NS].rearrange("p (c b t) -> p c b t", c=NC, b=NB)
        sml = sb("sml", [P, 4, 3 * H])
        tiny = sq
        yflat = y[:, :, :].rearrange("p k t -> p (k t)")
        X = yflat[:, 0:8 * P].rearrange("p (s n) -> p s n", n=P)
        XT = yflat[:, 8 * P:16 * P].rearrange("p (c h n) -> p c h n", c=2, h=H)
        Xs, XTs = (yflat[0:NS, (16 + n) * P:(17 + n) * P].rearrange("p (h n) -> p h n", h=H) for n in range(2))
        ATs = sb("ATs", [NS, H, NS])
        Tms = sb("Tms", [NS, H, NS])
        ps = ctx.enter_context(nc.psum_tensor("ps", [P, 8, 512], F32))

        def C(name, rows=P):
            at, w = CONST_AT[name]
            return cst[0:rows, at:at + w]

        ident, ones, bdones = C("ident"), C("ones"), C("bdones")
        level = C("level").rearrange("p (k n) -> p k n", k=7)
        retD = C("ret_d").rearrange("p (h n) -> p h n", h=H)
        retDs = C("ret_ds").rearrange("p (h n) -> p h n", h=H)
        retI = C("ret_inter").rearrange("p (a n) -> p a n", a=2)
        tail = C("ret_tail").rearrange("p (c h) -> p c h", c=3)
        dup = C("dup").rearrange("p (b n) -> p b n", b=2)
        bmask = C("bmask").rearrange("p (b n) -> p b n", b=4)
        sel2 = C("sel2").rearrange("p (a n) -> p a n", a=2)
        sign = C("sign")

        def B(bank, *shape, rows=P, off=0):
            n = int(np.prod(shape))
            v = ps[0:rows, bank, off:off + n]
            if len(shape) == 2:
                return v.rearrange("p (a b) -> p a b", a=shape[0])
            if len(shape) == 3:
                return v.rearrange("p (a b c) -> p a b c", a=shape[0], b=shape[1])
            return v

        def bc(ap, dim, n):
            a = ap.unsqueeze(dim)
            s = list(a.shape)
            s[dim] = n
            return a.broadcast_to(s)

        def slots(ap, m):
            if m == "ssd":
                return ap.rearrange("p (b a) n -> p a b n", a=2)
            return ap.rearrange("p (a b) n -> p a b n", a=2)

        def slots1(ap, m):
            if m == "ssd":
                return ap.rearrange("p (b a) -> p a b", a=2)
            return ap.rearrange("p (a b) -> p a b", a=2)

        def head(m, a, b):
            return 2 * b + a if m == "ssd" else 2 * a + b

        QT = {"gdn": 0, "ssd": 11, "ret": 14, "ml": 22}
        KTL = {"gdn": 2, "ssd": 10, "ret": 16, "ml": 24}
        VTL = {"gdn": 4, "ssd": 8, "ret": 18, "ml": 26}
        GATE = {"gdn": 6, "ssd": 12, "ret": 20, "ml": 28}
        DC = {"ssd": 0, "gdn": 4, "ml": 8}
        HW = {m: (HE if m == "ml" else HD) for m in MIX}
        NORM = {"ret": 0, "ssd": 2, "gdn": 4, "ml": 6}
        OUTB = {"gdn": (1, 4), "ssd": (5, 6), "ret": (5, 6), "ml": (5, 6)}

        def LB(kind, c, L):
            if c == 2:
                return B(6, H, NS, rows=NS, off=P * kind)
            return B(((0, 1), (2, 5), (7, 4))[kind][c], H, P)

        w_in_s = [sem(f"weights_loaded_{s}") for s in range(RING)]

        def gate_used(l, f, pair):
            return sem("gate_done"), l * 2 * FT + f * FT + pair * 2 + 2

        def up_used(l, f, pair):
            return sem("up_done"), l * 2 * FT + f * FT + pair * 2 + 2

        def used(l, pos):
            for f in range(2):
                n = pos - POS_FFN[f]
                if 0 <= n < 2 * PAIRS:
                    return (up_used if n % 2 else gate_used)(l, f, n // 2)
                if 2 * PAIRS <= n < FFN_SLOTS:
                    mp, part = divmod(n - 2 * PAIRS, 3)
                    if part < 2:
                        return sem("down_part_done"), l * 16 + f * 8 + 2 * mp + part + 1
                    return sem("post_product_done"), l * 24 + 16 * f + 2 * mp + 2
            if pos < POS_OUT:
                return sem("proj_done"), l * NPT + 2 * (pos - POS_IN) + 2
            return sem("post_product_done"), l * 24 + 8 + 2 * (pos - POS_OUT) + 2

        def ring_pos(l, pos):
            s, i = pos % RING, pos // RING
            per = PER_SLOT - (1 if s == (POSITIONS - 1) % RING else 0)
            return s, (l * per + i + 1) * 16

        ctx.enter_context(nc.allow_non_contiguous_dma(reason="a few small states with heads or features on partitions"))
        block = ctx.enter_context(nc.Block())

        @block.sync
        def _(sp):
            def hold(s, v):
                sp.wait_ge(s, v)
                sp.sem_inc(sem("sp_held"), 1)

            def load(l, pos, rows, src, free=None):
                if free is None:
                    free = used(l, pos - RING) if pos >= RING else (sem("y_done"), l * 24 + Y_CREDIT)
                hold(*free)
                s = pos % RING
                sp.dma_start(ring[:, s, 0:rows * 256].rearrange("p (k n) -> p k n", k=rows),
                             src).then_inc(w_in_s[s], 16)

            def ffn(l, f):
                wgd = I["ffn_w_gate"][bass.ds(l, 1), f].rearrange("o (k p) n -> p (o k) n", p=P)
                wud = I["ffn_w_up"][bass.ds(l, 1), f].rearrange("o (k p) n -> p (o k) n", p=P)
                wdd = I["ffn_w_down"][bass.ds(l, 1), f].rearrange("o (k p) n -> p (o k) n", p=P)
                pos = POS_FFN[f]
                for t in range(2):
                    for n, w in enumerate((wgd, wud)):
                        load(l, pos + 2 * t + n, KT, w[:, :, 256 * t:256 * t + 256])
                with sp.Fori(1, PAIRS // 2) as j:
                    for t in range(2):
                        for n, (w, before) in enumerate(((wgd, gate_used), (wud, up_used))):
                            load(l, pos + 2 * t + n, KT, w[:, :, bass.ds(j * 512 + 256 * t, 256)],
                                 before(l, f, j * 2 + (t - 2)))
                pos += 4 * (PAIRS // 2)
                for n, w in enumerate((wgd, wud)):
                    load(l, pos + n, KT, w[:, :, FF - 256:FF])
                pos += 2
                for mp in range(4):
                    for part, n in enumerate(DOWN):
                        load(l, pos + 3 * mp + part, n, wdd[:, 8 * part:8 * part + n, 256 * mp:256 * mp + 256])

            sp.wait_ge(sem("x_loaded"), 32)
            with sp.Fori(0, DEPTH) as l:
                ffn(l, 0)
                win = I["w_in"][bass.ds(l, 1)].rearrange("o (k p) n -> p (o k) n", p=P)
                for i, c0 in enumerate(BLOCKS):
                    load(l, POS_IN + i, KT, win[:, :, c0:c0 + 256])
                wo = I["w_out"][bass.ds(l, 1)].rearrange("o (k p) n -> p (o k) n", p=P)
                for i in range(4):
                    load(l, POS_OUT + i, KT, wo[:, :, 256 * i:256 * i + 256])
                ffn(l, 1)

        @block.tensor
        def _(pe):
            def mm(out, lhsT, rhs, start=True, stop=True, **k):
                return pe.matmul(out, lhsT, rhs, start=start, stop=stop, **k)

            def tr(out, in_):
                return pe.transpose(out, in_, ident[0:in_.shape[0], 0:in_.shape[0]])

            def hold(s, v):
                pe.wait_ge(s, v)
                pe.sem_inc(sem("pe_held"), 1)

            def slot_ready(l, pos, j=0):
                hold(sem("weights_split"), l * N_POS + pos + 1 + j * 4)

            hdnR = hdn[:, :, :].bitcast(F32R)

            def product(out, pos, t, rows, high, low_, start=True, stop=True, ready=None):
                wl, wh = ringR[:, pos % RING], whighR[:, pos % 2]
                cols = [slice(k * 256 + t * P, k * 256 + t * P + P) for k in range(rows)]
                for k in range(rows):
                    if ready is not None:
                        hold(sem("hdn_high"), ready[0] + k + 1)
                    mm(out, wh[:, cols[k]], high[:, k, :], start and k == 0, False)
                for k in range(rows):
                    mm(out, wl[:, cols[k]], high[:, k, :], False, False)
                for k in range(rows):
                    if ready is not None and k % 4 == 0:
                        hold(sem("hdn_low"), ready[1] + k // 4 + 1)
                    g = mm(out, wh[:, cols[k]], low_[:, k, :], False, stop and k == rows - 1)
                return g

            pe.sem_inc(sem("sadd_done"), FREE)
            pe.wait_ge(sem("const_loaded"), 16)
            pe.wait_ge(sem("x_loaded"), 32)
            for k in range(KT):
                for c, (o, L) in enumerate(CH):
                    g = tr(ps[:, k, o:o + L], xtok_s[0:L, c, k * P:(k + 1) * P])
                g.then_inc(sem("x_turned"), 1)
            pe.wait_ge(sem("x_done"), 2)
            pe.wait_ge(sem("gain_rows_loaded"), 16)
            tr(B(0, 96), gain_rows).then_inc(sem("gains_turned"), 1)
            pe.wait_ge(sem("param_rows_loaded"), 14 * 16)
            tr(B(1, 104), stage[0:104, :]).then_inc(sem("params_turned"), 1)
            pe.wait_ge(sem("x_done"), KT)

            def ffn(l, f):
                pre, post = (0, 0) if f == 0 else (2, 2)
                ready = [(l * 24 + pre * 8, l * 6 + pre * 2)]

                def pair(pos, tile0, j):
                    for n, done in enumerate(("gate_done", "up_done")):
                        slot_ready(l, pos + n, j)
                        for t in range(2):
                            hold(sem("h_done" if n else "silu_done"), tile0 + t + 1)
                            product(ps[:, 2 * t + n, 0:T], pos + n, t, KT, hdnR, yR,
                                    ready=ready.pop() if ready else None)\
                                .then_inc(sem(done), 1)

                base = POS_FFN[f]
                with pe.Fori(0, PAIRS // 2) as j:
                    for t in range(2):
                        pair(base + 2 * t, l * 44 + f * 22 + j * 4 + 2 * t, j)
                pair(base + 4 * (PAIRS // 2), l * 44 + f * 22 + 20, 0)
                pos = base + 2 * PAIRS
                hold(sem("h_done"), l * 44 + f * 22 + 22 + H_CREDIT)
                for mp in range(4):
                    for part, nk in enumerate(DOWN):
                        slot_ready(l, pos + 3 * mp + part)
                        ks = slice(8 * part, 8 * part + nk)
                        for t in range(2):
                            m = 2 * mp + t
                            if part == 0:
                                hold(sem("y_done"), l * 24 + post * 8 + m + 1)
                            d = product(ps[:, m % 4, 0:T], pos + 3 * mp + part, t, nk, bigR[:, ks], lowR[:, ks],
                                        part == 0, part == 2)
                            if part == 2:
                                d.then_inc(sem("post_product_done"), 1)
                        if part < 2:
                            d.then_inc(sem("down_part_done"), 1)

            def norm_post(l, post):
                pe.wait_ge(sem("squares_added"), l * 24 + post * 8 + 8)
                mm(ps[:, 4, 0:T], ones, ssum[:, :]).then_inc(sem("norm_sum"), 1)

            def norm_pre(l, pre):
                for k in range(KT):
                    pe.wait_ge(sem("x_squared"), l * 24 + pre * 8 + k + 1)
                    n = mm(ps[:, 4, 0:T], ones, y[:, k, :], k == 0, k == KT - 1)
                n.then_inc(sem("norm_sum"), 1)

            def mixers(l):
                l1 = l + 1
                def rotated():
                    hold(sem("hist_placed"), l1)
                    hold(sem("proj_read"), l * NPT + RET_T + 4)
                    for n in range(4):
                        g = mm(ps[:, 4 + n, 0:T], C("rot"), big[:, RET_T + n, :])
                    g.then_inc(sem("rotated"), 1)

                def cumulated():
                    hold(sem("rotated_read"), l1)
                    hold(sem("decays_ready"), l1)
                    cb, tb = B(4, 3, 12), B(7, 3, 12)
                    mm(cb[:, 0, :], C("tri"), G[:, 0, :])
                    mm(cb[:, 1, :], C("tri"), G[:, 1, :], True, False)
                    mm(cb[:, 1, 8:12], ones, G[:, 0, 8:12], False, True)
                    mm(cb[:, 2, :], C("tri_s"), G[:, 2, :])
                    mm(tb[:, 0, :], ones, G[:, 0, :])
                    mm(tb[:, 1, :], ones, G[:, 1, :])
                    mm(tb[:, 2, :], C("blk_s"), G[:, 2, :]).then_inc(sem("cum_done"), 1)

                def decay_rows():
                    hold(sem("decays_spread"), l1)
                    for n in range(4):
                        e = ps[:, 5 + n // 2, 160 * (n % 2):160 * (n % 2) + 160]
                        mm(e[:, 0:P], Gb[:, 0, 2 * n:2 * n + 2, :].rearrange("p s d -> p (s d)"), C("tri"))
                        mm(e[:, P:], Gb[:, 1, 2 * n:2 * n + 2, :].rearrange("p s d -> p (s d)"),
                           C("tri_s")[:, 0:NS])
                        mm(ps[:, 5, 320 + n:321 + n], Gb[:, 0, 2 * n:2 * n + 2, :].rearrange("p s d -> p (s d)"),
                           ones[:, 0:1])
                    mm(ps[:, 6, 320:336], C("blsel", NS), Gx[:, 0:16])
                    mm(ps[:, 6, 336:368], ones[0:NS, :], Gx[:, 16:48]).then_inc(sem("erow_done"), 1)

                def turned():
                    hold(sem("a_ready"), l1)
                    for c, (o, L) in enumerate(CH):
                        g = tr(ps[0:H, 4, o:o + L], aT[0:L, c, :])
                    g.then_inc(sem("a_turned"), 1)

                def qk_norms():
                    hold(sem("qk_squared"), l1)
                    hold(sem("er_read"), l1)
                    hold(sem("m_rows_arg"), l1)
                    for n in range(4):
                        g = mm(ps[:, 4 + n, 0:T], bdones, DTf[:, n * T:(n + 1) * T])
                    g.then_inc(sem("qk_norms_done"), 1)

                def gates_back():
                    hold(sem("gates_copied"), l1)
                    for c, (o, L) in enumerate(CH):
                        g = tr(ps[0:L, 4, 20 * c:20 * c + 20], lnr[0:20, o:o + L])
                    g.then_inc(sem("gates_turned"), 1)

                during = {4: gates_back, 17: rotated, 21: cumulated, 23: decay_rows, 25: turned, 27: qk_norms}
                for i in range(NPT):
                    if i >= 4:
                        hold(sem("proj_read"), l * NPT + i - 3)
                    if i % 2 == 0:
                        slot_ready(l, POS_IN + i // 2)
                    product(ps[:, i % 4, 0:T], POS_IN + i // 2, i % 2, KT, hdnR, yR,
                            ready=None if i else (l * 24 + 8, l * 6 + 2)).then_inc(sem("proj_done"), 1)
                    if i == 1:
                        hold(sem("layer_params"), l1)
                        gate_parts = ((wghf[:, :].bitcast(F32R), hdnR), (wgfR, hdnR), (wghf[:, :].bitcast(F32R), yR))
                        for n, (w, a) in enumerate(gate_parts):
                            for k in range(KT):
                                g = mm(ps[:, 5, 0:T], w[:, k * 20:k * 20 + P], a[:, k, :],
                                       n == 0 and k == 0, n == 2 and k == KT - 1)
                        g.then_inc(sem("gates_done"), 1)
                        hold(sem("hist_loaded"), l1 * 32)
                        for t in range(NC):
                            g = tr(B(6, NC, NB * 3)[:, t, :], hist[:, t, :])
                        g.then_inc(sem("hist_turned"), 1)
                    if i in during:
                        during[i]()
                hold(sem("qk_norms_read"), l1)
                hold(sem("beta_spread"), l1)
                hold(sem("m_rows_ready"), l1)
                for n, row in enumerate((mH, mL, eD)):
                    for c, (o, L) in enumerate(CH):
                        g = tr(ps[0:L, 7, 300 + (3 * n + c) * H:300 + (3 * n + c) * H + H], row[:, o:o + L])
                for a in range(2):
                    mm(ps[:, 6, 160 * a:160 * a + 160], sel2[0:H, a, :], eI[:, P:T])
                for a in range(2):
                    g = mm(ps[:, 6, 320 + a:321 + a], sel2[0:H, a, :], eD[:, P:P + 1])
                g.then_inc(sem("m_tok_done"), 1)
                for a in range(2):
                    for c, (o, L) in enumerate(CH):
                        g = mm(ps[:, 4 + a, o:o + L],
                               Bb[0:L, c, 2 * a:2 * a + 2, :].rearrange("p h d -> p (h d)"), ident[0:L, 0:L])
                g.then_inc(sem("beta_rows_done"), 1)
                hold(sem("ml_decay_spread"), l1)
                mm(ps[:, 7, 64:80], C("blsel", NS), Gx[:, 48:64]).then_inc(sem("ml_decS_done"), 1)
                hold(sem("proj_read"), l * NPT + NPT)
                for mi, m in enumerate(MIX):
                    mixer(l, l1, mi, m)
                hold(sem("mixed_ready"), l * 4 + 4 + FREE)
                for t in range(NC):
                    g = tr(ps[0:27, 4 + t // 4, (t % 4) * P:(t % 4 + 1) * P], last[:, t, :])
                g.then_inc(sem("last_turned"), 1)

            def mixer(l, l1, mi, m):
                w = HW[m]
                Sx = SX[m]
                hold(sem("mixed_ready"), l * 4 + mi + FREE)
                if m == "gdn":
                    hold(sem("qk_ready"), l * 4 + mi + 1)
                for c, (o, L) in enumerate(CH):
                    if c == 2:
                        hold(sem("v_read"), l * 12 + 3 * mi + 1)
                        hold(sem("k_read"), l * 12 + 3 * mi + 1)
                    kts = (KTL[m],) if m == "ssd" else (KTL[m], KTL[m] + 1)
                    for n, t in enumerate(kts):
                        tr(ps[0:L, (4, 7)[c % 2], n * P:(n + 1) * P], big[:, t, o:o + L])
                    for n in range(2):
                        g = tr(ps[0:L, (0, 2)[c % 2], n * P:(n + 1) * P], big[:, VTL[m] + n, o:o + L])
                    g.then_inc(sem("kv_turned"), 1)
                if m != "ret":
                    for c, (o, L) in enumerate(CH):
                        if c == 2:
                            hold(sem("decay_arg"), l * 9 + 3 * [0, 0, 1, 2][mi] + 1)
                        for s in range(H):
                            out = ps[0:L, (1, 5)[c % 2], s * L:(s + 1) * L]
                            if m == "ml":
                                g = mm(out, C("nident", H)[:, s:s + 1].broadcast_to([H, L]), mH[:, o:o + L])
                            else:
                                h = head(m, s // 2, s % 2)
                                tri = C("tri") if c < 2 else C("tri_s")[0:NS, 0:NS]
                                g = mm(out, G[0:L, c, DC[m] + h:DC[m] + h + 1].broadcast_to([L, L]), tri)
                        g.then_inc(sem("decay_rows"), 1)
                hold(sem("v_read"), l * 12 + 3 * mi + 3)
                hold(sem("k_read"), l * 12 + 3 * mi + 3)
                hold(sem("qk_ready"), l * 4 + mi + 1)
                for s in range(H):
                    g = mm(ps[:, 3, s * NS:(s + 1) * NS], dup[:, s % 2, :], qi[:, s // 2, P:])
                if m == "gdn":
                    for s in range(H):
                        g = mm(ps[:, 3, P + s * NS:P + (s + 1) * NS], dup[:, s % 2, :], ki[:, s // 2, P:])
                g.then_inc(sem("dup_done"), 1)
                if m == "ssd":
                    states_in(l1, m)
                    hold(sem("decay_arg"), l * 9 + 3 + 2)
                    for bp in range(4):
                        if bp >= 2:
                            hold(sem("snat_read"), l * 4 + bp - 1)
                        for s in range(H):
                            h = head(m, s // 2, s % 2)
                            g = tr(ps[:, 5 + bp % 2, s * HD:(s + 1) * HD],
                                   Snat[:, h, 2 * bp:2 * bp + 2, :].rearrange("p b n -> p (b n)"))
                        g.then_inc(sem("snat_turned"), 1)
                if m == "gdn":
                    gdn_solve(l, l1)
                hold(sem("qbd_ready"), l * 4 + mi + 1)

                def scores(c):
                    o, L = CH[c]
                    bank = c % 2
                    if c == 1 and m != "ret":
                        hold(sem("decay_arg"), l * 9 + 3 * [0, 0, 1, 2][mi] + 3)
                    if c == 2:
                        hold(sem("probs_ready"), l * 12 + 3 * mi + 1)
                    if m == "ssd":
                        g = mm(ps[0:L, bank, 0:2 * L], big[:, KTL[m], o:o + L], qbd[:, 0, :, o:o + L])
                    else:
                        for a in range(2):
                            g = mm(ps[0:L, bank, 2 * L * a:2 * L * (a + 1)], big[:, KTL[m] + a, o:o + L],
                                   qbd[:, a, :, o:o + L])
                    g.then_inc(sem("scores_done"), 1)

                scores(0)
                scores(1)
                for c, (o, L) in enumerate(CH):
                    if m == "gdn":
                        if c:
                            if c == 1:
                                for a in range(2):
                                    g = mm(ps[:, 5, a * P:(a + 1) * P], ki[:, a, 0:P],
                                           Sbd[:, a, :, 0:HD])
                            else:
                                states_in(l1, m)
                                for s in range(H):
                                    for bp in range(4):
                                        g = mm(ps[0:NS, 5, s * HD:(s + 1) * HD], KQX[:, s, bp, :],
                                               Sx[:, bp, s, 0:HD], bp == 0, bp == 3)
                            g.then_inc(sem("ks_done"), 1)
                        hold(sem("resid_ready"), l * 3 + c + 1)
                        for s in range(H):
                            xt = XT[:, c, s, :] if c < 2 else XTs[:, s, :]
                            g = mm(ps[0:L, 6, s * HD:(s + 1) * HD], xt, VW[0:L, c, s, 0:HD])
                        g.then_inc(sem("vnew_done"), 1)
                    hold(sem("probs_ready"), l * 12 + 3 * mi + c + 1)
                    hold(sem("values_ready"), l * 12 + 3 * mi + c + 1)
                    if c or mi:
                        hold(sem("raw_ready"), l * 12 + 3 * mi + c)
                    if c == 2:
                        states_in(l1, m)
                        hold(sem("qx_ready"), l * 4 + mi + 1)
                    for s in range(H):
                        out = ps[0:L, 2, s * w:(s + 1) * w]
                        if c == 1:
                            b = s % 2
                            mm(out, qi[:, s // 2, 0:P], Sbd[:, s // 2, b, 0:w], True, False)
                        if c == 2:
                            for bp in range(4):
                                mm(out, QX[:, s, bp, :], Sx[:, bp, s, 0:w], bp == 0, False)
                        g = mm(out, PT[0:L, c, s, 0:L], V[0:L, c, s, 0:w], c == 0, True)
                    g.then_inc(sem("out_done"), 1)
                    if c == 0:
                        scores(2)
                    hold(sem("vw_ready"), l * 12 + 3 * mi + c + 1)
                    if c < 2:
                        if c:
                            hold(sem("state_read"), l * 8 + 2 * mi + c)
                        for s in range(H):
                            a, b = s // 2, s % 2
                            kc = b if m == "ssd" else s
                            g = mm(ps[b * HD:(b + 1) * HD, 7, a * w:(a + 1) * w],
                                   K[:, c, kc * HD:(kc + 1) * HD], VW[:, c, s, 0:w])
                        g.then_inc(sem("state_add"), 1)
                        if c == 0:
                            hold(sem("state_read"), l * 8 + 2 * mi + 1)
                    else:
                        hold(sem("kx_ready"), l * 4 + mi + 1)
                        hold(sem("state_read"), l * 8 + 2 * mi + 2)
                        for n in range(4):
                            if n >= 2:
                                hold(sem("sadd_read"), l * 16 + 4 * mi + n - 1)
                            bank = (3, 7)[n % 2]
                            if m == "ssd":
                                g = mm(ps[0:HD, bank, :], VW[0:NS, 2, n, 0:HD],
                                       KX[:, n % 2, :, :].rearrange("p b n -> p (b n)"))
                            else:
                                for s in range(H):
                                    g = mm(ps[:, bank, s * w:(s + 1) * w],
                                           KX[:, s, 2 * n:2 * n + 2, :].rearrange("p b d -> p (b d)"),
                                           VW[0:NS, 2, s, 0:w])
                            g.then_inc(sem("sadd_done"), 1)
                if m == "ssd":
                    for a in range(2):
                        g = tr(ps[0:HD, 4, a * P:(a + 1) * P], S1[:, a, 0:HD])
                    g.then_inc(sem("ssd_state_turned"), 1)
                if m == "ssd":
                    hold(sem("raw_ready"), l * 12 + 3 * mi + 3)
                else:
                    hold(sem("on_ready"), l * 3 + [0, 1, 0, 2][mi] + 1)
                for c, (o, L) in enumerate(CH):
                    for n in range(2):
                        g = tr(outT(m, n)[:, o:o + L], on[0:L, c, n * P:(n + 1) * P])
                g.then_inc(sem("on_turned"), 1)
                if m == "ssd":
                    hold(sem("ssd_squared"), l1)
                    for n in range(2):
                        g = mm(ps[:, 0, 0:T], ones, tiny[:, n, :], n == 0, n == 1)
                    g.then_inc(sem("ssd_sum"), 1)

            def states_in(l1, m):
                hold(sem("states_loaded_" + m), l1 * {"ml": 256, "ssd": 64}.get(m, 128))

            def outT(m, n):
                return ps[:, OUTB[m][n], :]

            def gdn_solve(l, l1):
                hold(sem("kbd_ready"), l1)
                for c, (o, L) in enumerate(CH):
                    if c:
                        hold(sem("at_ready"), l * 3 + c)
                    for a in range(2):
                        g = mm(ps[0:L, 0, 2 * L * a:2 * L * (a + 1)], big[:, KTL["gdn"] + a, o:o + L],
                               kbd[:, a, :, o:o + L])
                    g.then_inc(sem("gram_done"), 1)
                hold(sem("at_ready"), l * 3 + 3)
                for k in range(7):
                    cs = (0, 1, 2) if k < 2 else (0, 1)
                    for c in cs:
                        L = CH[c][1]
                        n = k * 3 + c if k < 2 else 6 + (k - 2) * 2 + c
                        if k:
                            hold(sem("x_level"), l * 16 + ([0, 3, 6, 8, 10, 12, 14][k - 1]) + c + 1)
                        for s in range(H):
                            at = AT[:, c, s, :] if c < 2 else ATs[:, s, :]
                            xx = X[:, 4 * c + s, :] if c < 2 else Xs[:, s, :]
                            g = mm(LB(0, c, L)[:, s, :], at, xx)
                        g.then_inc(sem("level_t"), 1)
                    for c in cs:
                        L = CH[c][1]
                        hold(sem("t_masked"), l * 16 + [0, 3, 6, 8, 10, 12, 14][k] + c + 1)
                        for s in range(H):
                            xt = XT[:, c, s, :] if c < 2 else XTs[:, s, :]
                            tm = Tm[:, c, s, :] if c < 2 else Tms[:, s, :]
                            mm(LB(1, c, L)[:, s, :], xt, tm)
                            g = mm(LB(2, c, L)[:, s, :], tm, xt)
                        g.then_inc(sem("level_y"), 1)
                hold(sem("x_level"), l * 16 + 16)

            with pe.Fori(0, DEPTH) as l:
                norm_pre(l, 0)
                ffn(l, 0)
                norm_post(l, 0)
                norm_pre(l, 1)
                mixers(l)
                hold(sem("last_read"), l + 1)
                for i in range(4):
                    slot_ready(l, POS_OUT + i)
                    for t in range(2):
                        m = 2 * i + t
                        hold(sem("y_done"), l * 24 + 8 + m + 1)
                        product(ps[:, m % 4, 0:T], POS_OUT + i, t, KT, hdnR, bigR)\
                            .then_inc(sem("post_product_done"), 1)
                norm_post(l, 1)
                norm_pre(l, 2)
                ffn(l, 1)
                norm_post(l, 2)
            pe.wait_ge(sem("x_done"), 24 * DEPTH + KT)
            for c, (o, L) in enumerate(CH):
                if c:
                    pe.wait_ge(sem("x_out_read"), c)
                for k in range(KT):
                    g = tr(ps[0:L, k // 4, (k % 4) * P:(k % 4 + 1) * P], x[:, k, o:o + L])
                g.then_inc(sem("x_back"), 1)

        @block.scalar
        def _(act):
            A = act.activation
            n_chain = [0]

            def link(l, ins):
                n_chain[0] += 1
                ins.then_inc(sem("act_chain"), 1)
                act.wait_ge(sem("act_chain"), l * CHAIN["act"] + n_chain[0])

            act.sem_inc(sem("y_done"), Y_CREDIT)
            act.sem_inc(sem("silu_done"), H_CREDIT)
            act.dma_start(cst[:, :], I["const"]).then_inc(sem("const_loaded"), 16)
            act.dma_start(xtok_s[:, 0:2, :], I["x_prompt"].rearrange("o (c p) d -> p (o c) d", p=P))\
                .then_inc(sem("x_loaded"), 16)
            act.dma_start(xtok_s[0:NS, 2, :], I["x_sample"].rearrange("b t d -> (b t) d"))\
                .then_inc(sem("x_loaded"), 16)
            act.dma_start(gain_rows, I["norm_sandwich"].rearrange("l i (k p) -> (l i k) p", p=P))\
                .then_inc(sem("gain_rows_loaded"), 16)

            def upper(l, pos, rows=KT, free=None, j=0):
                s, v = ring_pos(l, pos)
                act.wait_ge(w_in_s[s], v + j * 16)
                if free:
                    act.wait_ge(*free)
                A(whighR[:, pos % 2, 0:rows * 256], ring[:, s, 0:rows * 256], ACT.Copy)\
                    .then_inc(sem("weights_high"), 1)

            def next_upper(l, pos):
                upper(l, pos, free=used(l, pos - 2) if pos >= 2 else None)

            def upper_hdn(l, n):
                for k in range(KT):
                    act.wait_ge(sem("hdn_full"), l * 24 + n * 8 + k + 1)
                    A(hdn[:, k, :].bitcast(F32R), y[:, k, :], ACT.Copy).then_inc(sem("hdn_high"), 1)

            def logs():
                act.preload_act_table_set("natural_log_exp_and_others")

            def norm(l, i):
                if i == 0 or i % 2:
                    logs()
                act.wait_ge(sem("norm_sum"), l * 6 + i + 1)
                act.wait_ge(sem("rrow_used"), l * 6 + i + FREE)
                link(l, A(lnr[:, :], ps[:, 4, 0:T], ACT.Ln, bias=epsc[:, :], scale=1.0 / D))
                A(rrow[:, :], lnr[:, :], ACT.Exp, scale=-0.5).then_inc(sem("rrow_ready"), 1)

            def squares(l, pre, post_done, during):
                for k in range(KT):
                    if k == 3:
                        for pos in during:
                            next_upper(l, pos)
                    act.wait_ge(sem("x_done"), post_done + k + 1)
                    A(y[:, k, :], x[:, k, :], ACT.Square).then_inc(sem("x_squared"), 1)

            def products(l, post, ms):
                for m in ms:
                    act.wait_ge(sem("post_product_done"), l * 24 + post * 8 + m + 1)
                    if m >= 2:
                        act.wait_ge(sem("squares_added"), l * 24 + post * 8 + m - 1)
                    A(sq[:, m % 2, :], ps[:, m % 4, 0:T], ACT.Square)
                    A(y[:, m, :], ps[:, m % 4, 0:T], ACT.Copy).then_inc(sem("y_done"), 1)

            def ffn(l, f):
                base = POS_FFN[f]

                def silus(i0):
                    for t in range(2):
                        act.wait_ge(sem("gate_done"), i0 + t + 1)
                        act.wait_ge(sem("h_done"), i0 + t - 1 + H_CREDIT)
                        A(sg[:, t, :], ps[:, 2 * t, 0:T], ACT.Silu).then_inc(sem("silu_done"), 1)

                act.preload_act_table_set("silu_and_others")
                with act.Fori(0, PAIRS // 2) as j:
                    for t in range(2):
                        silus(l * 2 * FT + f * FT + j * 4 + 2 * t)
                        upper(l, base + 2 * t + 2, free=gate_used(l, f, j * 2 + t), j=j)
                        upper(l, base + 2 * t + 3, free=up_used(l, f, j * 2 + t), j=j)
                silus(l * 2 * FT + f * FT + FT - 2)
                pos = base + 2 * PAIRS
                upper(l, pos, free=used(l, pos - 2))
                upper(l, pos + 1, free=used(l, pos - 1))
                for mp in range(4):
                    for part, rows in enumerate(DOWN):
                        n = 3 * mp + part
                        if n >= 2:
                            upper(l, pos + n, rows, used(l, pos + n - 2))
                    if mp:
                        products(l, 2 * f, (2 * mp - 2, 2 * mp - 1))
                if f == 0:
                    next_upper(l, POS_IN)
                products(l, 2 * f, (KT - 2, KT - 1))

            def mixers(l):
                l1 = l + 1
                def conv_silu(ct):
                    act.wait_ge(sem("conv_done"), l * NC + ct + 1)
                    A(big[:, CONV_T[ct], 0:SEQ], big[:, CONV_T[ct], 0:SEQ], ACT.Silu)\
                        .then_inc(sem("conv_silu"), 1)

                def gate_functions():
                    logs()
                    act.wait_ge(sem("u_ready"), l1)
                    link(l, A(AB[:, :, :], U[:, :, 0:12], ACT.Abs))
                    link(l, A(AB[:, :, :], AB[:, :, :], ACT.Exp, scale=-1.0))
                    A(AB[:, :, :], AB[:, :, :], ACT.Ln, bias=1.0)
                    A(alog[:, 0:8], alog[:, 0:8], ACT.Exp)
                    A(beta[:, :, :], U[:, :, 12:16], ACT.Exp).then_inc(sem("gate_exps"), 1)

                def sample_silu():
                    act.wait_ge(sem("conv_s_done"), l1)
                    for ct in range(NC):
                        g = A(big[:, CONV_T[ct], SEQ:T],
                              ctmp[:, ct, :, :].rearrange("p b t -> p (b t)"), ACT.Silu)
                    g.then_inc(sem("conv_s_silu"), 1)
                    act.wait_ge(sem("conv_s_silu"), l1)
                    A(DTf[:, 0:4 * T], big[:, 0:4, :].rearrange("p k t -> p (k t)"), ACT.Square)\
                        .then_inc(sem("qk_squared"), 1)

                def decay_factors():
                    act.wait_ge(sem("w_arg"), l1)
                    A(wexp[:, :, 0:8], wexp[:, :, 0:8], ACT.Exp).then_inc(sem("wexp_ready"), 1)
                    act.wait_ge(sem("erow_done"), l1)
                    for n in range(2):
                        A(er[:, 2 * n:2 * n + 2, :], B(5 + n, 2, 160), ACT.Exp)
                    A(decP[:, 0:4], ps[:, 5, 320:324], ACT.Exp)
                    A(decS[:, 0:48], ps[:, 6, 320:368], ACT.Exp).then_inc(sem("er_read"), 1)

                def late_factors():
                    logs()
                    act.wait_ge(sem("qk_norms_done"), l1)
                    for n in range(4):
                        g = A(DTf[:, n * T:(n + 1) * T], ps[:, 4 + n, 0:T], ACT.Ln, bias=epsc[:, :])
                    link(l, g)
                    A(DTf[:, 0:4 * T], DTf[:, 0:4 * T], ACT.Exp, scale=-0.5).then_inc(sem("qk_norms_read"), 1)
                    act.wait_ge(sem("m_rows_arg"), l1)
                    A(eI[:, :], eI[:, :], ACT.Exp)
                    A(eD[:, :], eD[:, :], ACT.Exp).then_inc(sem("m_rows_ready"), 1)
                    act.wait_ge(sem("ml_arg"), l1)
                    for rows, cc in ((P, slice(0, 2)), (NS, slice(2, 3))):
                        A(emt[0:rows, cc, :], mt[0:rows, cc, :], ACT.Exp, scale=-1.0)
                        g = A(wexp[0:rows, cc, 8:12], wexp[0:rows, cc, 8:12], ACT.Exp)
                    g.then_inc(sem("ml_exps"), 1)

                conv_at = {2 * ct + (5 if ct < 6 else 9): ct for ct in range(NC)}
                during = {14: gate_functions, 19: sample_silu, 26: decay_factors, 29: late_factors}
                for i in range(NPT):
                    act.wait_ge(sem("proj_done"), l * NPT + i + 1)
                    src = ps[:, i % 4, 0:T]
                    if i % 2 and i < NPT - 3:
                        next_upper(l, POS_IN + (i + 3) // 2)
                    if i in CONV_T:
                        ct = CONV_T.index(i)
                        A(xP[:, ct, 3:], src[:, 0:SEQ], ACT.Copy)
                        g = A(xS[:, ct, :, 3:], src[:, SEQ:].rearrange("p (b t) -> p b t", t=LS), ACT.Copy)
                    elif i in SILU_T:
                        g = A(big[:, i, :], src, ACT.Silu)
                    elif i >= 28:
                        g = A(big[:, i, :], src, ACT.Tanh, scale=0.5)
                    elif i in (16, 17, 24, 25):
                        g = A(big[:, i, :], src, ACT.Copy, scale=HD ** -0.5)
                    else:
                        g = A(big[:, i, :], src, ACT.Copy)
                    g.then_inc(sem("proj_read"), 1)
                    if i in conv_at:
                        conv_silu(conv_at[i])
                    if i in during:
                        during[i]()
                for mi, m in enumerate(MIX):
                    act.wait_ge(sem("mixed_ready"), l * 4 + mi + FREE)
                    if m == "gdn":
                        act.wait_ge(sem("kbd_ready"), l1)
                    q = QT[m]
                    for b in range(2):
                        r = slice(b * HD, (b + 1) * HD)
                        if m == "ssd":
                            g = A(qbd[r, 0, b, :], big[r, q, :], ACT.Copy)
                        else:
                            g = A(qbd[r, :, b, :], big[r, q:q + 2, :], ACT.Copy)
                    g.then_inc(sem("qbd_ready"), 1)
                    nk = P if m == "ssd" else GW
                    for c, (o, L) in enumerate(CH):
                        act.wait_ge(sem("kv_turned"), l * 12 + 3 * mi + c + 1)
                        A(K[0:L, c, 0:nk], ps[0:L, (4, 7)[c % 2], 0:nk], ACT.Copy).then_inc(sem("k_read"), 1)
                    if m != "ret":
                        for c, (o, L) in enumerate(CH):
                            act.wait_ge(sem("decay_arg"), l * 9 + 3 * [0, 0, 1, 2][mi] + c + 1)
                            A(DT[0:L, c, :, 0:L], DT[0:L, c, :, 0:L], ACT.Exp).then_inc(sem("decay_ready"), 1)
                    if m == "ml":
                        act.wait_ge(sem("ssm_samples_stored"), l1 * 64)
                        upper(l, POS_OUT)
                    if m == "ssd":
                        act.wait_ge(sem("ssd_gated"), l1)
                        for n in range(2):
                            g = A(tiny[:, n, :], big[:, 8 + n, :], ACT.Square)
                        g.then_inc(sem("ssd_squared"), 1)
                        act.wait_ge(sem("ssd_sum"), l1)
                        link(l, A(lnr[:, :], ps[:, 0, 0:T], ACT.Ln, bias=epsc[:, :], scale=1.0 / GW))
                        A(lnr[:, :], lnr[:, :], ACT.Exp, scale=-0.5).then_inc(sem("ssd_rrow"), 1)
                        continue
                    n3 = l * 3 + [0, 1, 0, 2][mi] + 1
                    act.wait_ge(sem("raw_ready"), l * 12 + 3 * mi + 3)
                    A(osq, on, ACT.Square).then_inc(sem("out_sq"), 1)
                    act.wait_ge(sem("out_ss"), n3)
                    link(l, A(sml[:, 1], sml[:, 0], ACT.Ln, bias=epsc[:, :], scale=1.0 / HD))
                    A(sml[:, 2], sml[:, 1], ACT.Exp, scale=-0.5).then_inc(sem("out_rn"), 1)
                act.wait_ge(sem("sadd_done"), l * 16 + 16 + FREE)
                upper(l, POS_OUT + 1)

            with act.Fori(0, DEPTH) as l:
                n_chain[0] = 0
                squares(l, 0, l * 24, (0, 1))
                norm(l, 0)
                upper_hdn(l, 0)
                ffn(l, 0)
                norm(l, 1)
                squares(l, 1, l * 24 + 8, (POS_IN + 1,))
                norm(l, 2)
                upper_hdn(l, 1)
                mixers(l)
                for i in (2, 3):
                    next_upper(l, POS_OUT + i)
                    products(l, 1, (2 * i - 4, 2 * i - 3))
                products(l, 1, (4, 5))
                next_upper(l, POS_FFN[1])
                products(l, 1, (6, 7))
                norm(l, 3)
                squares(l, 2, l * 24 + 16, (POS_FFN[1] + 1,))
                norm(l, 4)
                upper_hdn(l, 2)
                ffn(l, 1)
                norm(l, 5)
            assert n_chain[0] == CHAIN["act"]

        @block.vector
        def _(dve):
            TT, TS, STT, CP = dve.tensor_tensor, dve.tensor_scalar, dve.scalar_tensor_tensor, dve.tensor_copy
            n_chain = [0]

            def link(l, ins):
                n_chain[0] += 1
                ins.then_inc(sem("dve_chain"), 1)
                dve.wait_ge(sem("dve_chain"), l * CHAIN["dve"] + n_chain[0])

            dve.sem_inc(sem("h_done"), H_CREDIT)
            dve.sem_inc(sem("rrow_used"), FREE)
            dve.sem_inc(sem("mixed_ready"), FREE)
            dve.memset(epsc[:, :], EPS)
            dve.memset(gb2[:, :, 12:16], 0.0)
            dve.memset(ssum[:, :], 0.0).then_inc(sem("zeros_set"), 1)
            dve.wait_ge(sem("zeros_set"), 1)
            for tile in (wghf[:, KT * 20:].bitcast(F32R), wgfR[:, KT * 20:]):
                CP(tile, ssum[:, 0:P - 20])
            dve.memset(U[:, :, :], 0.0)
            dve.memset(V[:, :, :, HD:], 1.0)
            dve.memset(Sbd[:, :, :, :], 0.0)
            dve.memset(qbd[:, :, :, :], 0.0)
            dve.memset(cbias[:, 0:6], 0.0)
            dve.memset(al2[:, :, 8:12], -1.0).then_inc(sem("dve_set"), 1)
            for k in range(KT):
                dve.wait_ge(sem("x_turned"), k + 1)
                CP(x[:, k, :], ps[:, k, 0:T]).then_inc(sem("x_done"), 1)
            dve.wait_ge(sem("gains_turned"), 1)
            CP(gn[:, :, :, :].rearrange("p l i k -> p (l i k)"), B(0, 96)).then_inc(sem("params_placed"), 1)
            dve.wait_ge(sem("params_turned"), 1)
            CP(p2[:, :, :].rearrange("p l n -> p (l n)"), B(1, 104)).then_inc(sem("params_placed"), 1)
            dve.wait_ge(sem("x_done"), KT)
            dve.wait_ge(sem("params_placed"), 2)
            dve.wait_ge(sem("dve_set"), 1)

            def upper(out, in_):
                return CP(out, in_)

            def lower(out, in_, high):
                return TT(out, in_, high, ALU.subtract)

            def lower_weights(l, pos, rows=KT, j=0):
                dve.wait_ge(sem("weights_high"), l * N_POS + pos + 1 + j * 4)
                n = rows * 256
                lower(ringR[:, pos % RING, 0:n], ring[:, pos % RING, 0:n], whighR[:, pos % 2, 0:n].bitcast(F32)).then_inc(sem("weights_split"), 1)

            def pre(l, i):
                if i == 0:
                    lower_weights(l, 0)
                lower_weights(l, (POS_FFN[0], None, POS_IN, None, POS_FFN[1])[i] + 1)
                dve.wait_ge(sem("rrow_ready"), l * 6 + i + 1)
                for k in range(KT):
                    STT(y[:, k, :], x[:, k, :], gcol[:, i, k:k + 1], rrow[:, :], ALU.mult, ALU.mult)\
                        .then_inc(sem("hdn_full"), 1)
                for n in range(2):
                    ks = slice(4 * n, 4 * n + 4)
                    dve.wait_ge(sem("hdn_high"), l * 24 + i * 4 + 4 * n + 4)
                    lower(yR[:, ks, :], y[:, ks, :], hdn[:, ks, :]).then_inc(sem("hdn_low"), 1)
                TS(ssum[:, 0:1], rrow[:, 0:1], 1.0, None, ALU.mult).then_inc(sem("rrow_used"), 1)

            def add_squares(l, p, m):
                dve.wait_ge(sem("y_done"), l * 24 + 8 * p + m + 1 + Y_CREDIT)
                if m == 0:
                    g = CP(ssum[:, :], sq[:, 0, :])
                else:
                    dve.wait_ge(sem("squares_added"), l * 24 + 8 * p + m)
                    g = TT(ssum[:, :], ssum[:, :], sq[:, m % 2, :], ALU.add)
                g.then_inc(sem("squares_added"), 1)

            def post(l, p, half):
                i = 2 * p + 1
                g_ = ghalf if half else gcol
                if p < 2:
                    lower_weights(l, (POS_IN, POS_FFN[1])[p])
                dve.wait_ge(sem("rrow_ready"), l * 6 + i + 1)
                for k in range(KT):
                    link(l, STT(y[:, k, :], y[:, k, :], g_[:, i, k:k + 1], rrow[:, :], ALU.mult, ALU.mult))
                    TT(x[:, k, :], x[:, k, :], y[:, k, :], ALU.add).then_inc(sem("x_done"), 1)
                TS(ssum[:, 0:1], rrow[:, 0:1], 1.0, None, ALU.mult).then_inc(sem("rrow_used"), 1)

            def ffn(l, f):
                base = POS_FFN[f]

                def hidden(i, tile, t):
                    dve.wait_ge(sem("silu_done"), i + 1 + H_CREDIT)
                    dve.wait_ge(sem("up_done"), i + 1)
                    h, hR, highR = (v[:, bass.ds(tile, 1), :].rearrange("p o t -> p (o t)")
                                    for v in (low, lowR, bigR))
                    TT(h, sg[:, t, :], ps[:, 2 * t + 1, 0:T], ALU.mult).then_inc(sem("h_product"), 1)
                    dve.wait_ge(sem("h_product"), i + 1)
                    upper(highR, h).then_inc(sem("h_high"), 1)
                    dve.wait_ge(sem("h_high"), i + 1)
                    lower(hR, h, highR.bitcast(F32)).then_inc(sem("h_done"), 1)

                with dve.Fori(0, PAIRS // 2) as j:
                    for t in range(2):
                        i = l * 2 * FT + f * FT + j * 4 + 2 * t
                        lower_weights(l, base + 2 * t + 2, j=j)
                        hidden(i, j * 4 + 2 * t, 0)
                        hidden(i + 1, j * 4 + 2 * t + 1, 1)
                        lower_weights(l, base + 2 * t + 3, j=j)
                i = l * 2 * FT + f * FT + FT - 2
                pos = base + 2 * PAIRS
                lower_weights(l, pos)
                hidden(i, FT - 2, 0)
                hidden(i + 1, FT - 1, 1)
                lower_weights(l, pos + 1)
                for mp in range(4):
                    for part, rows in enumerate(DOWN):
                        n = 3 * mp + part
                        if n >= 2:
                            lower_weights(l, pos + n, rows)
                    if mp:
                        add_squares(l, 2 * f, 2 * mp - 2)
                        add_squares(l, 2 * f, 2 * mp - 1)
                add_squares(l, 2 * f, KT - 2)
                add_squares(l, 2 * f, KT - 1)
                post(l, 2 * f, True)

            def mixers(l):
                l1 = l + 1
                link(l, dve.memset(xP[:, :, 0:3], 0.0))
                dve.wait_ge(sem("layers_stored"), l + FREE)

                def weights(n):
                    lower_weights(l, POS_IN + n)

                weights(2)
                dve.wait_ge(sem("gates_done"), l1)
                CP(lnr[0:20, :], ps[0:20, 5, 0:T]).then_inc(sem("gates_copied"), 1)
                dve.wait_ge(sem("hist_turned"), l1)
                CP(xS[:, :, :, 0:3], B(6, NC, NB * 3).rearrange("p c (b j) -> p c b j", j=3))\
                    .then_inc(sem("hist_placed"), 1)
                def conv(ct):
                    i = CONV_T[ct]
                    dve.wait_ge(sem("proj_read"), l * NPT + i + 1)
                    out = big[:, i, 0:SEQ]
                    link(l, TS(out, xP[:, ct, 0:SEQ], taps[:, ct, 0:1], cbias[:, ct:ct + 1], ALU.mult, ALU.add))
                    for j in (1, 2, 3):
                        g = STT(out, xP[:, ct, j:j + SEQ], taps[:, ct, j:j + 1], out, ALU.mult, ALU.add)
                        if j < 3:
                            link(l, g)
                        else:
                            g.then_inc(sem("conv_done"), 1)

                conv(0)
                for ct in range(1, 6):
                    weights(ct + 2)
                    conv(ct)
                    if ct == 2:
                        dve.wait_ge(sem("gates_turned"), l1)
                        TT(U[:, 0:2, :], B(4, 2, 20), bc(gbias[:, :], 1, 2), ALU.add)
                        link(l, TT(U[0:NS, 2, :], ps[0:NS, 4, 40:60], gbias[0:NS, :], ALU.add))
                        TT(U[:, :, :], U[:, :, :], bc(sign, 1, 3), ALU.mult).then_inc(sem("u_ready"), 1)
                weights(8)
                dve.wait_ge(sem("proj_read"), l * NPT + CONV_T[-1] + 1)
                dve.wait_ge(sem("hist_placed"), l1)
                bcw = lambda j: taps[:, :, j:j + 1].unsqueeze(3).broadcast_to([P, NC, NB, LS])
                cs = C4[:, :, :, :]
                link(l, TT(ctmp[:, :, :, :], xS[:, :, :, 0:LS], bcw(0), ALU.mult))
                for j in (1, 2, 3):
                    link(l, TT(cs, xS[:, :, :, j:j + LS], bcw(j), ALU.mult))
                    link(l, TT(ctmp[:, :, :, :], ctmp[:, :, :, :], cs, ALU.add))
                TT(ctmp[:, :, :, :], ctmp[:, :, :, :],
                   cbias[:, :].unsqueeze(2).unsqueeze(3).broadcast_to([P, NC, NB, LS]), ALU.add)\
                    .then_inc(sem("conv_s_done"), 1)
                CP(last[:, :, 0:3], xP[:, :, SEQ:SEQ + 3])
                CP(last[:, :, 3:27].rearrange("p c (b j) -> p c b j", j=3), xS[:, :, :, LS:LS + 3])\
                    .then_inc(sem("last_ready"), 1)
                weights(9)
                dve.wait_ge(sem("rotated"), l1)
                rq = big[:, RET_T:RET_T + 4, :]
                sine3 = SX["ret"][:, :, :, :].rearrange("p b h d -> p (b h d)")[:, 0:3 * T]\
                    .rearrange("p (k t) -> p k t", k=3)
                TT(sine3, ps[:, 4:7, 0:T], bc(C("sin"), 1, 3), ALU.mult)
                TT(lnr[:, :], ps[:, 7, 0:T], C("sin"), ALU.mult).then_inc(sem("rotated_read"), 1)
                dve.wait_ge(sem("rotated_read"), l1)
                link(l, TT(rq, rq, bc(C("cos"), 1, 4), ALU.mult))
                TT(rq[:, 0:3, :], rq[:, 0:3, :], sine3, ALU.add)
                link(l, TT(rq[:, 3, :], rq[:, 3, :], lnr[:, :], ALU.add))
                weights(10)
                dve.wait_ge(sem("gate_exps"), l1)
                link(l, STT(SP[:, :, :], U[:, :, 0:12], 0.0, AB[:, :, :], ALU.max, ALU.add))
                TS(alog[:, 0:8], alog[:, 0:8], -1.0, None, ALU.mult)
                link(l, TS(beta[:, :, :], beta[:, :, :], 1.0, None, ALU.add))
                link(l, dve.reciprocal(beta[:, :, :], beta[:, :, :]))
                TT(G[:, :, :], SP[:, :, :], bc(alog[:, :], 1, 3), ALU.mult).then_inc(sem("decays_ready"), 1)
                conv(6)
                weights(11)
                dve.wait_ge(sem("decays_ready"), l1)
                dve.wait_ge(sem("conv_s_silu"), l1)
                CP(Gb[:, :, 0:4, :].rearrange("p c (a b) d -> p c a b d", a=2)[:, 0],
                   bc(slots1(G[:, 1, 0:4], "ssd"), 3, HD))
                CP(Gb[:, :, 0:4, :].rearrange("p c (a b) d -> p c a b d", a=2)[:, 1],
                   bc(slots1(G[:, 2, 0:4], "ssd"), 3, HD))
                CP(Gb[:, :, 4:8, :], bc(G[:, 1:3, 4:8], 3, HD))
                TT(Gx[:, 0:16].rearrange("p (a h) -> p a h", h=H), bc(G[0:NS, 2, 4:8], 1, 4),
                   bc(C("obp", NS), 2, H), ALU.mult)
                TT(Gx[:, 16:48].rearrange("p (a h) -> p a h", h=H), bc(G[0:NS, 2, 0:4], 1, NB),
                   bc(C("onehot", NS), 2, H), ALU.mult).then_inc(sem("decays_spread"), 1)
                conv(7)
                weights(12)
                dve.wait_ge(sem("cum_done"), l1)
                link(l, CP(cum[:, :, :], B(4, 3, 12)))
                TT(wexp[:, :, 0:8], B(7, 3, 12)[:, :, 0:8], cum[:, :, 0:8], ALU.subtract).then_inc(sem("w_arg"), 1)
                TT(aT[:, :, :], U[:, :, 16:20], cum[:, :, 8:12], ALU.subtract).then_inc(sem("a_ready"), 1)
                conv(8)
                weights(13)
                dve.wait_ge(sem("a_turned"), l1)
                link(l, CP(aH[:, :], ps[0:H, 4, 0:T]))
                link(l, TT(aH[:, SEQ::LS], aH[:, SEQ::LS], mmc[:, :], ALU.max))
                link(l, dve.tensor_tensor_scan(mH[:, :], C("reset", H), aH[:, :], 0.0, ALU.add, ALU.max))
                CP(mL[:, 0:SEQ].rearrange("p (c n) -> p c n", c=2), bc(mH[:, P - 1:SEQ:P], 2, P))
                CP(mL[:, SEQ:].rearrange("p (b t) -> p b t", t=LS), bc(mH[:, SEQ + LS - 1::LS], 2, LS))
                dve.memset(mPv[:, 0:P], 0.0)
                CP(mPv[:, P:SEQ], mH[:, P - 1:P].broadcast_to([H, P]))
                link(l, CP(mPv[:, SEQ:].rearrange("p (b t) -> p b t", t=LS), bc(mmc[:, :], 2, LS)))
                TT(eI[:, :], mPv[:, :], mH[:, :], ALU.subtract)
                TT(eD[:, :], mPv[:, :], mL[:, :], ALU.subtract).then_inc(sem("m_rows_arg"), 1)
                conv(9)
                weights(14)
                CP(Bb[:, :, :, :], bc(beta[:, :, :], 3, HD)).then_inc(sem("beta_spread"), 1)
                dve.wait_ge(sem("proj_read"), l1 * NPT)
                TS(big[:, 28:30, :].rearrange("p k t -> p (k t)"),
                   big[:, 28:30, :].rearrange("p k t -> p (k t)"), 0.5, 0.5, ALU.mult, ALU.add)
                dve.wait_ge(sem("qk_norms_read"), l1)
                STT(big[:, 0:2, :].rearrange("p k t -> p (k t)"), big[:, 0:2, :].rearrange("p k t -> p (k t)"),
                    HD ** -0.5, DTf[:, 0:2 * T], ALU.mult, ALU.mult)
                link(l, TT(big[:, 2:4, :].rearrange("p k t -> p (k t)"),
                           big[:, 2:4, :].rearrange("p k t -> p (k t)"), DTf[:, 2 * T:4 * T], ALU.mult))
                TT(ki[:, :, :], big[:, 2:4, P:T], er[:, 2:4, :], ALU.mult)
                dve.wait_ge(sem("m_tok_done"), l1)
                mtk = lambda n: ps[:, 7, 300 + 12 * n:312 + 12 * n].rearrange("p (c h) -> p c h", h=H)
                for rows, cc in ((P, slice(0, 2)), (NS, slice(2, 3))):
                    TT(mt[0:rows, cc, :], mtk(0)[0:rows, cc, :], cum[0:rows, cc, 8:12], ALU.add)
                    g = TT(wexp[0:rows, cc, 8:12], aT[0:rows, cc, :], mtk(1)[0:rows, cc, :], ALU.subtract)
                g.then_inc(sem("ml_arg"), 1)
                CP(er[:, 4:6, :], B(6, 2, 160))
                CP(decP[:, 4:6], ps[:, 6, 320:322])
                link(l, CP(sml[0:NS, 3, 0:H], mtk(2)[0:NS, 2, :]))
                TT(Gx[:, 48:64].rearrange("p (a h) -> p a h", h=H), bc(sml[0:NS, 3, 0:H], 1, 4),
                   bc(C("first", NS), 2, H), ALU.mult).then_inc(sem("ml_decay_spread"), 1)
                dve.wait_ge(sem("beta_rows_done"), l1)
                dve.wait_ge(sem("kbd_clear"), l1)
                for b in range(2):
                    r = slice(b * HD, (b + 1) * HD)
                    g = TT(kbd[r, :, b, :], big[r, 2:4, :], ps[r, 4:6, 0:T], ALU.mult)
                g.then_inc(sem("kbd_ready"), 1)
                dve.wait_ge(sem("ml_decS_done"), l1)
                link(l, CP(decS[:, 48:64], ps[:, 7, 64:80]))
                for mi, m in enumerate(MIX):
                    mixer(l, l1, mi, m)
                dve.wait_ge(sem("last_turned"), l1)
                dve.wait_ge(sem("layers_stored"), l + FREE)
                for n in range(3):
                    w = min(4, NC - 4 * n)
                    g = CP(lastT[:, 4 * n:4 * n + w, :].rearrange("p c n -> p (c n)"), ps[0:27, 4 + n, 0:w * P])
                g.then_inc(sem("last_read"), 1)

            def mixer(l, l1, mi, m):
                w = HW[m]
                Sx = SX[m]
                i12 = l * 12 + 3 * mi
                q = QT[m]
                if m == "ssd":
                    g = TT(qi[:, :, :], bc(big[:, q, P:T], 1, 2), er[:, 0:2, :], ALU.mult)
                else:
                    e = retI if m == "ret" else er[:, 2:4, :] if m == "gdn" else er[:, 4:6, :]
                    g = TT(qi[:, :, :], big[:, q:q + 2, P:T], e, ALU.mult)
                g.then_inc(sem("qk_ready"), 1)
                for c, (o, L) in enumerate(CH):
                    dve.wait_ge(sem("kv_turned"), i12 + c + 1)
                    vsrc = slots(B((0, 2)[c % 2], H, HD, rows=L), m)
                    vdst = V[0:L, c, :, 0:HD].rearrange("p (a b) d -> p a b d", a=2)
                    if m == "ssd":
                        TT(Dx[0:L, c].rearrange("p (a b) d -> p a b d", a=2), vsrc,
                           bc(slots1(sD[0:L, :], m), 3, HD), ALU.mult)
                        g = TT(vdst, vsrc, bc(slots1(SP[0:L, c, 0:4], m), 3, HD), ALU.mult)
                    else:
                        g = CP(vdst, vsrc)
                    g.then_inc(sem("v_read"), 1)
                if m != "ret":
                    neg = (C("neg"), C("neg"), C("neg_s", NS))
                    for c, (o, L) in enumerate(CH):
                        dve.wait_ge(sem("decay_rows"), l * 9 + 3 * [0, 0, 1, 2][mi] + c + 1)
                        for s in range(H):
                            h = head(m, s // 2, s % 2)
                            if m == "ml":
                                col, op = aT[0:L, c, s:s + 1], ALU.add
                            else:
                                col, op = cum[0:L, c, DC[m] + h:DC[m] + h + 1], ALU.subtract
                            g = STT(DT[0:L, c, s, 0:L], ps[0:L, (1, 5)[c % 2], s * L:(s + 1) * L], col, neg[c], op, ALU.add)
                        g.then_inc(sem("decay_arg"), 1)
                dve.wait_ge(sem("dup_done"), l * 4 + mi + 1)
                spread = lambda off: bc(B(3, H, NS, off=off), 2, 4)
                g = TT(QX[:, :, :, :], spread(0), bc(bmask, 1, H), ALU.mult)
                if m == "gdn":
                    g = TT(KQX[:, :, :, :], spread(P), bc(bmask, 1, H), ALU.mult)
                g.then_inc(sem("qx_ready"), 1)
                if m == "ssd":
                    for bp in range(4):
                        dve.wait_ge(sem("snat_turned"), l * 4 + bp + 1)
                        CP(Sx[:, bp, :, 0:HD], B(5 + bp % 2, H, HD)).then_inc(sem("snat_read"), 1)
                if m == "gdn":
                    gdn_solve(l, l1)
                def probs(c):
                    L = CH[c][1]
                    dve.wait_ge(sem("scores_done"), i12 + c + 1)
                    if m == "ret":
                        d = retD if c < 2 else retDs[0:NS]
                    else:
                        dve.wait_ge(sem("decay_ready"), l * 9 + 3 * [0, 0, 1, 2][mi] + c + 1)
                        d = DT[0:L, c, :, 0:L]
                    if m == "ssd":
                        g = TT(PT[0:L, c, :, 0:L].rearrange("p (a b) n -> p a b n", a=2),
                               bc(B(c % 2, 2, L, rows=L), 1, 2), d.rearrange("p (a b) n -> p a b n", a=2), ALU.mult)
                    else:
                        g = TT(PT[0:L, c, :, 0:L], B(c % 2, H, L, rows=L), d, ALU.mult)
                    g.then_inc(sem("probs_ready"), 1)

                probs(0)
                for c, (o, L) in enumerate(CH):
                    if m == "gdn":
                        bt = bc(beta[0:L, c, :], 2, HD)
                        if c:
                            dve.wait_ge(sem("ks_done"), l * 2 + c)
                            link(l, TT(VW[0:L, c, :, 0:HD], V[0:L, c, :, 0:HD], B(5, H, HD, rows=L), ALU.subtract))
                            TT(VW[0:L, c, :, 0:HD], VW[0:L, c, :, 0:HD], bt, ALU.mult)\
                                .then_inc(sem("resid_ready"), 1)
                        else:
                            TT(VW[0:L, c, :, 0:HD], V[0:L, c, :, 0:HD], bt, ALU.mult)\
                                .then_inc(sem("resid_ready"), 1)
                        dve.wait_ge(sem("vnew_done"), l * 3 + c + 1)
                        g = CP(V[0:L, c, :, 0:HD], B(6, H, HD, rows=L))
                    else:
                        g = TS(sml[0:1, 0, 0:1], epsc[0:1, :], 1.0, None, ALU.mult)
                    g.then_inc(sem("values_ready"), 1)
                    if c < 2:
                        probs(c + 1)
                    dve.wait_ge(sem("values_ready"), i12 + c + 1)
                    if m == "ret":
                        wt = bc(tail[0:L, c, :], 2, w)
                    elif m == "ssd":
                        wt = bc(slots1(wexp[0:L, c, 0:4], m), 3, w)
                    else:
                        wt = bc(wexp[0:L, c, DC[m]:DC[m] + 4], 2, w)
                    dst, src = VW[0:L, c, :, 0:w], V[0:L, c, :, 0:w]
                    if m == "ssd":
                        dst, src = (v.rearrange("p (a b) n -> p a b n", a=2) for v in (dst, src))
                    TT(dst, src, wt, ALU.mult).then_inc(sem("vw_ready"), 1)
                    if c < 2:
                        dve.wait_ge(sem("state_add"), l * 8 + 2 * mi + c + 1)
                        sp_ = B(7, 2, w)
                        if c == 0:
                            if mi:
                                dve.wait_ge(sem("prompt_stored"), l * PSTORES + PS_BEFORE[m])
                            for b in range(2):
                                r = slice(b * HD, (b + 1) * HD)
                                CP(Sbd[r, :, b, 0:w], sp_[r])
                            g = CP(S1[:, :, 0:w], sp_)
                        else:
                            dec = C("ret_dec") if m == "ret" else decP[:, {"ssd": 0, "gdn": 2, "ml": 4}[m]:][:, 0:2]
                            for a in range(2):
                                g = STT(S1[:, a, 0:w], S1[:, a, 0:w], dec[:, a:a + 1], sp_[:, a, :],
                                        ALU.mult, ALU.add)
                        g.then_inc(sem("state_read"), 1)
                        dve.wait_ge(sem("state_read"), l * 8 + 2 * mi + c + 1)
                    raw_outputs(l, l1, mi, m, c, L)
                sample_decay(l, l1, mi, m)
                n3 = l * 3 + [0, 1, 0, 2][mi] + 1
                if m != "ssd":
                    dve.wait_ge(sem("out_sq"), n3)
                    dve.tensor_reduce(sml[:, 0, :], osq.rearrange("p c (h d) -> p (c h) d", h=H), AX, ALU.add)\
                        .then_inc(sem("out_ss"), 1)
                sample_states(l, l1, mi, m, (0, 1))
                if m != "ssd":
                    on12 = on.rearrange("p c (h d) -> p (c h) d", h=H)
                    dve.wait_ge(sem("out_rn"), n3)
                    TT(on12, on12, bc(sml[:, 2, :], 2, HD), ALU.mult).then_inc(sem("on_ready"), 1)
                sample_states(l, l1, mi, m, (2, 3))
                gt, ot, nb = GATE[m], OUT_T[m], NORM[m]
                dve.wait_ge(sem("on_turned"), l * 4 + mi + 1)
                if m == "ssd":
                    for n in range(2):
                        g = TT(big[:, 8 + n, :], ps[:, OUTB[m][n], 0:T], big[:, gt + n, :], ALU.mult)
                    g.then_inc(sem("ssd_gated"), 1)
                    dve.wait_ge(sem("ssd_state_turned"), l1)
                    CP(fin[:, :, :], B(4, 2, P, rows=HD)).then_inc(sem("ssd_state_read"), 1)
                    dve.wait_ge(sem("ssd_rrow"), l1)
                    for n in range(2):
                        g = STT(big[:, ot + n, :], big[:, 8 + n, :], pcol[:, nb + n:nb + n + 1], lnr[:, :],
                                ALU.mult, ALU.mult)
                else:
                    for n in range(2):
                        g = STT(big[:, ot + n, :], ps[:, OUTB[m][n], 0:T], pcol[:, nb + n:nb + n + 1],
                                big[:, gt + n, :], ALU.mult, ALU.mult)
                g.then_inc(sem("mixed_ready"), 1)
                dve.wait_ge(sem("mixed_ready"), l * 4 + mi + 1 + FREE)
                link(l, upper(hdn[:, ot:ot + 2, :].bitcast(F32R), big[:, ot:ot + 2, :]))
                link(l, lower(bigR[:, ot:ot + 2, :], big[:, ot:ot + 2, :], hdn[:, ot:ot + 2, :]))

            def raw_outputs(l, l1, mi, m, c, L):
                w = HW[m]
                o4 = B(2, H, w, rows=L)
                on4 = on[0:L, c, :].rearrange("p (h d) -> p h d", h=H)
                dve.wait_ge(sem("out_done"), l * 12 + 3 * mi + c + 1)
                if m == "ssd":
                    g = TT(slots(on4, m), o4.rearrange("p (a b) d -> p a b d", a=2),
                           Dx[0:L, c].rearrange("p (a b) d -> p a b d", a=2), ALU.add)
                elif m == "ml":
                    den = o4[:, :, HD:HE].rearrange("p h o -> p (h o)")
                    link(l, CP(sml[0:L, 3, 0:H], den))
                    link(l, STT(sml[0:L, 3, 0:H], sml[0:L, 3, 0:H], -1.0, sml[0:L, 3, 0:H], ALU.mult, ALU.max))
                    link(l, TT(sml[0:L, 3, 0:H], sml[0:L, 3, 0:H], emt[0:L, c, :], ALU.max))
                    link(l, dve.reciprocal(sml[0:L, 3, 0:H], sml[0:L, 3, 0:H]))
                    g = TT(on4, o4[:, :, 0:HD], bc(sml[0:L, 3, 0:H], 2, HD), ALU.mult)
                else:
                    g = CP(on4, o4)
                g.then_inc(sem("raw_ready"), 1)

            def sample_decay(l, l1, mi, m):
                w = HW[m]
                if m == "ssd":
                    d = decS[0:HD, 16:48].rearrange("p (b h) -> p h b", h=H)
                    v = Snat[:, :, :, :]
                    link(l, TT(v, v, bc(d, 3, HD), ALU.mult))
                    return
                Sx = SX[m]
                if m == "ret":
                    d = bc(bc(C("ret_decs"), 1, 4), 3, w)
                else:
                    at = 0 if m == "gdn" else 48
                    d = bc(decS[:, at:at + 16].rearrange("p (a h) -> p a h", h=H), 3, w)
                link(l, TT(Sx[:, :, :, 0:w], Sx[:, :, :, 0:w], d, ALU.mult))

            def sample_states(l, l1, mi, m, parts):
                w = HW[m]
                for n in parts:
                    dve.wait_ge(sem("sadd_done"), l * 16 + 4 * mi + n + 1 + FREE)
                    bank = (3, 7)[n % 2]
                    if m == "ssd":
                        h = head(m, n // 2, n % 2)
                        g = TT(Snat[:, h], Snat[:, h], B(bank, NB, HD, rows=HD), ALU.add)
                    else:
                        g = TT(SX[m][:, n, :, 0:w], SX[m][:, n, :, 0:w], B(bank, H, w), ALU.add)
                    g.then_inc(sem("sadd_read"), 1)

            def gdn_solve(l, l1):
                for c, (o, L) in enumerate(CH):
                    dve.wait_ge(sem("gram_done"), l * 3 + c + 1)
                    dve.wait_ge(sem("decay_ready"), l * 9 + c + 1)
                    at = AT[:, c] if c < 2 else ATs[:, :, :]
                    TT(at, B(0, H, L, rows=L), DT[0:L, c, :, 0:L], ALU.mult)
                    idb = bc(ident[0:L, 0:L], 1, H)
                    CP(X[:, 4 * c:4 * c + 4, :] if c < 2 else Xs[:, :, :], idb)
                    CP(XT[:, c] if c < 2 else XTs[:, :, :], idb).then_inc(sem("at_ready"), 1)
                for k in range(7):
                    cs = (0, 1, 2) if k < 2 else (0, 1)
                    i0 = l * 16 + [0, 3, 6, 8, 10, 12, 14][k]
                    for c in cs:
                        L = CH[c][1]
                        dve.wait_ge(sem("level_t"), i0 + c + 1)
                        tm = Tm[:, c] if c < 2 else Tms[:, :, :]
                        TT(tm, LB(0, c, L), bc(level[0:L, k, 0:L], 1, H), ALU.mult).then_inc(sem("t_masked"), 1)
                    for c in cs:
                        L = CH[c][1]
                        dve.wait_ge(sem("level_y"), i0 + c + 1)
                        xx = X[:, 4 * c:4 * c + 4, :] if c < 2 else Xs[:, :, :]
                        xt = XT[:, c] if c < 2 else XTs[:, :, :]
                        TT(xx, xx, LB(1, c, L), ALU.subtract)
                        TT(xt, xt, LB(2, c, L), ALU.subtract).then_inc(sem("x_level"), 1)

            with dve.Fori(0, DEPTH) as l:
                n_chain[0] = 0
                l1 = l + 1
                CP(gcol[:, :, :], gn[:, bass.ds(l, 1), :, :].rearrange("p o i k -> p (o i) k"))
                link(l, CP(pcol[:, :], p2[:, bass.ds(l, 1), :].rearrange("p o n -> p (o n)")))
                TS(ghalf[:, :, :], gcol[:, :, :], 0.5, None, ALU.mult)
                CP(taps[:, 0:6, :], pcol[:, 28:52].rearrange("p (j t) -> p t j", j=4))
                CP(taps[:, 6:10, :], pcol[:, 12:28].rearrange("p (j t) -> p t j", j=4))
                CP(cbias[:, 6:10], pcol[:, 8:12]).then_inc(sem("layer_gains"), 1)
                dve.wait_ge(sem("layer_gains"), l1)
                pre(l, 0)
                dve.wait_ge(sem("gate_params_loaded"), 16 * 18)
                CP(gbias[:, :], gb2[:, bass.ds(l, 1), :].rearrange("p o n -> p (o n)"))
                CP(alog[:, :], al2[:, bass.ds(l, 1), :].rearrange("p o n -> p (o n)"))
                CP(sD[:, :], sd2[:, bass.ds(l, 1), :].rearrange("p o n -> p (o n)"))
                CP(mmc[:, :], mm[:, bass.ds(l, 1), :].rearrange("p o n -> p (o n)"))
                link(l, CP(wg[:, :, :], wg2[:, bass.ds(l, 1), :, :].rearrange("p o k n -> p (o k) n")))
                link(l, upper(wgh[:, :, :].bitcast(F32R), wg[:, :, :]))
                lower(wgR[:, :, :], wg[:, :, :], wgh[:, :, :]).then_inc(sem("layer_params"), 1)
                dve.wait_ge(sem("layer_params"), l1)
                dve.sem_inc(sem("dve_held"), 1)
                ffn(l, 0)
                pre(l, 2)
                mixers(l)
                for i in range(4):
                    lower_weights(l, POS_OUT + i)
                for m in range(KT):
                    add_squares(l, 1, m)
                post(l, 1, False)
                pre(l, 4)
                ffn(l, 1)
            assert n_chain[0] == CHAIN["dve"]
            for c, (o, L) in enumerate(CH):
                dve.wait_ge(sem("x_back"), c + 1)
                for n in range(2):
                    g = CP(xtok_s[0:L, c, 512 * n:512 * n + 512], ps[0:L, n, :])
                g.then_inc(sem("x_out_read"), 1)

        @block.gpsimd
        def _(pool):
            dma = pool.dma_start

            def hold(s, v):
                pool.wait_ge(s, v)
                pool.sem_inc(sem("pool_held"), 1)

            pool.sem_inc(sem("layers_stored"), FREE)
            pr = sem("param_rows_loaded")
            for l in range(DEPTH):
                r = 52 * l
                for n, v in enumerate(("ret_norm", "ssm_norm", "gdn_norm", "mlstm_norm")):
                    dma(stage[r + 2 * n:r + 2 * n + 2, :], I[v][l].rearrange("(k p) -> k p", p=P)).then_inc(pr, 16)
                dma(stage[r + 8:r + 12, :], I["ssm_conv_b"][l].rearrange("(k p) -> k p", p=P)).then_inc(pr, 16)
                dma(stage[r + 12:r + 28, :], I["ssm_conv_w"][l].rearrange("j (k p) -> (j k) p", p=P)).then_inc(pr, 16)
                dma(stage[r + 28:r + 52, :], I["gdn_conv_w"][l].rearrange("j (k p) -> (j k) p", p=P)).then_inc(pr, 16)

            gl = sem("gate_params_loaded")
            win = I["w_in"].rearrange("l (k p) n -> p l k n", p=P)
            for n, c0 in enumerate((DT0, GAB0, MIF0 + H, GAB0 + H, MIF0)):
                for l in range(DEPTH):
                    dma(wg2[:, l, :, 4 * n:4 * n + 4], win[:, l, :, c0:c0 + 4]).then_inc(gl, 16)
            for n, v in enumerate(("ssm_dt_bias", "gdn_dt_bias", "mlstm_f_bias", None, "mlstm_i_bias")):
                if v:
                    dma(gb2[:, :, 4 * n:4 * n + 4], I[v].partition_broadcast(P)).then_inc(gl, 16)
            dma(al2[:, :, 0:4], I["ssm_A_log"].partition_broadcast(P)).then_inc(gl, 16)
            dma(al2[:, :, 4:8], I["gdn_A_log"].partition_broadcast(P)).then_inc(gl, 16)
            dma(sd2[:, :, :], I["ssm_D"].partition_broadcast(P)).then_inc(gl, 16)
            dma(mm[:, :, :], I["state_mlstm_m"].rearrange("l b h -> h l b")).then_inc(gl, 16)
            def at(name, l):
                return I[name][bass.ds(l, 1)]

            with pool.Fori(0, DEPTH) as l:
                l1 = l + 1
                dma(hist[:, 0:6, :], at("state_gdn_conv", l).rearrange("o b j (k p) -> (o b j) k p", p=P))\
                    .then_inc(sem("hist_loaded"), 16)
                dma(hist[:, 6:10, :], at("state_ssm_conv", l).rearrange("o b j (k p) -> (o b j) k p", p=P))\
                    .then_inc(sem("hist_loaded"), 16)
                def load_states(m):
                    name = {"gdn": "state_gdn", "ret": "state_ret", "ml": "state_mlstm_C", "ssd": "state_ssm"}[m]
                    if m == "ssd":
                        for h in range(H):
                            dma(Snat[:, h], at(name, l)[:, :, h].rearrange("o b d e -> d (o b) e"))\
                                .then_inc(sem("states_loaded_ssd"), 16)
                        return
                    for b in range(NB):
                        src = at(name, l)[:, b].rearrange("o h d e -> d (o h) e")
                        dst = SX[m][(b % 2) * HD:(b % 2 + 1) * HD, b // 2, :, 0:HD]
                        dma(dst, src).then_inc(sem("states_loaded_" + m), 16)
                    if m == "ml":
                        for b in range(NB):
                            dma(SX["ml"][(b % 2) * HD:(b % 2 + 1) * HD, b // 2, :, HD:],
                                at("state_mlstm_n", l)[:, b].rearrange("o h d -> d (o h)").unsqueeze(2))\
                                .then_inc(sem("states_loaded_ml"), 16)

                load_states("gdn")
                hold(sem("decays_ready"), l1)
                load_states("ret")
                hold(sem("proj_done"), l1 * NPT)
                pool.memset(kbd, 0.0).then_inc(sem("kbd_clear"), 1)
                for mi, m in enumerate(MIX):
                    if m == "gdn":
                        hold(sem("x_level"), l * 16 + 16)
                    hold(sem("k_read"), l * 12 + 3 * mi + 3)
                    hold(sem("sadd_done"), l * 16 + 4 * mi + FREE)
                    for s in range(2 if m == "ssd" else H):
                        g = pool.tensor_tensor(KX[:, s], bc(K[0:NS, 2, s * HD:(s + 1) * HD], 1, NB),
                                               bc(C("onehot", NS), 2, HD), ALU.mult)
                    g.then_inc(sem("kx_ready"), 1)
                    pstored = sem("prompt_stored")
                    hold(sem("state_read"), l * 8 + 2 * mi + 2)
                    if m == "ssd":
                        hold(sem("ssd_state_read"), l1)
                        for a in range(2):
                            dma(O["p_ssm"][bass.ds(l, 1), 0].rearrange("o (g a) p n -> a p (o g) n", a=2)[a],
                                fin[:, a, :].rearrange("p (g n) -> p g n", g=2)).then_inc(pstored, 16)
                    else:
                        out = {"gdn": "p_gdn", "ret": "p_ret", "ml": "p_mC"}[m]
                        for a in range(2):
                            dma(O[out][bass.ds(l, 1), 0, 2 * a:2 * a + 2].rearrange("o h d e -> (o h d) e"),
                                S1[:, a, 0:HD]).then_inc(pstored, 16)
                            if m == "ml":
                                dma(O["p_mn"][bass.ds(l, 1), 0, 2 * a:2 * a + 2].rearrange("o h d -> (o h d)").unsqueeze(1),
                                    S1[:, a, HD:]).then_inc(pstored, 16)
                    stored = sem("sample_stored")
                    hold(sem("sadd_read"), l * 16 + 4 * mi + 4)
                    out = {"gdn": "s_gdn", "ret": "s_ret", "ml": "s_mC", "ssd": "s_ssm"}[m]
                    if m == "ssd":
                        for h in range(H):
                            dma(O[out][bass.ds(l, 1), :, h].rearrange("o b d e -> d (o b) e"), Snat[:, h])\
                                .then_inc(sem("ssm_samples_stored"), 16)
                    for b in range(NB if m != "ssd" else 0):
                        dst = O[out][bass.ds(l, 1), b].rearrange("o h d e -> d (o h) e")
                        src = SX[m][(b % 2) * HD:(b % 2 + 1) * HD, b // 2, :, 0:HD]
                        dma(dst, src).then_inc(stored, 16)
                        if m == "ml":
                            dma(O["s_mn"][bass.ds(l, 1), b].rearrange("o h d -> d (o h)").unsqueeze(2),
                                SX[m][(b % 2) * HD:(b % 2 + 1) * HD, b // 2, :, HD:]).then_inc(stored, 16)
                    if m == "gdn":
                        hold(sem("mixed_ready"), l * 4 + 1 + FREE)
                        hold(stored, l * SSTORES + NB * 16)
                        load_states("ssd")
                    if m == "ret":
                        hold(stored, l * SSTORES + 2 * NB * 16)
                        load_states("ml")
                dma(O["p_mm"][bass.ds(l, 1), 0], mt[P - 1:P, 1, :]).then_inc(stored, 16)
                dma(O["s_mm"][bass.ds(l, 1)].rearrange("o b h -> (o b) h"), mt[LS - 1:NS:LS, 2, :]).then_inc(stored, 16)
                hold(sem("last_read"), l1)
                ls = sem("last_stored")
                gc = lastT[:, 0:6, :].rearrange("p c n -> p (c n)")
                sc = lastT[:, 6:10, :].rearrange("p c n -> p (c n)")
                dma(O["p_gdn_conv"][bass.ds(l, 1), 0].rearrange("o j c -> (o j) c"), gc[0:3]).then_inc(ls, 16)
                dma(O["p_ssm_conv"][bass.ds(l, 1), 0].rearrange("o j c -> (o j) c"), sc[0:3]).then_inc(ls, 16)
                dma(O["s_gdn_conv"][bass.ds(l, 1)].rearrange("o b j c -> (o b j) c"), gc[3:27]).then_inc(ls, 16)
                dma(O["s_ssm_conv"][bass.ds(l, 1)].rearrange("o b j c -> (o b j) c"), sc[3:27]).then_inc(ls, 16)
                hold(sem("prompt_stored"), l1 * PSTORES)
                hold(stored, l1 * SSTORES)
                hold(sem("ssm_samples_stored"), l1 * 64)
                pool.wait_ge(ls, l1 * 64)
                pool.sem_inc(sem("layers_stored"), 1)
            yp = O["y_prompt"].rearrange("o (c p) d -> c p (o d)", p=P)
            ys = O["y_sample"].rearrange("b t d -> (b t) d")
            for c in range(3):
                pool.wait_ge(sem("x_out_read"), c + 1)
                dma(yp[c] if c < 2 else ys, xtok_s[0:CH[c][1], c, :]).then_inc(sem("y_stored"), 16)
            pool.wait_ge(sem("y_stored"), 48)


_INS = ["x_prompt", "x_sample", "state_ret", "state_ssm", "state_ssm_conv", "state_gdn", "state_gdn_conv",
        "state_mlstm_C", "state_mlstm_n", "state_mlstm_m", "w_in", "w_out", "norm_sandwich", "ffn_w_gate",
        "ffn_w_up", "ffn_w_down", "ret_norm", "ssm_conv_w", "ssm_conv_b", "ssm_dt_bias", "ssm_A_log", "ssm_D",
        "ssm_norm", "gdn_conv_w", "gdn_dt_bias", "gdn_A_log", "gdn_norm", "mlstm_i_bias", "mlstm_f_bias",
        "mlstm_norm"]
_OUTS = {"y_prompt": (1, SEQ, D), "y_sample": (NB, LS, D)}
for _p, _b in (("p", 1), ("s", NB)):
    _OUTS |= {f"{_p}_ret": (DEPTH, _b, H, HD, HD), f"{_p}_ssm": (DEPTH, _b, H, HD, HD),
              f"{_p}_ssm_conv": (DEPTH, _b, 3, SSM_CH), f"{_p}_gdn": (DEPTH, _b, H, HD, HD),
              f"{_p}_gdn_conv": (DEPTH, _b, 3, GDN_CH), f"{_p}_mC": (DEPTH, _b, H, HD, HD),
              f"{_p}_mn": (DEPTH, _b, H, HD), f"{_p}_mm": (DEPTH, _b, H)}


def kernel(**inputs):
    import concourse.bacc as bacc
    from concourse.bass_utils import run_bass_kernel_spmd

    nc = bacc.Bacc("TRN2", target_bir_lowering=False, num_devices=1)
    arrays, ins, outs = {}, {}, {}
    for name in _INS:
        a = np.ascontiguousarray(inputs[name])
        arrays["in_" + name] = a
        ins[name] = nc.dram_tensor("in_" + name, a.shape, mybir.dt.from_np(a.dtype), kind="ExternalInput").ap()
    table = np.ascontiguousarray(np.concatenate(list(CONST.values()), axis=1))
    arrays["in_const"] = table
    ins["const"] = nc.dram_tensor("in_const", table.shape, F32, kind="ExternalInput").ap()
    for name, shape in _OUTS.items():
        outs[name] = nc.dram_tensor("out_" + name, shape, F32, kind="ExternalOutput").ap()
    trunk_kernel(nc, ins, outs)
    r = run_bass_kernel_spmd(nc, [arrays], core_ids=[0])
    return tuple(r.results[0]["out_" + name] for name in _OUTS)
```
